# Optimizing a Trainium2 kernel written in Bass

```python
import jax, jax.numpy as jnp
from jax import lax
import numpy as np
import math

D_MODEL = 1024
BATCH = 1
SEQ = 1024
DEPTH = 1

D_MIX = D_MODEL
D_SGU = D_MIX // 2
SGU_GROUPS = 4
SGU_GROUP_DIM = D_SGU // SGU_GROUPS
CHUNK = 128
N_HEADS = 8
HEAD_DIM = (D_MIX - D_SGU) // N_HEADS
N_KV_HEADS = 2
GQA_GROUP = N_HEADS // N_KV_HEADS
ROT_DIM = HEAD_DIM // 4
ROPE_THETA = 500000.0
IDX_HEADS = 8
IDX_DIM = 64
TOPK_MAX = 256
Q_BLOCK = 128
D_FF = 4 * D_MODEL
EPS = 1e-6
COL_SIZES = (D_SGU, D_SGU,
             N_HEADS * HEAD_DIM,
             N_KV_HEADS * HEAD_DIM,
             N_KV_HEADS * HEAD_DIM,
             IDX_HEADS * IDX_DIM,
             IDX_DIM,
             IDX_HEADS)
D_IN = sum(COL_SIZES)


def rms_norm(x, g):
    x32 = x.astype(jnp.float32)
    y = x32 * lax.rsqrt(jnp.mean(x32 * x32, axis=-1, keepdims=True) + EPS)
    return (y * g.astype(jnp.float32)).astype(x.dtype)

def rope_tables(positions):
    inv_freq = ROPE_THETA ** (-jnp.arange(0, ROT_DIM, 2, dtype=jnp.float32) / ROT_DIM)
    ang = positions.astype(jnp.float32)[..., None] * inv_freq
    return jnp.cos(ang), jnp.sin(ang)

def partial_rope(x, cos, sin):
    half = ROT_DIM // 2
    c = cos[:, :, None, :].astype(x.dtype)
    s = sin[:, :, None, :].astype(x.dtype)
    x1, x2, xp = x[..., :half], x[..., half:ROT_DIM], x[..., ROT_DIM:]
    return jnp.concatenate([x1 * c - x2 * s, x2 * c + x1 * s, xp], axis=-1)

def split_cols(p):
    outs, start = [], 0
    for n in COL_SIZES:
        outs.append(p[..., start:start + n])
        start += n
    return outs

def spatial_gating(u, v, g_v, w_s, b_s):
    B, S, _ = u.shape
    v = rms_norm(v.reshape(B, S, SGU_GROUPS, SGU_GROUP_DIM), g_v.reshape(SGU_GROUPS, SGU_GROUP_DIM))
    v = v.reshape(B, S // CHUNK, CHUNK, SGU_GROUPS, SGU_GROUP_DIM)
    causal = jnp.tril(jnp.ones((CHUNK, CHUNK), dtype=w_s.dtype))
    w_m = w_s * causal[None]
    mixed = jnp.einsum('gts,bnsgc->bntgc', w_m, v) + b_s.T[None, None, :, :, None]
    return u * mixed.reshape(B, S, D_SGU)

def dsa_attention(q, k, v, q_idx, k_idx, w_idx):
    B, S = q.shape[0], q.shape[1]
    topk = min(TOPK_MAX, S // 4)
    nb = S // Q_BLOCK
    key_pos = jnp.arange(S)

    def blocks(a):
        return a.reshape((B, nb, Q_BLOCK) + a.shape[2:]).swapaxes(0, 1)

    def one_block(args):
        qb, qib, wb, start = args
        t_pos = start + jnp.arange(Q_BLOCK)
        causal = key_pos[None, :] <= t_pos[:, None]
        dots = jnp.einsum('bthd,bsd->bths', qib, k_idx,
                          preferred_element_type=jnp.float32) * (IDX_DIM ** -0.5)
        score = jnp.einsum('bth,bths->bts', wb.astype(jnp.float32) * (IDX_HEADS ** -0.5),
                           jax.nn.relu(dots))
        score = jnp.where(causal[None], score, -jnp.inf)
        _, idx = lax.top_k(score, topk)
        sel_ok = idx <= t_pos[None, :, None]
        kg = jax.vmap(lambda kb, ib: kb[ib])(k, idx)
        vg = jax.vmap(lambda vb, ib: vb[ib])(v, idx)
        qg = qb.reshape(B, Q_BLOCK, N_KV_HEADS, GQA_GROUP, HEAD_DIM)
        logits = jnp.einsum('btkgd,btjkd->btkgj', qg, kg,
                            preferred_element_type=jnp.float32) * (HEAD_DIM ** -0.5)
        logits = jnp.where(sel_ok[:, :, None, None, :], logits, -jnp.inf)
        p = jax.nn.softmax(logits, axis=-1).astype(v.dtype)
        o = jnp.einsum('btkgj,btjkd->btkgd', p, vg)
        return o.reshape(B, Q_BLOCK, N_HEADS * HEAD_DIM)

    starts = jnp.arange(nb, dtype=jnp.int32) * Q_BLOCK
    out = lax.map(one_block, (blocks(q), blocks(q_idx), blocks(w_idx), starts))
    return out.swapaxes(0, 1).reshape(B, S, N_HEADS * HEAD_DIM)

def first_inputs(seed: int = 0) -> dict:
    key = jax.random.key(seed)
    ks = jax.random.split(key, 24)
    f32 = jnp.float32
    L, D = DEPTH, D_MODEL

    def nrm(k, shape, scale):
        return jax.random.normal(k, shape, f32) * scale

    def gain(k, shape):
        return 1.0 + 0.02 * jax.random.normal(k, shape, f32)

    x = jax.random.normal(ks[0], (BATCH, SEQ, D), f32)
    c = jax.random.normal(ks[1], (BATCH, D), f32)
    offset = jax.random.randint(ks[2], (BATCH, 1), 0, 1024, dtype=jnp.int32)
    positions = offset + jnp.arange(SEQ, dtype=jnp.int32)[None, :]
    return {
        "x": x,
        "c": c,
        "positions": positions,
        "w_ada": nrm(ks[3], (L, D, 6 * D), D ** -0.5),
        "b_ada": nrm(ks[4], (L, 6 * D), 0.02),
        "g_pre_mix": gain(ks[5], (L, D)),
        "w_in": nrm(ks[6], (L, D, D_IN), D ** -0.5),
        "g_sgu_v": gain(ks[7], (L, D_SGU)),
        "w_spatial": nrm(ks[8], (L, SGU_GROUPS, CHUNK, CHUNK), CHUNK ** -0.5),
        "b_spatial": gain(ks[9], (L, SGU_GROUPS, CHUNK)),
        "g_out_sgu": gain(ks[10], (L, D_SGU)),
        "g_out_attn": gain(ks[11], (L, N_HEADS * HEAD_DIM)),
        "w_out": nrm(ks[12], (L, D_MIX, D), D_MIX ** -0.5),
        "g_post_mix": gain(ks[13], (L, D)),
        "g_pre_ffn": gain(ks[14], (L, D)),
        "w_ff1": nrm(ks[15], (L, D, D_FF), D ** -0.5),
        "w_ff2": nrm(ks[16], (L, D_FF, D), D_FF ** -0.5),
        "g_post_ffn": gain(ks[17], (L, D)),
    }

def first_block(x, c, positions, w_ada, b_ada, g_pre_mix, w_in, g_sgu_v, w_spatial, b_spatial,
              g_out_sgu, g_out_attn, w_out, g_post_mix, g_pre_ffn, w_ff1, w_ff2, g_post_ffn):
    B, S, _ = x.shape
    cos, sin = rope_tables(positions)
    c_act = jax.nn.silu(c)
    for l in range(DEPTH):
        mod = jnp.einsum('bd,de->be', c_act, w_ada[l]) + b_ada[l]
        sh1, sc1, g1, sh2, sc2, g2 = jnp.split(mod[:, None, :], 6, axis=-1)

        h = rms_norm(x, g_pre_mix[l]) * (1.0 + sc1) + sh1
        proj = jnp.einsum('bsd,de->bse', h, w_in[l])
        p_u, p_v, p_q, p_k, p_val, p_qi, p_ki, p_wi = split_cols(proj)

        z_u, z_v = jax.nn.gelu(p_u), jax.nn.gelu(p_v)
        y_a = spatial_gating(z_u, z_v, g_sgu_v[l], w_spatial[l], b_spatial[l])

        q = partial_rope(p_q.reshape(B, S, N_HEADS, HEAD_DIM), cos, sin)
        k = partial_rope(p_k.reshape(B, S, N_KV_HEADS, HEAD_DIM), cos, sin)
        v = p_val.reshape(B, S, N_KV_HEADS, HEAD_DIM)
        q_idx = partial_rope(p_qi.reshape(B, S, IDX_HEADS, IDX_DIM), cos, sin)
        k_idx = partial_rope(p_ki.reshape(B, S, 1, IDX_DIM), cos, sin)[:, :, 0, :]
        y_b = dsa_attention(q, k, v, q_idx, k_idx, p_wi)

        merged = jnp.concatenate([rms_norm(y_a, g_out_sgu[l]), rms_norm(y_b, g_out_attn[l])], axis=-1)
        o = jnp.einsum('bse,ed->bsd', merged, w_out[l])
        x = x + g1 * rms_norm(o, g_post_mix[l])

        h2 = rms_norm(x, g_pre_ffn[l]) * (1.0 + sc2) + sh2
        f = jnp.square(jax.nn.relu(jnp.einsum('bsd,df->bsf', h2, w_ff1[l])))
        f = jnp.einsum('bsf,fd->bsd', f, w_ff2[l])
        x = x + g2 * rms_norm(f, g_post_ffn[l])
    return x


_first_inputs = first_inputs


def first_inputs(seed=0):
    import zlib

    import numpy as np

    out = dict(_first_inputs(seed))
    spreads = {}
    factors = {'g_pre_mix': 2.966,
     'g_sgu_v': 200.0,
     'b_spatial': 200.0,
     'g_out_sgu': 98.496,
     'g_out_attn': 99.103,
     'g_post_mix': 15.215,
     'g_pre_ffn': 61.56,
     'g_post_ffn': 81.784}
    for name, (base, spread) in spreads.items():
        noise = np.random.default_rng([zlib.crc32(name.encode()), seed]).standard_normal(out[name].shape)
        drawn = base * np.exp(spread * noise) if base else spread * noise
        out[name] = __import__('jax').numpy.asarray(drawn.astype(out[name].dtype))
    for name, factor in factors.items():
        out[name] = (out[name] * factor).astype(out[name].dtype)
    return out


_narrow_inputs = first_inputs


def first_inputs(seed=0):

    out = dict(_narrow_inputs(seed))
    wider = {'g_sgu_v': 6.97,
     'b_spatial': 5.34,
     'g_out_sgu': 3.84,
     'g_out_attn': 3.83,
     'g_post_ffn': 3.31}
    for name, times in wider.items():
        mean = out[name].mean()
        out[name] = (mean + times * (out[name] - mean)).astype(out[name].dtype)
    return out


RWKV_WIDTH = D_MODEL // 2
RWKV_HEAD = 64
RWKV_HEADS = RWKV_WIDTH // RWKV_HEAD
DECAY_LORA = 64
AAA_LORA = 64
GATE_LORA = 128
LNX_EPS = 64e-5
DECAY_SCALE = math.exp(-0.5)
SSM_WIDTH = D_MODEL // 2
SSM_GROUP = 16
SSM_GROUPS = SSM_WIDTH // SSM_GROUP
SSM_STATE = 64
D_FF_2 = 4 * D_MODEL
NORM_EPS = 1e-6
SHIFT_COLS = 3 * RWKV_WIDTH + DECAY_LORA + AAA_LORA + GATE_LORA
IN_COLS = SHIFT_COLS + SSM_WIDTH + 2 * D_MODEL


def rmsnorm(x, g):
    xf = x.astype(jnp.float32)
    y = xf * lax.rsqrt(jnp.mean(xf * xf, axis=-1, keepdims=True) + NORM_EPS)
    return (y * g.astype(jnp.float32)).astype(x.dtype)

def token_shift(z):
    return jnp.pad(z[:, :-1], ((0, 0), (1, 0), (0, 0)))

def rwkv7_time_mix(zm, k_k, k_a, r_k, w0, w_decay_up, a0, w_aaa_up, w_gate_up,
                   lnx_w, lnx_b, w_proj):
    bsz, seq, _ = zm.shape
    W, H, N = RWKV_WIDTH, RWKV_HEADS, RWKV_HEAD
    f32 = jnp.float32
    r, k, v, wd, ad, gd = jnp.split(
        zm, [W, 2 * W, 3 * W, 3 * W + DECAY_LORA, 3 * W + DECAY_LORA + AAA_LORA], axis=-1)
    w = jnp.exp(-DECAY_SCALE * jax.nn.sigmoid((w0 + jnp.tanh(wd) @ w_decay_up).astype(f32)))
    a = jax.nn.sigmoid(a0 + ad @ w_aaa_up)
    g = jax.nn.sigmoid(gd) @ w_gate_up
    kk = k * k_k
    k_mod = k * (1.0 + (a - 1.0) * k_a)

    heads = lambda t: t.reshape(bsz, seq, H, N).astype(f32)
    rh, kh, vh, wh, ah, kkh = map(heads, (r, k_mod, v, w, a, kk))
    kkh = kkh / jnp.maximum(jnp.sqrt(jnp.sum(kkh * kkh, axis=-1, keepdims=True)), 1e-12)
    tm = lambda t: jnp.swapaxes(t, 0, 1)

    def step(state, inp):
        r_t, w_t, k_t, v_t, kk_t, b_t = inp
        sk = jnp.einsum('bhvk,bhk->bhv', state, kk_t)
        state = (state * w_t[:, :, None, :]
                 - sk[..., None] * b_t[:, :, None, :]
                 + v_t[..., None] * k_t[:, :, None, :])
        return state, jnp.einsum('bhvk,bhk->bhv', state, r_t)

    state0 = jnp.zeros((bsz, H, N, N), f32)
    _, y = lax.scan(step, state0, tuple(map(tm, (rh, wh, kh, vh, kkh, kkh * ah))))
    y = tm(y)
    mu = jnp.mean(y, axis=-1, keepdims=True)
    var = jnp.mean(jnp.square(y - mu), axis=-1, keepdims=True)
    y = ((y - mu) * lax.rsqrt(var + LNX_EPS)).reshape(bsz, seq, W)
    y = y * lnx_w.astype(f32) + lnx_b.astype(f32)
    bonus = (jnp.sum(rh * kh * r_k.astype(f32), axis=-1, keepdims=True) * vh).reshape(bsz, seq, W)
    y = (y + bonus).astype(zm.dtype) * g
    return y @ w_proj

def _complex_scan_op(e1, e2):
    a1r, a1i, b1r, b1i = e1
    a2r, a2i, b2r, b2i = e2
    return (a2r * a1r - a2i * a1i,
            a2r * a1i + a2i * a1r,
            a2r * b1r - a2i * b1i + b2r,
            a2r * b1i + a2i * b1r + b2i)

def s5_ssm(u, a_re, a_im, log_dt, b_re, b_im, c_re, c_im, d_skip, w_glu, b_glu):
    bsz, seq, _ = u.shape
    G, C, P = SSM_GROUPS, SSM_GROUP, SSM_STATE
    f32 = jnp.float32
    uf = u.astype(f32).reshape(bsz, seq, G, C)
    dt = jnp.exp(log_dt.astype(f32))[:, None]
    are = jnp.minimum(a_re.astype(f32), -1e-4)
    aim = a_im.astype(f32)
    mag = jnp.exp(dt * are)
    abar_re = mag * jnp.cos(dt * aim)
    abar_im = mag * jnp.sin(dt * aim)
    den = are * are + aim * aim
    nr = abar_re - 1.0
    coef_re = (nr * are + abar_im * aim) / den
    coef_im = (abar_im * are - nr * aim) / den
    br, bi = b_re.astype(f32), b_im.astype(f32)
    bbar_re = coef_re[..., None] * br - coef_im[..., None] * bi
    bbar_im = coef_re[..., None] * bi + coef_im[..., None] * br
    bu_re = jnp.einsum('gpc,bsgc->bsgp', bbar_re, uf)
    bu_im = jnp.einsum('gpc,bsgc->bsgp', bbar_im, uf)
    a_seq_re = jnp.broadcast_to(abar_re, (1, seq, G, P))
    a_seq_im = jnp.broadcast_to(abar_im, (1, seq, G, P))
    _, _, xr, xi = lax.associative_scan(_complex_scan_op, (a_seq_re, a_seq_im, bu_re, bu_im), axis=1)
    y = (jnp.einsum('gcp,bsgp->bsgc', c_re.astype(f32), xr)
         - jnp.einsum('gcp,bsgp->bsgc', c_im.astype(f32), xi)
         + d_skip.astype(f32).reshape(G, C) * uf)
    y = jax.nn.gelu(y.reshape(bsz, seq, SSM_WIDTH), approximate=False).astype(u.dtype)
    z = y @ w_glu + b_glu
    za, zb = jnp.split(z, 2, axis=-1)
    return za * jax.nn.sigmoid(zb)

def sq_relu_mlp(x, w_up, w_down):
    return jnp.square(jax.nn.relu(x @ w_up)) @ w_down

def second_inputs(seed: int = 0) -> dict:
    key = jax.random.key(seed)
    ks = iter(jax.random.split(key, 40))
    L, D, W, H, N = DEPTH, D_MODEL, RWKV_WIDTH, RWKV_HEADS, RWKV_HEAD
    G, C, P = SSM_GROUPS, SSM_GROUP, SSM_STATE
    nrm = lambda shape, s: jax.random.normal(next(ks), shape, jnp.float32) * s
    unif = lambda shape, lo, hi: jax.random.uniform(next(ks), shape, jnp.float32, lo, hi)
    return {
        "x": nrm((BATCH, SEQ, D), 1.0),
        "norm1_g": 1.0 + nrm((L, D), 0.02),
        "w_in": nrm((L, D, IN_COLS), D ** -0.5),
        "mu_shift": unif((L, SHIFT_COLS), 0.0, 1.0),
        "k_k": 0.85 + nrm((L, W), 0.05),
        "k_a": 1.0 + nrm((L, W), 0.05),
        "r_k": nrm((L, H, N), 0.1),
        "w0": unif((L, W), -3.0, 3.0),
        "w_decay_up": nrm((L, DECAY_LORA, W), 0.1),
        "a0": nrm((L, W), 0.1),
        "w_aaa_up": nrm((L, AAA_LORA, W), 0.1),
        "w_gate_up": nrm((L, GATE_LORA, W), GATE_LORA ** -0.5),
        "lnx_w": 1.0 + nrm((L, W), 0.02),
        "lnx_b": nrm((L, W), 0.01),
        "w_rwkv_proj": nrm((L, W, D), W ** -0.5),
        "a_re": -0.5 + nrm((L, G, P), 0.01),
        "a_im": jnp.pi * jnp.arange(P, dtype=jnp.float32) + nrm((L, G, P), 0.01),
        "log_dt": unif((L, G), math.log(1e-3), math.log(1e-1)),
        "b_re": nrm((L, G, P, C), (2 * C) ** -0.5),
        "b_im": nrm((L, G, P, C), (2 * C) ** -0.5),
        "c_re": nrm((L, G, C, P), (2 * P) ** -0.5),
        "c_im": nrm((L, G, C, P), (2 * P) ** -0.5),
        "d_skip": nrm((L, SSM_WIDTH), 1.0),
        "w_glu": nrm((L, SSM_WIDTH, 2 * D), SSM_WIDTH ** -0.5),
        "b_glu": nrm((L, 2 * D), 0.01),
        "w_out": nrm((L, D, D), D ** -0.5),
        "norm2_g": 1.0 + nrm((L, D), 0.02),
        "w_ff_up": nrm((L, D, D_FF_2), D ** -0.5),
        "w_ff_down": nrm((L, D_FF_2, D), D_FF_2 ** -0.5),
        "norm_f_g": 1.0 + nrm((D,), 0.02),
    }

def second_block(x, norm1_g, w_in, mu_shift, k_k, k_a, r_k, w0, w_decay_up, a0, w_aaa_up,
              w_gate_up, lnx_w, lnx_b, w_rwkv_proj, a_re, a_im, log_dt, b_re, b_im, c_re,
              c_im, d_skip, w_glu, b_glu, w_out, norm2_g, w_ff_up, w_ff_down, norm_f_g):
    for l in range(DEPTH):
        xn = rmsnorm(x, norm1_g[l])
        z = xn @ w_in[l]
        z_rwkv, u, gates = jnp.split(z, [SHIFT_COLS, SHIFT_COLS + SSM_WIDTH], axis=-1)
        z_mix = z_rwkv + (token_shift(z_rwkv) - z_rwkv) * mu_shift[l]
        y_a = rwkv7_time_mix(z_mix, k_k[l], k_a[l], r_k[l], w0[l], w_decay_up[l], a0[l],
                             w_aaa_up[l], w_gate_up[l], lnx_w[l], lnx_b[l], w_rwkv_proj[l])
        y_b = s5_ssm(u, a_re[l], a_im[l], log_dt[l], b_re[l], b_im[l], c_re[l], c_im[l],
                     d_skip[l], w_glu[l], b_glu[l])
        g_a, g_b = jnp.split(jax.nn.sigmoid(gates), 2, axis=-1)
        x = x + (g_a * y_a + g_b * y_b) @ w_out[l]
        x = x + sq_relu_mlp(rmsnorm(x, norm2_g[l]), w_ff_up[l], w_ff_down[l])
    return rmsnorm(x, norm_f_g)


_first_inputs_2 = second_inputs


def second_inputs(seed=0):
    import zlib

    import numpy as np

    out = dict(_first_inputs_2(seed))
    spreads = {}
    factors = {'norm1_g': 4.237,
     'k_k': 64.0,
     'k_a': 3.289,
     'a0': 4.103,
     'lnx_w': 64.0,
     'lnx_b': 64.0,
     'a_re': 64.0,
     'a_im': 37.704,
     'log_dt': 38.976,
     'b_re': 52.312,
     'b_im': 54.176,
     'c_re': 53.552,
     'c_im': 52.896,
     'b_glu': 64.0,
     'norm2_g': 12.976,
     'norm_f_g': 8.612}
    for name, (base, spread) in spreads.items():
        noise = np.random.default_rng([zlib.crc32(name.encode()), seed]).standard_normal(out[name].shape)
        drawn = base * np.exp(spread * noise) if base else spread * noise
        out[name] = __import__('jax').numpy.asarray(drawn.astype(out[name].dtype))
    for name, factor in factors.items():
        out[name] = (out[name] * factor).astype(out[name].dtype)
    return out


_narrow_inputs_2 = second_inputs


def second_inputs(seed=0):
    out = dict(_narrow_inputs_2(seed))
    wider = {'k_k': 4.37, 'lnx_w': 3.25, 'lnx_b': 6.61, 'b_glu': 5.62, 'norm_f_g': 3.3}
    for name, times in wider.items():
        mean = out[name].mean()
        out[name] = (mean + times * (out[name] - mean)).astype(out[name].dtype)
    return out


def setup_inputs(seed=0):
    out = dict(first_inputs(seed))
    for name, value in second_inputs(seed + 1).items():
        if name != "x":
            out[name + "_2"] = value
    return out


def reference(
    x, c, positions, w_ada, b_ada, g_pre_mix, w_in, g_sgu_v, w_spatial, b_spatial, g_out_sgu,
    g_out_attn, w_out, g_post_mix, g_pre_ffn, w_ff1, w_ff2, g_post_ffn, norm1_g_2, w_in_2,
    mu_shift_2, k_k_2, k_a_2, r_k_2, w0_2, w_decay_up_2, a0_2, w_aaa_up_2, w_gate_up_2, lnx_w_2,
    lnx_b_2, w_rwkv_proj_2, a_re_2, a_im_2, log_dt_2, b_re_2, b_im_2, c_re_2, c_im_2, d_skip_2,
    w_glu_2, b_glu_2, w_out_2, norm2_g_2, w_ff_up_2, w_ff_down_2, norm_f_g_2,
):
    x = first_block(
        x, c, positions, w_ada, b_ada, g_pre_mix, w_in, g_sgu_v, w_spatial, b_spatial,
        g_out_sgu, g_out_attn, w_out, g_post_mix, g_pre_ffn, w_ff1, w_ff2, g_post_ffn,
    )
    return second_block(
        x, norm1_g_2, w_in_2, mu_shift_2, k_k_2, k_a_2, r_k_2, w0_2, w_decay_up_2, a0_2,
        w_aaa_up_2, w_gate_up_2, lnx_w_2, lnx_b_2, w_rwkv_proj_2, a_re_2, a_im_2, log_dt_2,
        b_re_2, b_im_2, c_re_2, c_im_2, d_skip_2, w_glu_2, b_glu_2, w_out_2, norm2_g_2,
        w_ff_up_2, w_ff_down_2, norm_f_g_2,
    )


_drawn_inputs = setup_inputs


def setup_inputs(seed=0):
    import zlib

    import numpy as np

    out = dict(_drawn_inputs(seed))
    spreads = {}
    factors = {}
    for name, (base, spread) in spreads.items():
        noise = np.random.default_rng([zlib.crc32(name.encode()), seed]).standard_normal(out[name].shape)
        drawn = base * np.exp(spread * noise) if base else spread * noise
        out[name] = __import__('jax').numpy.asarray(drawn.astype(out[name].dtype))
    for name, factor in factors.items():
        out[name] = (out[name] * factor).astype(out[name].dtype)
    return out
```

```python
from contextlib import ExitStack

import numpy as np

import concourse.bass as bass
from concourse import mybir

P = 128
S = 1024
D = 1024
HALF = 512
KT = D // P
NT = S // P
D_SGU = 512
HEADS = 8
HD = 64
TOPK = 256
D_FF = 4096
FT = D_FF // P
W2 = 512
WT = W2 // P
CH = 64
SHIFT_TILES = 14
GATE_TILES = 16
SSM_TILES = 16
RING = 4
EPS = 1e-6
LNX_EPS = 64e-5
DECAY_SCALE = float(np.exp(-0.5))
GELU_TILES = 4

FAR = -2.0e38
TAKEN = -3.0e38
NEVER = -1.0e30

F32 = mybir.dt.float32
U32 = mybir.dt.uint32
I32 = mybir.dt.int32
ACT = mybir.ActivationFunctionType
ALU = mybir.AluOpType
AX = mybir.AxisListType

COLS = [
    ("c", 8), ("b_ada", 48), ("g_pre_mix", 8), ("g_sgu_v", 4), ("g_out_sgu", 4), ("g_out_attn", 4),
    ("g_post_mix", 8), ("g_pre_ffn", 8), ("g_post_ffn", 8), ("norm1_g", 8), ("mu", 14), ("k_k", 4),
    ("k_a", 4), ("r_k", 4), ("w0", 4), ("a0", 4), ("lnx_w", 4), ("lnx_b", 4), ("d_skip", 4),
    ("b_glu", 16), ("norm2_g", 8), ("norm_f_g", 8), ("a_re", 16), ("a_im", 16), ("log_dt", 16),
    ("inv_freq", 1), ("eps", 1), ("lnx_eps", 1), ("minus_pi", 1),
]
COL_AT = {}
_n = 0
for _name, _k in COLS:
    COL_AT[_name] = (_n, _k)
    _n += _k
N_COLS = _n

CONSTS = [
    ("ident", 128), ("ones", 128), ("head_ones", 128), ("rope_swap", 128), ("t_ge_s", 128),
]
CONST_AT = {}
_n = 0
for _name, _k in CONSTS:
    CONST_AT[_name] = (_n, _k)
    _n += _k
N_CONSTS = _n


class Signal:

    def __init__(self, nc, ctx, name):
        self.sem = ctx.enter_context(nc.semaphore(name))
        self.n = 0


class Core:

    def __init__(self, nc, ctx, dram):
        self.nc, self.ctx, self.dram = nc, ctx, dram
        self.names = {}
        self.psum = ctx.enter_context(nc.psum_tensor("psum", [P, 8, HALF], F32))
        self.ring = self.sbuf(ctx, "weight_ring", [P, RING, KT * P])
        self.cols = self.sbuf(ctx, "cols", [P, N_COLS])
        self.consts = self.sbuf(ctx, "consts", [P, N_CONSTS])
        self.mod = self.sbuf(ctx, "mod", [P, 48])
        self.setup = self.flag("setup_loaded")
        self.slab_loaded = [self.flag(f"slab_loaded_{i}") for i in range(RING)]
        self.slab_used = self.flag("slab_used")
        self.acc_free = self.flag("acc_free")
        self.posted = self.flag("posted")
        self.sq_ready = self.flag("square_ready")
        self.sq_used = self.flag("square_used")
        self.root_ready = self.flag("root_ready")
        self.scale_ready = self.flag("scale_ready")
        self.scaled = self.flag("scaled")
        self.act_done = self.flag("act_done")
        self.dve_done = self.flag("dve_done")
        self.pool_done = self.flag("pool_done")
        self.pe_done = self.flag("pe_done")
        self.load_done = self.flag("load_done")
        self.store_done = self.flag("store_done")

    def sbuf(self, ctx, name, shape, dt=F32):
        n = self.names[name] = self.names.get(name, 0) + 1
        return ctx.enter_context(self.nc.sbuf_tensor(name if n == 1 else f"{name}_{n}", shape, dt))

    def flag(self, name):
        return Signal(self.nc, self.ctx, name)

    def col(self, name, t=0, n=1):
        at = COL_AT[name][0] + t
        return self.cols[:, at:at + n]

    def const(self, name):
        at, n = CONST_AT[name]
        return self.consts[:, at:at + n]


class Chain:

    def __init__(self, eng, of):
        self.eng, self.of, self.n = eng, of, of.n

    def step(self, ins):
        ins.then_inc(self.of.sem, 1)
        self.n += 1
        return self.n

    def wait(self, n=None):
        self.eng.wait_ge(self.of.sem, self.n if n is None else n)

    def __call__(self, ins):
        self.step(ins)
        self.wait()


def load_setup(nc, K):
    with nc.Block() as block:
        @block.sync
        def _(sp):
            sp.dma_start(K.cols[:], K.dram["cols"]).then_inc(K.setup.sem, 16)
            sp.dma_start(K.consts[:], K.dram["consts"]).then_inc(K.setup.sem, 16)
            sp.wait_ge(K.setup.sem, 32)

        @block.tensor
        def _(pe):
            pe.sem_inc(K.slab_used.sem, RING)

        @block.scalar
        def _(act):
            act.sem_inc(K.acc_free.sem, 2)
            act.sem_inc(K.posted.sem, 2)
    K.setup.n = 32


def dense(nc, K, weights, n_tiles, kg, kt, rhs, width, step, on="scalar", post=None):
    un = 4 if kg == 1 else 2
    loops, rest = n_tiles // un, n_tiles % un
    per = un * kg
    spans = [(lo, min(HALF, width - lo)) for lo in range(0, width, HALF)]
    used0, accfree0, post0 = K.slab_used.n, K.acc_free.n, K.posted.n
    loaded0 = [s.n for s in K.slab_loaded]
    uses = per // RING
    psum = K.psum

    def acc(j):
        b = 2 * (j % 2)
        return psum[:, b:b + len(spans), 0:spans[0][1]]

    def over_tiles(eng, tile):
        if loops:
            with eng.Fori(0, loops) as i:
                for j in range(un):
                    tile(i, j)
        for j in range(rest):
            tile(loops, j)

    with nc.Block() as block:
        @block.sync
        def _(sp):
            def load(i, j):
                for s in range(j * kg, (j + 1) * kg):
                    sp.wait_ge(K.slab_used.sem, i * per + (used0 + s + 1))
                    sp.dma_start(K.ring[:, s % RING, 0:kt * P], weights[i * per + s]) \
                        .then_inc(K.slab_loaded[s % RING].sem, 16)
            over_tiles(sp, load)

        @block.tensor
        def _(pe):
            def tile(i, j):
                pe.wait_ge(K.acc_free.sem, i * un + (accfree0 + j + 1))
                for g in range(kg):
                    s = j * kg + g
                    slot = s % RING
                    pe.wait_ge(K.slab_loaded[slot].sem,
                               i * (16 * uses) + (loaded0[slot] + 16 * (s // RING + 1)))
                    for k in range(kt):
                        for h, (lo, n) in enumerate(spans):
                            mm = pe.matmul(psum[:, 2 * (j % 2) + h, 0:n],
                                           K.ring[:, slot, k * P:(k + 1) * P], rhs(g * kt + k, lo, n),
                                           start=(g == 0 and k == 0), stop=(g == kg - 1 and k == kt - 1))
                    mm.then_inc(K.slab_used.sem, 1)
            over_tiles(pe, tile)

        def drain(eng):
            def tile(i, j):
                if post:
                    eng.wait_ge(K.posted.sem, i * un + (post0 + j + 1))
                eng.wait_ge(K.slab_used.sem, i * per + (used0 + RING + (j + 1) * kg))
                eng.wait_ge(K.setup.sem, 32)
                step(eng, acc(j), i * un + j, j % 2).then_inc(K.acc_free.sem, 1)
            over_tiles(eng, tile)

        if on == "scalar":
            @block.scalar
            def _(act):
                drain(act)
        if on == "vector":
            @block.vector
            def _(dve):
                drain(dve)
        if post:
            @block.vector
            def _(dve):
                def finish(i, j):
                    dve.wait_ge(K.acc_free.sem, i * un + (accfree0 + 2 + j + 1))
                    dve.wait_ge(K.setup.sem, 32)
                    post(dve, i * un + j, j % 2).then_inc(K.posted.sem, 1)
                over_tiles(dve, finish)

    total = n_tiles * kg
    K.slab_used.n += total
    K.acc_free.n += n_tiles
    K.posted.n += n_tiles if post else 0
    for slot in range(RING):
        K.slab_loaded[slot].n += 16 * sum(1 for s in range(total) if s % RING == slot)


def ada(nc, K):
    dram = K.dram
    with ExitStack() as ctx:
        act_c = K.sbuf(ctx, "silu_c", [P, KT])
        base = K.act_done.n
        with nc.Block() as block:
            @block.scalar
            def _(act):
                act.activation(act_c[:], K.col("c", 0, KT), ACT.Silu).then_inc(K.act_done.sem, 1)
                act.wait_ge(K.act_done.sem, base + 1)
        K.act_done.n += 1
        dense(nc, K, dram["w_ada"], 48, 1, KT, lambda k, lo, n: act_c[:, k:k + 1], 1,
              lambda eng, acc, t, j: eng.tensor_tensor(
                  out=K.mod[:, bass.ds(t, 1)], in0=acc[:, 0, :], in1=K.cols[:, bass.ds(t + COL_AT["b_ada"][0], 1)],
                  op=ALU.add), "vector")
        with nc.Block() as block:
            @block.vector
            def _(dve):
                c = Chain(dve, K.dve_done)
                for at, gain in ((8, "g_pre_mix"), (32, "g_pre_ffn")):
                    dve.scalar_tensor_tensor(out=K.mod[:, at:at + 8], in0=K.mod[:, at:at + 8], scalar=1.0,
                                             in1=K.col(gain, 0, 8), op0=ALU.add, op1=ALU.mult)
                for at, gain in ((16, "g_post_mix"), (40, "g_post_ffn")):
                    ins = dve.tensor_tensor(out=K.mod[:, at:at + 8], in0=K.mod[:, at:at + 8],
                                            in1=K.col(gain, 0, 8), op=ALU.mult)
                c(ins)
                K.dve_done.n = c.n


def rms_norm(nc, K, ctx, src, tiles, out, gain, bias=None, add=None, size=None, eps="eps"):
    size = size or tiles * P
    with ExitStack() as ctx:
        sq = K.sbuf(ctx, "squares", [P, 2, S])
        root = K.sbuf(ctx, "root", [P, S])
        sq0, used0, root0, scale0, scaled0 = (K.sq_ready.n, K.sq_used.n, K.root_ready.n,
                                              K.scale_ready.n, K.scaled.n)
        with nc.Block() as block:
            @block.scalar
            def _(act):
                for t in range(tiles):
                    if t >= 2:
                        act.wait_ge(K.sq_used.sem, used0 + t - 1)
                    act.activation(sq[:, t % 2, :], src[:, t, :], ACT.Square).then_inc(K.sq_ready.sem, 1)
                act.wait_ge(K.sq_used.sem, used0 + tiles)
                act.activation(root[:], K.psum[:, 4:6, :], ACT.Sqrt, scale=1.0 / size, bias=K.col(eps)) \
                    .then_inc(K.root_ready.sem, 1)
                if bias is not None:
                    for t in range(tiles):
                        act.wait_ge(K.scaled.sem, scaled0 + t + 1)
                        ins = act.activation(out[:, t, :], out[:, t, :], ACT.Identity, bias=bias(t))
                        ins.then_inc(K.act_done.sem, 1)

            @block.tensor
            def _(pe):
                for t in range(tiles):
                    pe.wait_ge(K.sq_ready.sem, sq0 + t + 1)
                    for h in range(2):
                        mm = pe.matmul(K.psum[:, 4 + h, :], K.const("ones"),
                                       sq[:, t % 2, h * HALF:(h + 1) * HALF],
                                       start=(t == 0), stop=(t == tiles - 1))
                    mm.then_inc(K.sq_used.sem, 1)

            @block.vector
            def _(dve):
                dve.wait_ge(K.root_ready.sem, root0 + 1)
                dve.reciprocal(root[:], root[:]).then_inc(K.scale_ready.sem, 1)
                dve.wait_ge(K.scale_ready.sem, scale0 + 1)
                for t in range(tiles):
                    to = src if add is not None else out
                    dve.scalar_tensor_tensor(out=to[:, t, :], in0=src[:, t, :], scalar=gain(t), in1=root[:],
                                             op0=ALU.mult, op1=ALU.mult).then_inc(K.scaled.sem, 1)
                    if add is not None:
                        dve.wait_ge(K.scaled.sem, scaled0 + t + 1)
                        dve.tensor_tensor(out=out[:, t, :], in0=src[:, t, :], in1=add[:, t, :], op=ALU.add)
    K.sq_ready.n += tiles
    K.sq_used.n += tiles
    K.root_ready.n += 1
    K.scale_ready.n += 1
    K.scaled.n += tiles
    K.act_done.n += tiles if bias is not None else 0


def move(nc, K, pairs):
    with nc.Block() as block:
        @block.sync
        def _(sp):
            for to, of in pairs:
                sp.dma_start(to, of).then_inc(K.load_done.sem, 16)
                K.load_done.n += 16
            sp.wait_ge(K.load_done.sem, K.load_done.n)


def token_products(nc, K, h, zv, val, w_idx):
    ready0, act0, free0, load0 = K.pe_done.n, K.act_done.n, K.dve_done.n, K.load_done.n
    with ExitStack() as ctx:
        wv = K.sbuf(ctx, "w_v", [P, KT, D_SGU])
        wa = K.sbuf(ctx, "w_val", [P, KT, 136])
        with nc.Block() as block:
            @block.sync
            def _(sp):
                sp.dma_start(wv[:], K.dram["w_v"]).then_inc(K.load_done.sem, 16)
                sp.dma_start(wa[:], K.dram["w_val"]).then_inc(K.load_done.sem, 16)

            @block.tensor
            def _(pe):
                pe.wait_ge(K.load_done.sem, load0 + 32)
                for n in range(NT):
                    if n >= 2:
                        pe.wait_ge(K.act_done.sem, act0 + n - 1)
                        pe.wait_ge(K.dve_done.sem, free0 + n - 1)
                    for k in range(KT):
                        pe.matmul(K.psum[:, n % 2, :], h[:, k, n * P:(n + 1) * P], wv[:, k, :],
                                  start=(k == 0), stop=(k == KT - 1))
                    for k in range(KT):
                        mm = pe.matmul(K.psum[:, 2 + n % 2, 0:136], h[:, k, n * P:(n + 1) * P], wa[:, k, :],
                                       start=(k == 0), stop=(k == KT - 1))
                    mm.then_inc(K.pe_done.sem, 1)

            @block.scalar
            def _(act):
                for n in range(NT):
                    act.wait_ge(K.pe_done.sem, ready0 + n + 1)
                    act.activation(zv[:, n, :], K.psum[:, n % 2, :], ACT.Gelu_apprx_tanh) \
                        .then_inc(K.act_done.sem, 1)

            @block.vector
            def _(dve):
                for n in range(NT):
                    dve.wait_ge(K.pe_done.sem, ready0 + n + 1)
                    dve.tensor_copy(val[:, n, :], K.psum[:, 2 + n % 2, 0:P])
                    dve.tensor_scalar(w_idx[:, n, :], K.psum[:, 2 + n % 2, P:P + HEADS], HEADS ** -0.5, None,
                                      op0=ALU.mult).then_inc(K.dve_done.sem, 1)
    K.load_done.n += 32
    K.pe_done.n += NT
    K.act_done.n += NT
    K.dve_done.n += NT


TWO_PI_1 = 6.28125
TWO_PI_2 = float(np.float32(np.frombuffer(np.array(
    [np.frombuffer(np.float32(2 * np.pi - 6.28125).tobytes(), np.uint32)[0] & 0xFFFFF000],
    np.uint32).tobytes(), np.float32)[0]))
TWO_PI_3 = float(2 * np.pi - 6.28125 - TWO_PI_2)
MAGIC = 12582912.0
PI_IN = 3.1415925


def reduce_angle(dve, c, out, turns, angle, shift):
    c(dve.tensor_scalar(turns, angle, float(1 / (2 * np.pi)), shift, op0=ALU.mult, op1=ALU.add))
    c(dve.tensor_scalar(turns, turns, MAGIC, None, op0=ALU.add))
    c(dve.tensor_scalar(turns, turns, -MAGIC, None, op0=ALU.add))
    c(dve.scalar_tensor_tensor(out=out, in0=turns, scalar=-TWO_PI_1, in1=angle, op0=ALU.mult, op1=ALU.add))
    c(dve.scalar_tensor_tensor(out=out, in0=turns, scalar=-TWO_PI_2, in1=out, op0=ALU.mult, op1=ALU.add))
    c(dve.scalar_tensor_tensor(out=out, in0=turns, scalar=-TWO_PI_3, in1=out, op0=ALU.mult, op1=ALU.add))
    if shift:
        c(dve.tensor_scalar(out, out, float(shift * 2 * np.pi), None, op0=ALU.add))
    c(dve.tensor_scalar(out, out, PI_IN, -PI_IN, op0=ALU.min, op1=ALU.max))


def rope_tables(nc, K, cos, sin):
    with ExitStack() as ctx:
        pos_i = K.sbuf(ctx, "positions_int", [P, S], I32)
        angle = K.sbuf(ctx, "angle", [P, S])
        turns = K.sbuf(ctx, "turns", [P, S])
        load0, dve0, act0 = K.load_done.n, K.dve_done.n, K.act_done.n
        with nc.Block() as block:
            @block.sync
            def _(sp):
                sp.dma_start(pos_i[:], K.dram["positions"].broadcast_to([P, S])).then_inc(K.load_done.sem, 16)

            @block.vector
            def _(dve):
                dve.wait_ge(K.load_done.sem, load0 + 16)
                c = Chain(dve, K.dve_done)
                c(dve.tensor_copy(angle[:], pos_i[:]))
                c(dve.tensor_scalar(angle[:], angle[:], K.col("inv_freq"), None, op0=ALU.mult))
                reduce_angle(dve, c, sin[:], turns[:], angle[:], 0.0)
                reduce_angle(dve, c, cos[:], turns[:], angle[:], 0.25)
                K.dve_done.n = c.n

            @block.scalar
            def _(act):
                act.wait_ge(K.dve_done.sem, K.dve_done.n)
                act.activation(sin[:], sin[:], ACT.Sin).then_inc(K.act_done.sem, 1)
                act.activation(cos[:], cos[:], ACT.Sin).then_inc(K.act_done.sem, 1)
    K.load_done.n += 16
    K.act_done.n += 2


def rope(nc, K, x, tiles, cos, sin):
    with ExitStack() as ctx:
        turned = K.sbuf(ctx, "turned", [P, 2, S])
        pe0, dve0, free0 = K.pe_done.n, K.dve_done.n, K.scaled.n
        with nc.Block() as block:
            @block.tensor
            def _(pe):
                with pe.Fori(0, tiles // 2) as i:
                    for j in range(2):
                        pe.wait_ge(K.acc_free.sem, i * 2 + (K.acc_free.n + j + 1))
                        for h in range(2):
                            mm = pe.matmul(K.psum[:, 2 * j + h, :], K.const("rope_swap"),
                                           x[:, bass.ds(i * 2 + j, 1), h * HALF:(h + 1) * HALF],
                                           start=True, stop=True)
                        mm.then_inc(K.pe_done.sem, 1)

            @block.vector
            def _(dve):
                with dve.Fori(0, tiles // 2) as i:
                    for j in range(2):
                        tile = x[:, bass.ds(i * 2 + j, 1), :]
                        dve.wait_ge(K.pe_done.sem, i * 2 + (pe0 + j + 1))
                        dve.wait_ge(K.setup.sem, 32)
                        dve.tensor_tensor(out=turned[:, j:j + 1, :], in0=K.psum[:, 2 * j:2 * j + 2, :],
                                          in1=sin[:], op=ALU.mult).then_inc(K.acc_free.sem, 1)
                        dve.tensor_tensor(out=tile, in0=tile, in1=cos[:], op=ALU.mult) \
                            .then_inc(K.dve_done.sem, 1)
                        dve.wait_ge(K.dve_done.sem, i * 4 + (dve0 + 2 * j + 1))
                        dve.wait_ge(K.acc_free.sem, i * 2 + (K.acc_free.n + 2 + j + 1))
                        dve.wait_ge(K.setup.sem, 32)
                        dve.tensor_tensor(out=tile, in0=tile, in1=turned[:, j:j + 1, :], op=ALU.add) \
                            .then_inc(K.dve_done.sem, 1)
    K.pe_done.n += tiles
    K.dve_done.n += 2 * tiles
    K.acc_free.n += tiles


def spatial_gating(nc, K, zu, zv, out):
    load0, act0, dve0, pe0 = K.load_done.n, K.act_done.n, K.dve_done.n, K.pe_done.n
    with ExitStack() as ctx:
        w = K.sbuf(ctx, "w_spatial", [P, 4, P])
        b = K.sbuf(ctx, "b_spatial", [P, 4, P])
        junk = K.sbuf(ctx, "square_out", [P, D_SGU])
        ms = K.sbuf(ctx, "mean_squares", [P, NT, 4])
        mixed = K.sbuf(ctx, "mixed", [P, 2, HALF])
        with nc.Block() as block:
            @block.sync
            def _(sp):
                sp.dma_start(w[:], K.dram["w_spatial"]).then_inc(K.load_done.sem, 16)
                sp.dma_start(b[:], K.dram["b_spatial"].broadcast_to([P, 4, P])).then_inc(K.load_done.sem, 16)

            @block.vector
            def _(dve):
                c = Chain(dve, K.dve_done)
                dve.wait_ge(K.load_done.sem, load0 + 32)
                for g in range(4):
                    dve.tensor_tensor(out=w[:, g, :], in0=w[:, g, :], in1=K.const("t_ge_s"), op=ALU.mult)
                for n in range(NT):
                    for g in range(4):
                        z = zv[:, n, g * P:(g + 1) * P]
                        if n:
                            c.wait(c.n - 3)
                        ins = dve.tensor_tensor_reduce(
                            out=junk[:, g * P:(g + 1) * P], in0=z, in1=z, scale=1.0, scalar=0.0,
                            op0=ALU.mult, op1=ALU.add, accum_out=ms[:, n, g:g + 1])
                        c.step(ins)
                c.wait()
                dve.wait_ge(K.act_done.sem, act0 + 1)
                c(dve.reciprocal(ms[:], ms[:]))
                for n in range(NT):
                    for g in range(4):
                        z = zv[:, n, g * P:(g + 1) * P]
                        ins = dve.tensor_scalar(z, z, ms[:, n, g:g + 1], None, op0=ALU.mult)
                    c.step(ins)
                normed = c.n
                for m in range(8):
                    g, h = m // 2, m % 2
                    bank = K.psum[:, m % 4, :]
                    dve.wait_ge(K.pe_done.sem, pe0 + m + 1)
                    bias = b[:, g:g + 1, :].broadcast_to([P, 4, P])
                    s = c.step(dve.scalar_tensor_tensor(
                        out=mixed[:, m % 2, :].rearrange("p (n t) -> p n t", n=4),
                        in0=bank.rearrange("p (n t) -> p n t", n=4), scalar=K.col("g_sgu_v", g), in1=bias,
                        op0=ALU.mult, op1=ALU.add))
                    c.wait(s)
                    ins = dve.tensor_tensor(out=out[:, g, h * HALF:(h + 1) * HALF], in0=mixed[:, m % 2, :],
                                            in1=zu[:, g, h * HALF:(h + 1) * HALF], op=ALU.mult)
                    c.step(ins)
                K.normed_at = normed
                K.dve_done.n = c.n

            @block.scalar
            def _(act):
                act.wait_ge(K.dve_done.sem, dve0 + 4 * NT)
                act.activation(ms[:], ms[:], ACT.Sqrt, scale=1.0 / P, bias=K.col("eps")) \
                    .then_inc(K.act_done.sem, 1)

            @block.tensor
            def _(pe):
                pe.wait_ge(K.dve_done.sem, K.normed_at)
                for m in range(8):
                    g, h = m // 2, m % 2
                    if m >= 4:
                        pe.wait_ge(K.dve_done.sem, K.normed_at + 2 * (m - 4) + 1)
                    for q in range(4):
                        n = h * 4 + q
                        mm = pe.matmul(K.psum[:, m % 4, q * P:(q + 1) * P], zv[:, n, g * P:(g + 1) * P],
                                       w[:, g, :], start=True, stop=True)
                    mm.then_inc(K.pe_done.sem, 1)
    K.load_done.n += 32
    K.act_done.n += 1
    K.pe_done.n += 8


def attention(nc, K, rot, val, w_idx, out):
    Q, KK, QI, KI = 0, 4, 5, 9
    with ExitStack() as ctx:
        sig = {name: K.flag(name) for name in (
            "scores_ready", "relu_done", "acc_done", "causal_done", "mask_step", "logits_ready", "logits_masked",
            "exp_done", "sum_inverted", "p_ready", "p_turned", "p_copied", "pv_ready", "y_copied")}
        sig = {name: s.sem for name, s in sig.items()}
        relu = K.sbuf(ctx, "relu_scores", [P, 2, S])
        score = K.sbuf(ctx, "score", [P, S])
        never = K.sbuf(ctx, "never", [P, S])
        logit = K.sbuf(ctx, "logits", [P, 2, S])
        turned = K.sbuf(ctx, "p_turned_sbuf", [P, 2, NT, 4, P])
        top = K.sbuf(ctx, "top8", [P, 8])
        low = K.sbuf(ctx, "minus_max", [P, HEADS])
        total = K.sbuf(ctx, "exp_sum", [P, HEADS])
        psum = K.psum
        rounds = TOPK // 8

        def pair(m, n):
            if n <= HALF:
                return psum[:, 2 * (m % 2), 0:n]
            return psum[:, 2 * (m % 2):2 * (m % 2) + 2, :].rearrange("p b f -> p (b f)")[:, 0:n]

        with nc.Block() as block:
            @block.tensor
            def _(pe):
                def product(m, lhs, rhs, n):
                    for lo in range(0, n, HALF):
                        w = min(HALF, n - lo)
                        mm = pe.matmul(psum[:, 2 * (m % 2) + lo // HALF, 0:w], lhs, rhs[:, lo:lo + w],
                                       start=True, stop=True)
                    return mm

                def turn(b, h):
                    g, j = h // 4, h % 4
                    pe.wait_ge(sig["p_ready"], HEADS * b + h + 1)
                    if b or h:
                        pe.wait_ge(sig["p_copied"], HEADS * b + h)
                    for c in range(b + 1):
                        mm = pe.transpose(psum[:, 4 + c // 4, (c % 4) * P:(c % 4 + 1) * P],
                                          logit[:, h % 2, c * P:(c + 1) * P], K.const("ident"))
                    mm.then_inc(sig["p_turned"], 1)

                def values(b, g):
                    pe.wait_ge(sig["p_copied"], HEADS * b + 4 * g + 4)
                    if b:
                        pe.wait_ge(sig["y_copied"], 2 * (b - 1) + g + 1)
                    for c in range(b + 1):
                        mm = pe.matmul(psum[:, 6 + g, :], val[:, c, :], turned[:, g, c, :, :],
                                       start=(c == 0), stop=(c == b))
                    mm.then_inc(sig["pv_ready"], 1)

                for b in range(NT):
                    n, blk = (b + 1) * P, slice(b * P, (b + 1) * P)
                    for h in range(HEADS):
                        if h >= 2:
                            pe.wait_ge(sig["relu_done"], HEADS * b + h - 1)
                        elif b:
                            pe.wait_ge(sig["logits_masked"], HEADS * (b - 1) + 6 + h + 1)
                        at = slice((h % 2) * HD, (h % 2 + 1) * HD)
                        product(h, rot[at, QI + h // 2, blk], rot[at, KI, :], n).then_inc(sig["scores_ready"], 1)
                    for h in range(HEADS):
                        if h >= 2:
                            pe.wait_ge(sig["logits_masked"], HEADS * b + h - 1)
                        else:
                            pe.wait_ge(sig["relu_done"], HEADS * b + 6 + h + 1)
                        g, j = h // 4, h % 4
                        at = slice(g * HD, (g + 1) * HD)
                        product(h, rot[at, Q + j, blk], rot[at, KK, :], n).then_inc(sig["logits_ready"], 1)
                        if h >= 1:
                            turn(b, h - 1)
                        if h == 5:
                            values(b, 0)
                    turn(b, 7)
                    values(b, 1)

            @block.scalar
            def _(act):
                def copy_turned(b, h):
                    g, j = h // 4, h % 4
                    act.wait_ge(sig["p_turned"], HEADS * b + h + 1)
                    if b:
                        act.wait_ge(sig["pv_ready"], 2 * (b - 1) + g + 1)
                    act.activation(turned[:, g, 0:b + 1, j, :],
                                   psum[:, 4:6, :].rearrange("p b (c t) -> p (b c) t", t=P)[:, 0:b + 1, :],
                                   ACT.Copy).then_inc(sig["p_copied"], 1)

                def copy_y(b, g):
                    act.wait_ge(sig["pv_ready"], 2 * b + g + 1)
                    at = slice(g * HD, (g + 1) * HD)
                    act.activation(out[at, :, b * P:(b + 1) * P],
                                   psum[at, 6 + g, :].rearrange("p (j t) -> p j t", j=4), ACT.Copy) \
                        .then_inc(sig["y_copied"], 1)

                for b in range(NT):
                    n = (b + 1) * P
                    for h in range(HEADS):
                        act.wait_ge(sig["scores_ready"], HEADS * b + h + 1)
                        if b or h >= 2:
                            act.wait_ge(sig["acc_done"], HEADS * b + h - 1)
                        act.activation(relu[:, h % 2, 0:n], pair(h, n), ACT.Relu, scale=HD ** -0.5) \
                            .then_inc(sig["relu_done"], 1)
                    for h in range(HEADS):
                        act.wait_ge(sig["logits_masked"], HEADS * b + h + 1)
                        act.activation(logit[:, h % 2, 0:n], logit[:, h % 2, 0:n], ACT.Exp, scale=-1.0,
                                       bias=low[:, h:h + 1], accum_out=total[:, h:h + 1]) \
                            .then_inc(sig["exp_done"], 1)
                        if h >= 1:
                            copy_turned(b, h - 1)
                        if h == 5:
                            copy_y(b, 0)
                    copy_turned(b, 7)
                    copy_y(b, 1)

            @block.gpsimd
            def _(pool):
                for b in range(NT):
                    pool.wait_ge(sig["acc_done"], HEADS * (b + 1))
                    own = score[:, b * P:(b + 1) * P]
                    pool.affine_select(out=own, in_=own, pattern=[[-1, P]], compare_op=ALU.is_ge, fill=FAR,
                                       base=0, channel_multiplier=1).then_inc(sig["causal_done"], 1)

            @block.vector
            def _(dve):
                steps = 0
                for b in range(NT):
                    n = (b + 1) * P
                    for h in range(HEADS):
                        w = w_idx[:, b, h:h + 1]
                        dve.wait_ge(sig["relu_done"], HEADS * b + h + 1)
                        if h == 0:
                            ins = dve.tensor_scalar(score[:, 0:n], relu[:, 0, 0:n], w, None, op0=ALU.mult)
                        else:
                            dve.wait_ge(sig["acc_done"], HEADS * b + h)
                            ins = dve.scalar_tensor_tensor(out=score[:, 0:n], in0=relu[:, h % 2, 0:n], scalar=w,
                                                           in1=score[:, 0:n], op0=ALU.mult, op1=ALU.add)
                        ins.then_inc(sig["acc_done"], 1)
                    dve.wait_ge(sig["causal_done"], b + 1)
                    if n > TOPK:
                        for r in range(rounds):
                            dve.max(top[:], score[:, 0:n]).then_inc(sig["mask_step"], 1)
                            steps += 1
                            dve.wait_ge(sig["mask_step"], steps)
                            dve.match_replace(score[:, 0:n], top[:], score[:, 0:n], TAKEN) \
                                .then_inc(sig["mask_step"], 1)
                            steps += 1
                            dve.wait_ge(sig["mask_step"], steps)
                        ins = dve.tensor_scalar(never[:, 0:n], score[:, 0:n], 0.5 * (TAKEN + FAR), NEVER,
                                                op0=ALU.is_gt, op1=ALU.mult)
                    else:
                        ins = dve.tensor_scalar(never[:, 0:n], score[:, 0:n], 0.5 * FAR, NEVER,
                                                op0=ALU.is_lt, op1=ALU.mult)
                    ins.then_inc(sig["mask_step"], 1)
                    steps += 1
                    dve.wait_ge(sig["mask_step"], steps)

                    def normalise(h):
                        dve.wait_ge(sig["exp_done"], HEADS * b + h + 1)
                        dve.reciprocal(total[:, h:h + 1], total[:, h:h + 1]).then_inc(sig["sum_inverted"], 1)
                        dve.wait_ge(sig["sum_inverted"], HEADS * b + h + 1)
                        p = logit[:, h % 2, 0:n]
                        dve.tensor_scalar(p, p, total[:, h:h + 1], None, op0=ALU.mult) \
                            .then_inc(sig["p_ready"], 1)
                    for h in range(HEADS):
                        dve.wait_ge(sig["logits_ready"], HEADS * b + h + 1)
                        if b or h >= 2:
                            dve.wait_ge(sig["p_turned"], HEADS * b + h - 1)
                        dve.tensor_tensor_reduce(out=logit[:, h % 2, 0:n], in0=pair(h, n), in1=never[:, 0:n],
                                                 scale=-HD ** -0.5, scalar=3.0e38, op0=ALU.add, op1=ALU.min,
                                                 accum_out=low[:, h:h + 1]).then_inc(sig["logits_masked"], 1)
                        if h >= 1:
                            normalise(h - 1)
                    normalise(7)


def squared_relu_mlp(nc, K, h, w_up, w_down, out):
    with ExitStack() as ctx:
        hidden = K.sbuf(ctx, "hidden", [P, FT, HALF])
        relu = K.sbuf(ctx, "relu", [P, 2, HALF])
        for half in range(S // HALF):
            at = half * HALF
            dense(nc, K, w_up, FT, 1, KT, lambda k, lo, n: h[:, k, at + lo:at + lo + n], HALF,
                  lambda eng, acc, t, j: eng.activation(relu[:, j, :], acc, ACT.Relu),
                  post=lambda eng, t, j: eng.tensor_tensor(
                      out=hidden[:, bass.ds(t, 1), :], in0=relu[:, j:j + 1, :], in1=relu[:, j:j + 1, :],
                      op=ALU.mult))
            dense(nc, K, w_down, KT, FT // KT, KT, lambda k, lo, n: hidden[:, k, lo:lo + n], HALF,
                  lambda eng, acc, t, j: eng.activation(out[:, bass.ds(t, 1), at:at + HALF], acc, ACT.Copy))


def add_tiles(nc, K, x, o):
    with nc.Block() as block:
        @block.vector
        def _(dve):
            for t in range(0, KT, 2):
                dve.tensor_tensor(out=x[:, t, :], in0=x[:, t, :], in1=o[:, t, :], op=ALU.add)

        @block.gpsimd
        def _(pool):
            for t in range(1, KT, 2):
                pool.tensor_tensor(out=x[:, t, :], in0=x[:, t, :], in1=o[:, t, :], op=ALU.add)


R_CONSTS = [("transposed", 4 * P), ("minus_lower", P), ("lower", 6 * P), ("upper", 6 * P), ("no_reset", S)]
R_AT = {}
_n = 0
for _name, _k in R_CONSTS:
    R_AT[_name] = (_n, _k)
    _n += _k
N_R = _n
ALPHA, RHO, BETA, KAPPA, BETA_END, KAPPA_END, V_PART, N_PARTS = 0, 1, 2, 3, 4, 5, 6, 7


def rwkv_features(nc, K, zm, gate, bonus, parts_dram, decay_dram):
    dram = K.dram
    with ExitStack() as ctx:
        def buf(name, shape=(P, S)):
            return K.sbuf(ctx, name, list(shape))
        up = buf("lora_up", (P, 2, W2))
        no_reset = buf("no_reset", (P, S))
        rate, a, kk, norm, k_mod, b = (buf(n) for n in ("rate", "a", "kk", "norm", "k_mod", "b"))
        run, tmp, e = (buf(n) for n in ("run", "tmp", "exps"))
        end = buf("decay_end", (P, WT, S // CH))
        parts = buf("parts", (P, 6, S))
        load0 = K.load_done.n
        pe_sem, act_sem, dve_sem, st_sem = (K.pe_done.sem, K.act_done.sem, K.dve_done.sem, K.store_done.sem)
        pe0, act0, dve0, st0 = K.pe_done.n, K.act_done.n, K.dve_done.n, K.store_done.n
        PE_PER, ACT_PER, DVE_PER, ST_PER = 3, 10, 19, 9 * 16
        R, KF, V = 0, 4, 8
        psum = K.psum

        def two(bank):
            return psum[:, bank:bank + 2, :].rearrange("p b f -> p (b f)")

        with nc.Block() as block:
            @block.sync
            def _(sp):
                sp.dma_start(up[:], dram["lora_up"]).then_inc(K.load_done.sem, 16)
                sp.dma_start(no_reset[:], dram["r_consts"][:, R_AT["no_reset"][0]:R_AT["no_reset"][0] + S]) \
                    .then_inc(K.load_done.sem, 16)
                for j in range(WT):
                    sp.wait_ge(dve_sem, dve0 + DVE_PER * (j + 1))
                    for c in range(6):
                        sp.dma_start(parts_dram[:, :, c, j, :].rearrange("n p t -> p n t"),
                                     parts[:, c, :].rearrange("p (n t) -> p n t", t=P)).then_inc(st_sem, 16)
                    sp.dma_start(parts_dram[:, :, V_PART, j, :].rearrange("n p t -> p n t"),
                                 zm[:, V + j, :].rearrange("p (n t) -> p n t", t=P)).then_inc(st_sem, 16)
                    for half in range(2):
                        sp.dma_start(decay_dram[:, 2 * j + half, :], end[half * HD:(half + 1) * HD, j, :]) \
                            .then_inc(st_sem, 16)
                sp.wait_ge(st_sem, st0 + ST_PER * WT)

            @block.tensor
            def _(pe):
                pe.wait_ge(K.load_done.sem, load0 + 32)
                pe.wait_ge(act_sem, act0 + 2)
                for j in range(WT):
                    cols = slice(j * P, (j + 1) * P)
                    if j:
                        pe.wait_ge(act_sem, act0 + 2 + ACT_PER * (j - 1) + 3)
                        pe.wait_ge(dve_sem, dve0 + DVE_PER * j)
                    for h in range(2):
                        at = slice(h * HALF, (h + 1) * HALF)
                        pe.matmul(psum[:, h, :], up[0:64, 0, cols], zm[0:64, 12, at], start=True, stop=True)
                        pe.matmul(psum[:, 2 + h, :], up[64:128, 0, cols], zm[64:128, 12, at],
                                  start=True, stop=True)
                        mm = pe.matmul(psum[:, 4 + h, :], up[:, 1, cols], zm[:, 13, at], start=True, stop=True)
                    mm.then_inc(pe_sem, 1)
                    pe.wait_ge(act_sem, act0 + 2 + ACT_PER * j + 4)
                    for h in range(2):
                        mm = pe.matmul(psum[:, 6 + h, :], K.const("head_ones"), norm[:, h * HALF:(h + 1) * HALF],
                                       start=True, stop=True)
                    mm.then_inc(pe_sem, 1)
                    pe.wait_ge(dve_sem, dve0 + DVE_PER * j + 14)
                    for h in range(2):
                        mm = pe.matmul(psum[:, 6 + h, :], K.const("head_ones"), tmp[:, h * HALF:(h + 1) * HALF],
                                       start=True, stop=True)
                    mm.then_inc(pe_sem, 1)

            @block.scalar
            def _(act):
                c = Chain(act, K.act_done)
                c.step(act.activation(zm[0:64, 12, :], zm[0:64, 12, :], ACT.Tanh))
                c.step(act.activation(zm[:, 13, :], zm[:, 13, :], ACT.Sigmoid))
                for j in range(WT):
                    base = dve0 + DVE_PER * j
                    act.wait_ge(pe_sem, pe0 + PE_PER * j + 1)
                    if j:
                        act.wait_ge(dve_sem, base)
                    c.step(act.activation(rate[:], two(0), ACT.Sigmoid, bias=K.col("w0", j)))
                    c.step(act.activation(a[:], two(2), ACT.Sigmoid, bias=K.col("a0", j)))
                    c.step(act.activation(gate[:, j, :], two(4), ACT.Copy))
                    act.wait_ge(dve_sem, base + 1)
                    c.step(act.activation(norm[:], kk[:], ACT.Square))
                    act.wait_ge(pe_sem, pe0 + PE_PER * j + 2)
                    c(act.activation(norm[:], two(6), ACT.Sqrt))
                    act.wait_ge(dve_sem, base + 9)
                    c.step(act.activation(e[:], tmp[:], ACT.Exp, scale=-DECAY_SCALE))
                    act.wait_ge(dve_sem, base + 10)
                    c.step(act.activation(e[:], run[:], ACT.Exp, scale=-DECAY_SCALE))
                    act.wait_ge(dve_sem, base + 11)
                    c.step(act.activation(e[:], run[:], ACT.Exp, scale=DECAY_SCALE))
                    c.step(act.activation(end[:, j, :], run[:, CH - 1:S:CH], ACT.Exp, scale=-DECAY_SCALE))
                    act.wait_ge(dve_sem, base + 16)
                    c.step(act.activation(e[:], run[:], ACT.Exp, scale=-DECAY_SCALE))
                K.act_done.n = c.n

            @block.vector
            def _(dve):
                c = Chain(dve, K.dve_done)
                dve.wait_ge(K.load_done.sem, load0 + 32)
                for j in range(WT):
                    r, k, v = zm[:, R + j, :], zm[:, KF + j, :], zm[:, V + j, :]
                    abase = act0 + 2 + ACT_PER * j
                    c(dve.tensor_scalar(kk[:], k, K.col("k_k", j), None, op0=ALU.mult))
                    dve.wait_ge(act_sem, abase + 5)
                    c(dve.tensor_scalar(norm[:], norm[:], 1e-12, None, op0=ALU.max))
                    c(dve.reciprocal(norm[:], norm[:]))
                    c(dve.tensor_tensor(out=kk[:], in0=kk[:], in1=norm[:], op=ALU.mult))
                    c(dve.tensor_scalar(k_mod[:], a[:], -1.0, K.col("k_a", j), op0=ALU.add, op1=ALU.mult))
                    c(dve.scalar_tensor_tensor(out=k_mod[:], in0=k_mod[:], scalar=1.0, in1=k,
                                               op0=ALU.add, op1=ALU.mult))
                    c(dve.tensor_tensor(out=b[:], in0=kk[:], in1=a[:], op=ALU.mult))
                    c(dve.tensor_tensor_scan(run[:], no_reset[:], rate[:], 0.0, ALU.mult, ALU.add))
                    c(dve.tensor_tensor(out=tmp[:], in0=run[:], in1=rate[:], op=ALU.subtract))
                    if j:
                        dve.wait_ge(st_sem, st0 + ST_PER * j)
                    dve.wait_ge(act_sem, abase + 6)
                    c(dve.tensor_tensor(out=parts[:, ALPHA, :], in0=e[:], in1=kk[:], op=ALU.mult))
                    dve.wait_ge(act_sem, abase + 7)
                    c(dve.tensor_tensor(out=parts[:, RHO, :], in0=e[:], in1=r, op=ALU.mult))
                    dve.wait_ge(act_sem, abase + 8)
                    c(dve.tensor_tensor(out=parts[:, BETA, :], in0=e[:], in1=b[:], op=ALU.mult))
                    c(dve.tensor_tensor(out=parts[:, KAPPA, :], in0=e[:], in1=k_mod[:], op=ALU.mult))
                    c(dve.scalar_tensor_tensor(out=tmp[:], in0=r, scalar=K.col("r_k", j), in1=k_mod[:],
                                               op0=ALU.mult, op1=ALU.mult))
                    dve.wait_ge(act_sem, abase + 9)
                    left = run[:].rearrange("p (c t) -> p c t", t=CH)
                    c(dve.tensor_copy(norm[:, 0:S // CH], run[:, CH - 1:S:CH]))
                    c(dve.tensor_tensor(out=left, in0=norm[:, 0:S // CH].unsqueeze(2).broadcast_to([P, S // CH, CH]),
                                        in1=left, op=ALU.subtract))
                    dve.wait_ge(act_sem, abase + 10)
                    c(dve.tensor_tensor(out=parts[:, BETA_END, :], in0=e[:], in1=b[:], op=ALU.mult))
                    c(dve.tensor_tensor(out=parts[:, KAPPA_END, :], in0=e[:], in1=k_mod[:], op=ALU.mult))
                    dve.wait_ge(pe_sem, pe0 + PE_PER * j + 3)
                    c(dve.tensor_tensor(out=bonus[:, j, :], in0=two(6), in1=v, op=ALU.mult))
                K.dve_done.n = c.n
    K.load_done.n += 32
    K.pe_done.n += PE_PER * WT
    K.store_done.n += ST_PER * WT


def shift_mix(nc, K, h, zm):
    with ExitStack() as ctx:
        one_less = K.sbuf(ctx, "one_less_mu", [P, SHIFT_TILES])
        before = K.sbuf(ctx, "z_before", [P, 2, S + 1])
        dve0 = K.dve_done.n
        with nc.Block() as block:
            @block.vector
            def _(dve):
                dve.memset(before[:, :, 0:1], 0.0)
                dve.tensor_scalar(one_less[:], K.col("mu", 0, SHIFT_TILES), -1.0, 1.0, op0=ALU.mult, op1=ALU.add) \
                    .then_inc(K.dve_done.sem, 1)
                dve.wait_ge(K.dve_done.sem, dve0 + 1)
        K.dve_done.n += 1

        def drain(eng, acc, t, j):
            eng.activation(before[:, j, 1:S + 1], acc.rearrange("p b f -> p (b f)"), ACT.Copy)
            return eng.activation(zm[:, bass.ds(t, 1), :], acc, ACT.Identity, scale=one_less[:, bass.ds(t, 1)])

        def add(eng, t, j):
            tile = zm[:, bass.ds(t, 1), :]
            return eng.scalar_tensor_tensor(
                out=tile, in0=before[:, j:j + 1, 0:S], scalar=K.cols[:, bass.ds(t + COL_AT["mu"][0], 1)], in1=tile,
                op0=ALU.mult, op1=ALU.add)
        dense(nc, K, K.dram["w_shift"], SHIFT_TILES, 1, KT, lambda k, lo, n: h[:, k, lo:lo + n], S, drain, post=add)


def rwkv_chunks(nc, K, parts_dram, decay_dram, y):
    H = HEADS
    with ExitStack() as ctx:
        def buf(name, shape):
            return K.sbuf(ctx, name, list(shape))

        def signals(*names):
            return [K.flag(n).sem for n in names]
        (loaded0, loaded1, masked, turned, copied, pe_low, low_masked, t_made, pe_w, w_copied, pe_delta,
         t_grown, pe_bv, bv_copied, pe_gu, gu_copied, pe_m, m_made, pe_rho, rho_copied, pe_z, z_copied, pe_y,
         y_copied, pe_abde) = signals(
            "parts_loaded_0", "parts_loaded_1", "abde_masked", "parts_turned", "turned_copied",
            "a_ready", "a_masked", "t_started", "w_ready", "w_copied", "delta_ready", "t_grown", "bv_ready",
            "bv_copied", "gu_ready", "gu_copied", "m_ready", "m_made", "rho_ready", "rho_copied", "z_ready",
            "z_copied", "y_ready", "y_tile_copied", "abde_ready")
        loaded = [loaded0, loaded1]
        con = buf("r_consts_sbuf", (P, N_R - S))
        decay = buf("decay", (HD, H, S // CH))
        parts = buf("parts_in", (P, 2, N_PARTS, WT, P))
        abde = buf("abde", (P, H, 4, P))
        low = buf("a_low", (P, H, P))
        T = buf("t", (P, H, P))
        TT = buf("t_turned", (P, H, P))
        W = buf("w", (P, H, P))
        tok = buf("token_major", (P, 2, W2))
        ends = buf("ends", (P, 2, 2, W2))
        bv = buf("bv", (P, W2))
        gu = buf("minus_g_u", (P, 2, W2))
        m_t = buf("m_turned", (HD, 2, H, HD))
        dd = buf("decay_diagonal", (HD, 2, H, HD))
        rho = buf("rho_less_dg", (HD, H, P))
        z = buf("state", (HD, 2, H, HD))
        idle = buf("idle", (P, 3))
        psum = K.psum
        load0 = K.load_done.n
        LEVELS = [2, 4, 8, 16, 32]

        def mask(name, i=0, n=P):
            at = R_AT[name][0] + i * n
            return con[:, at:at + n]

        def head(h):
            return slice((h % 2) * HD, (h % 2 + 1) * HD), h // 2

        def four(bank):
            return psum[:, bank, :].rearrange("p (h t) -> p h t", h=4)

        def body(eng, per_tile):
            with eng.Fori(0, NT // 2) as i:
                for s in range(2):
                    per_tile(i, s)

        def count(i, s, per, k):
            return i * (2 * per) + (s * per + k)

        with nc.Block() as block:
            @block.sync
            def _(sp):
                sp.dma_start(con[:], K.dram["r_consts"][:, 0:N_R - S]).then_inc(K.load_done.sem, 16)
                sp.dma_start(decay[:], decay_dram).then_inc(K.load_done.sem, 16)

                def tile(i, s):
                    sp.wait_ge(y_copied, count(i, s, 1, 1))
                    sp.dma_start(parts[:, s], parts_dram[i * 2 + s]).then_inc(loaded[s], 16)
                body(sp, tile)

            @block.gpsimd
            def _(pool):
                pool.wait_ge(K.load_done.sem, load0 + 32)

                def tile(i, s):
                    pool.wait_ge(m_made, count(i, s, 2, 1))
                    for c in range(2):
                        ins = pool.tensor_tensor(
                            out=dd[:, c], in0=K.const("ident")[0:HD, 0:HD].unsqueeze(1).broadcast_to([HD, H, HD]),
                            in1=decay[:, :, bass.ds(i * 4 + (2 * s + c), 1)].broadcast_to([HD, H, HD]), op=ALU.mult)
                    ins.then_inc(K.pool_done.sem, 1)
                body(pool, tile)

            @block.tensor
            def _(pe):
                pe.wait_ge(K.load_done.sem, load0 + 32)

                def tile(i, s):
                    x = parts[:, s]
                    pe.wait_ge(loaded[s], i * 16 + 16)
                    for h in range(H):
                        at, j = head(h)
                        if h >= 4:
                            pe.wait_ge(masked, count(i, s, H, h - 3))
                        pe.matmul(psum[:, h % 4, 0:2 * P], x[at, BETA, j, :], x[at, 0:2, j, :],
                                  start=True, stop=True)
                        pe.matmul(psum[:, h % 4, 2 * P:4 * P], x[at, KAPPA, j, :], x[at, 0:2, j, :],
                                  start=True, stop=True).then_inc(pe_abde, 1)
                    for h in range(H):
                        at, j = head(h)
                        mm = pe.matmul(four(4 + h % 2)[:, j, :], x[at, ALPHA, j, :], x[at, BETA, j, :],
                                       start=True, stop=True)
                        if h >= H - 2:
                            mm.then_inc(pe_low, 1)
                    for m, part in enumerate((ALPHA, BETA_END, KAPPA_END, V_PART)):
                        if m >= 2:
                            pe.wait_ge(copied, count(i, s, 4, m - 1))
                        for j in range(WT):
                            mm = pe.transpose(psum[:, 6 + m % 2, j * P:(j + 1) * P], x[:, part, j, :],
                                              K.const("ident"))
                        mm.then_inc(turned, 1)
                    pe.wait_ge(t_made, count(i, s, 1, 1))
                    for lv in range(len(LEVELS)):
                        last = lv == len(LEVELS) - 1
                        for q in range(2):
                            if lv:
                                pe.wait_ge(t_grown, count(i, s, 2 * len(LEVELS), 2 * (lv - 1) + q + 1))
                            for h in range(4 * q, 4 * q + 4):
                                mm = pe.matmul(four(3 * q)[:, h % 4, :], abde[:, h, 0, :], T[:, h, :],
                                               start=True, stop=True)
                            mm.then_inc(pe_w, 1)
                        for q in range(2):
                            pe.wait_ge(w_copied, count(i, s, 2 * len(LEVELS), 2 * lv + q + 1))
                            for h in range(4 * q, 4 * q + 4):
                                if not last:
                                    pe.matmul(four(3 * q + 1)[:, h % 4, :], TT[:, h, :], W[:, h, :],
                                              start=True, stop=True)
                                mm = pe.matmul(four(3 * q + 2)[:, h % 4, :], W[:, h, :], TT[:, h, :],
                                               start=True, stop=True)
                            mm.then_inc(pe_delta, 1)
                    pe.wait_ge(copied, count(i, s, 4, 4))
                    for h in range(H):
                        mm = pe.matmul(psum[:, 6, h * HD:(h + 1) * HD], abde[:, h, 2, :],
                                       tok[:, 1, h * HD:(h + 1) * HD], start=True, stop=True)
                    mm.then_inc(pe_bv, 1)
                    pe.wait_ge(t_grown, count(i, s, 2 * len(LEVELS), 2 * len(LEVELS)))
                    for h in range(H):
                        cols = slice(h * HD, (h + 1) * HD)
                        pe.matmul(psum[:, 7, cols], TT[:, h, :], tok[:, 0, cols], start=True, stop=True)
                    pe.wait_ge(bv_copied, count(i, s, 1, 1))
                    for h in range(H):
                        cols = slice(h * HD, (h + 1) * HD)
                        mm = pe.matmul(psum[:, 0, cols], TT[:, h, :], bv[:, cols], start=True, stop=True)
                    mm.then_inc(pe_gu, 1)
                    pe.wait_ge(gu_copied, count(i, s, 1, 1))
                    for c in range(2):
                        for h in range(H):
                            cols = slice(h * HD, (h + 1) * HD)
                            mm = pe.matmul(psum[0:HD, 1 + c, cols], gu[:, 0, cols], ends[:, c, 0, cols],
                                           start=True, stop=True)
                        mm.then_inc(pe_m, 1)
                    for h in range(H):
                        at, j = head(h)
                        o = psum[0:HD, 3 + h // 4, (h % 4) * P:(h % 4 + 1) * P]
                        pe.matmul(o, gu[:, 0, h * HD:(h + 1) * HD], abde[:, h, 1, :], start=(h % 4 == 0), stop=False,
                                  skip_group_check=True)
                        mm = pe.matmul(o, K.const("ident")[:, at], x[:, RHO, j, :], start=False, stop=(h % 4 == 3),
                                       skip_group_check=True)
                    mm.then_inc(pe_rho, 1)
                    for c in range(2):
                        o = psum[0:HD, 5 + c, :]
                        for h in range(H):
                            cols = slice(h * HD, (h + 1) * HD)
                            pe.matmul(o[:, cols], ends[:, c, 1, cols], tok[:, 1, cols], start=(h == 0), stop=False,
                                      skip_group_check=True)
                            if h == H - 1:
                                pe.wait_ge(m_made, count(i, s, 2, c + 2))
                                pe.wait_ge(z_copied, count(i, s, 2, c + 1))
                            pe.matmul(o[:, cols], ends[:, c, 0, cols], gu[:, 1, cols], start=False, stop=False,
                                      skip_group_check=True)
                        for h in range(H):
                            cols = slice(h * HD, (h + 1) * HD)
                            mm = pe.matmul(o[:, cols], m_t[:, c, h, :], z[:, c, h, :], start=False, stop=(h == H - 1),
                                           skip_group_check=True)
                        if c == 0:
                            mm.then_inc(pe_z, 1)
                    pe.wait_ge(rho_copied, count(i, s, 1, 1))
                    for odd in range(2):
                        o = psum[:, 7 if odd == 0 else 0, :]
                        for j in range(WT):
                            h = 2 * j + odd
                            pair = slice(j * P, (j + 1) * P)
                            cols = slice(j * P, (j + 1) * P)
                            pe.matmul(o[:, cols], tok[:, 1, pair], abde[:, h, 3, :], start=(j == 0), stop=False,
                                      skip_group_check=True)
                            pe.matmul(o[:, cols], gu[:, 1, pair], abde[:, h, 1, :], start=False, stop=False,
                                      skip_group_check=True)
                            for c in range(2):
                                mm = pe.matmul(o[:, j * P + c * CH:j * P + (c + 1) * CH], z[:, c, 2 * j:2 * j + 2, :],
                                               rho[:, h, c * CH:(c + 1) * CH], start=False,
                                               stop=(j == WT - 1 and c == 1), skip_group_check=True)
                    mm.then_inc(pe_y, 1)
                    pe.wait_ge(z_copied, count(i, s, 2, 3))
                    pe.wait_ge(y_copied, count(i, s, 1, 3))
                body(pe, tile)

            @block.scalar
            def _(act):
                act.wait_ge(z_copied, 1)

                def tile(i, s):
                    for m in range(4):
                        act.wait_ge(turned, count(i, s, 4, m + 1))
                        of = psum[:, 6 + m % 2, :]
                        if m in (0, 3):
                            ins = act.activation(tok[:, m // 3, :], of, ACT.Copy)
                        else:
                            for c in range(2):
                                rows = slice(c * CH, (c + 1) * CH)
                                ins = act.activation(ends[rows, c, m - 1, :], of[rows], ACT.Copy)
                        ins.then_inc(copied, 1)
                    for lv in range(len(LEVELS)):
                        for q in range(2):
                            act.wait_ge(pe_w, count(i, s, 2 * len(LEVELS), 2 * lv + q + 1))
                            act.activation(W[:, 4 * q:4 * q + 4, :], four(3 * q), ACT.Copy).then_inc(w_copied, 1)
                    act.wait_ge(pe_bv, count(i, s, 1, 1))
                    act.activation(bv[:], psum[:, 6, :], ACT.Copy).then_inc(bv_copied, 1)
                    act.wait_ge(pe_gu, count(i, s, 1, 1))
                    act.activation(gu[:, 0, :], psum[:, 7, :], ACT.Copy, scale=-1.0)
                    act.activation(gu[:, 1, :], psum[:, 0, :], ACT.Copy, scale=-1.0).then_inc(gu_copied, 1)
                    act.wait_ge(pe_rho, count(i, s, 1, 1))
                    act.activation(rho[:, 0:4, :], four(3)[0:HD], ACT.Copy)
                    act.activation(rho[:, 4:8, :], four(4)[0:HD], ACT.Copy).then_inc(rho_copied, 1)
                body(act, tile)

            @block.vector
            def _(dve):
                dve.memset(ends[:], 0.0)
                dve.memset(z[:], 0.0).then_inc(z_copied, 1)
                dve.sem_inc(m_made, 1)
                dve.sem_inc(y_copied, 2)
                dve.wait_ge(K.load_done.sem, load0 + 32)

                def tile(i, s):
                    for h in range(H):
                        dve.wait_ge(pe_abde, count(i, s, H, h + 1))
                        dve.tensor_tensor(out=abde[:, h].rearrange("p a t -> p (a t)"), in0=psum[:, h % 4, :],
                                          in1=mask("transposed", 0, 4 * P), op=ALU.mult).then_inc(masked, 1)
                    dve.wait_ge(pe_low, count(i, s, 2, 2))
                    for q in range(2):
                        dve.tensor_tensor(out=low[:, q:H:2, :], in0=four(4 + q),
                                          in1=mask("minus_lower").unsqueeze(1).broadcast_to([P, 4, P]), op=ALU.mult) \
                            .then_inc(low_masked, 1)
                    for m in (T, TT):
                        ins = dve.tensor_copy(m[:], K.const("ident").unsqueeze(1).broadcast_to([P, H, P]))
                    ins.then_inc(low_masked, 1)
                    dve.wait_ge(low_masked, count(i, s, 3, 3))
                    dve.wait_ge(masked, count(i, s, H, H))
                    dve.memset(idle[:, 2:3], 0.0)
                    for m, name, of in ((T, "lower", low[:]), (TT, "upper", abde[:, :, 0, :])):
                        ins = dve.copy_predicated(
                            m[:], mask(name, 0).bitcast(U32).unsqueeze(1).broadcast_to([P, H, P]), of)
                    ins.then_inc(t_made, 1)
                    for lv in range(len(LEVELS)):
                        for q in range(2):
                            dve.wait_ge(pe_delta, count(i, s, 2 * len(LEVELS), 2 * lv + q + 1))
                            dve.memset(idle[:, q:q + 1], 0.0)
                            for m, name, bank in ((T, "lower", 3 * q + 1), (TT, "upper", 3 * q + 2)):
                                if lv == len(LEVELS) - 1 and m is T:
                                    continue
                                ins = dve.copy_predicated(
                                    m[:, 4 * q:4 * q + 4, :],
                                    mask(name, lv + 1).bitcast(U32).unsqueeze(1).broadcast_to([P, 4, P]), four(bank))
                            ins.then_inc(t_grown, 1)
                    dve.wait_ge(K.pool_done.sem, count(i, s, 1, K.pool_done.n + 1))
                    for c in range(2):
                        dve.wait_ge(pe_m, count(i, s, 2, c + 1))
                        dve.tensor_tensor(out=m_t[:, c], in0=psum[0:HD, 1 + c, :].rearrange("p (h k) -> p h k", h=H),
                                          in1=dd[:, c], op=ALU.add).then_inc(m_made, 1)
                    dve.wait_ge(pe_z, count(i, s, 1, 1))
                    dve.tensor_copy(z[:, 1], psum[0:HD, 5, :].rearrange("p (h k) -> p h k", h=H)).then_inc(z_copied, 1)
                    dve.wait_ge(pe_y, count(i, s, 1, 1))
                    dve.tensor_copy(z[:, 0], psum[0:HD, 6, :].rearrange("p (h k) -> p h k", h=H)).then_inc(z_copied, 1)
                    for odd in range(2):
                        rows = slice(odd * HD, (odd + 1) * HD)
                        ins = dve.tensor_copy(y[rows, :, bass.ds(i * (2 * P) + s * P, P)],
                                              psum[rows, 7 if odd == 0 else 0, :].rearrange("p (j t) -> p j t", j=WT))
                    ins.then_inc(y_copied, 1)
                body(dve, tile)
    K.load_done.n += 32
    K.pool_done.n += NT


def rwkv_finish(nc, K, y, bonus, gate):
    with ExitStack() as ctx:
        sq = K.sbuf(ctx, "centred_squares", [P, 2, S])
        root = K.sbuf(ctx, "head_root", [P, 2, S])
        pe0, act0, dve0 = K.pe_done.n, K.act_done.n, K.dve_done.n
        pe_sem, act_sem, dve_sem = K.pe_done.sem, K.act_done.sem, K.dve_done.sem

        def two(b):
            return K.psum[:, b:b + 2, :].rearrange("p b f -> p (b f)")
        with nc.Block() as block:
            @block.tensor
            def _(pe):
                for t in range(WT):
                    for h in range(2):
                        mm = pe.matmul(K.psum[:, 2 * (t % 2) + h, :], K.const("head_ones"),
                                       y[:, t, h * HALF:(h + 1) * HALF], start=True, stop=True)
                    mm.then_inc(pe_sem, 1)
                    pe.wait_ge(act_sem, act0 + 2 * t + 1)
                    for h in range(2):
                        mm = pe.matmul(K.psum[:, 4 + 2 * (t % 2) + h, :], K.const("head_ones"),
                                       sq[:, t % 2, h * HALF:(h + 1) * HALF], start=True, stop=True)
                    mm.then_inc(pe_sem, 1)

            @block.scalar
            def _(act):
                for t in range(WT):
                    act.wait_ge(dve_sem, dve0 + 5 * t + 1)
                    act.activation(sq[:, t % 2, :], y[:, t, :], ACT.Square).then_inc(act_sem, 1)
                    act.wait_ge(pe_sem, pe0 + 2 * t + 2)
                    act.activation(root[:, t % 2, :], two(4 + 2 * (t % 2)), ACT.Sqrt, scale=1.0 / HD,
                                   bias=K.col("lnx_eps")).then_inc(act_sem, 1)

            @block.vector
            def _(dve):
                c = Chain(dve, K.dve_done)
                for t in range(WT):
                    dve.wait_ge(pe_sem, pe0 + 2 * t + 1)
                    c(dve.scalar_tensor_tensor(out=y[:, t, :], in0=two(2 * (t % 2)), scalar=-1.0 / HD,
                                               in1=y[:, t, :], op0=ALU.mult, op1=ALU.add))
                    dve.wait_ge(act_sem, act0 + 2 * t + 2)
                    c(dve.reciprocal(root[:, t % 2, :], root[:, t % 2, :]))
                    c(dve.scalar_tensor_tensor(out=y[:, t, :], in0=y[:, t, :], scalar=K.col("lnx_w", t),
                                               in1=root[:, t % 2, :], op0=ALU.mult, op1=ALU.mult))
                    c(dve.scalar_tensor_tensor(out=y[:, t, :], in0=y[:, t, :], scalar=K.col("lnx_b", t),
                                               in1=bonus[:, t, :], op0=ALU.add, op1=ALU.add))
                    c(dve.tensor_tensor(out=y[:, t, :], in0=y[:, t, :], in1=gate[:, t, :], op=ALU.mult))
                K.dve_done.n = c.n
    K.pe_done.n += 2 * WT
    K.act_done.n += 2 * WT


def ssm_prepare(nc, K, s5):
    mag, power, b_t, c_re, c_im, table = s5
    N = SSM_TILES
    with ExitStack() as ctx:
        def buf(name, shape=(P, N)):
            return K.sbuf(ctx, name, list(shape))
        dt, are, small, em, theta, turns, cos, sin, half = (
            buf(n) for n in ("dt", "are", "dt_are", "expm1", "theta", "theta_turns", "cos_theta", "sin_theta",
                             "sin_half"))
        t0, t1, nr, ai, rden, cr, ci = (buf(n) for n in ("s5_t0", "s5_t1", "nr", "abar_im", "rden", "coef_re", "coef_im"))
        b_re, b_im, b1, b2 = (buf(n, (P, N, 32)) for n in ("b_re", "b_im", "bbar_re", "bbar_im"))
        tmp = buf("s5_tmp", (P, N, 64))
        a_im = K.col("a_im", 0, N)
        act0, dve0, load0, pe0 = K.act_done.n, K.dve_done.n, K.load_done.n, K.pe_done.n
        at = {}

        def wide(x, n):
            return x.unsqueeze(2).broadcast_to([P, N, n])

        with nc.Block() as block:
            @block.sync
            def _(sp):
                for to, name in ((b_re, "b_re"), (b_im, "b_im"), (c_re, "c_re"), (c_im, "c_im")):
                    sp.dma_start(to[:], K.dram[name]).then_inc(K.load_done.sem, 16)

            @block.vector
            def _(dve):
                c = Chain(dve, K.dve_done)
                dve.wait_ge(K.act_done.sem, act0 + 1)
                c(dve.tensor_scalar(are[:], K.col("a_re", 0, N), -1e-4, None, op0=ALU.min))
                c(dve.tensor_tensor(out=small[:], in0=dt[:], in1=are[:], op=ALU.mult))
                c(dve.tensor_tensor(out=theta[:], in0=dt[:], in1=a_im, op=ALU.mult))
                reduce_angle(dve, c, sin[:], turns[:], theta[:], 0.0)
                reduce_angle(dve, c, cos[:], turns[:], theta[:], 0.25)
                c(dve.tensor_scalar(theta[:], theta[:], 0.5, None, op0=ALU.mult))
                reduce_angle(dve, c, half[:], turns[:], theta[:], 0.0)
                at["angles"] = c.n
                c(dve.tensor_scalar(em[:], small[:], 1.0 / 10, 1.0, op0=ALU.mult, op1=ALU.add))
                for m in range(9, 1, -1):
                    c(dve.scalar_tensor_tensor(out=em[:], in0=em[:], scalar=1.0 / m, in1=small[:],
                                               op0=ALU.mult, op1=ALU.mult))
                    c(dve.tensor_scalar(em[:], em[:], 1.0, None, op0=ALU.add))
                c(dve.tensor_tensor(out=em[:], in0=em[:], in1=small[:], op=ALU.mult))
                dve.wait_ge(K.act_done.sem, act0 + 5)
                c(dve.tensor_scalar(t0[:], t0[:], -1.0, None, op0=ALU.add))
                c(dve.tensor_scalar(t1[:], small[:], -0.5, None, op0=ALU.is_lt))
                c(dve.copy_predicated(em[:], t1[:].bitcast(U32), t0[:]))
                c(dve.tensor_scalar(mag, em[:], 1.0, None, op0=ALU.add))
                c(dve.tensor_tensor(out=nr[:], in0=em[:], in1=cos[:], op=ALU.mult))
                c(dve.scalar_tensor_tensor(out=half[:], in0=half[:], scalar=-2.0, in1=half[:], op0=ALU.mult,
                                           op1=ALU.mult))
                c(dve.tensor_tensor(out=nr[:], in0=nr[:], in1=half[:], op=ALU.add))
                c(dve.tensor_tensor(out=ai[:], in0=mag, in1=sin[:], op=ALU.mult))
                c(dve.tensor_tensor(out=t0[:], in0=are[:], in1=are[:], op=ALU.mult))
                c(dve.tensor_tensor(out=t1[:], in0=a_im, in1=a_im, op=ALU.mult))
                c(dve.tensor_tensor(out=rden[:], in0=t0[:], in1=t1[:], op=ALU.add))
                c(dve.reciprocal(rden[:], rden[:]))
                for o, x, y, op in ((cr, are[:], a_im, ALU.add), (ci, a_im, are[:], ALU.subtract)):
                    c(dve.tensor_tensor(out=t0[:], in0=nr[:], in1=x, op=ALU.mult))
                    c(dve.tensor_tensor(out=t1[:], in0=ai[:], in1=y, op=ALU.mult))
                    c(dve.tensor_tensor(out=o[:], in0=t1[:], in1=t0[:], op=op))
                    c(dve.tensor_tensor(out=o[:], in0=o[:], in1=rden[:], op=ALU.mult))
                dve.wait_ge(K.load_done.sem, load0 + 64)
                t32 = tmp[:, :, 0:32]
                for o, x, y, op in ((b1, b_re, b_im, ALU.subtract), (b2, b_im, b_re, ALU.add)):
                    c(dve.tensor_tensor(out=o[:], in0=x[:], in1=wide(cr[:], 32), op=ALU.mult))
                    c(dve.tensor_tensor(out=t32, in0=y[:], in1=wide(ci[:], 32), op=ALU.mult))
                    c(dve.tensor_tensor(out=o[:], in0=o[:], in1=t32, op=op))
                at["bbar"] = c.n
                c(dve.tensor_scalar(c_im, c_im, -1.0, None, op0=ALU.mult))
                c(dve.tensor_copy(power[:, 0, 0, :], cos[:]))
                c(dve.tensor_copy(power[:, 1, 0, :], sin[:]))
                for m in range(1, 10):
                    pc, ps = power[:, 0, m - 1, :], power[:, 1, m - 1, :]
                    c(dve.tensor_tensor(out=t0[:], in0=pc, in1=pc, op=ALU.mult))
                    c(dve.tensor_tensor(out=t1[:], in0=ps, in1=ps, op=ALU.mult))
                    c(dve.tensor_tensor(out=power[:, 0, m, :], in0=t0[:], in1=t1[:], op=ALU.subtract))
                    c(dve.scalar_tensor_tensor(out=power[:, 1, m, :], in0=pc, scalar=2.0, in1=ps, op0=ALU.mult,
                                               op1=ALU.mult))
                c(dve.memset(table[:, 0, :, 0:1], 1.0))
                c(dve.memset(table[:, 1, :, 0:1], 0.0))
                for m in range(7):
                    n = 1 << m
                    pc, ps = wide(power[:, 0, m, :], n), wide(power[:, 1, m, :], n)
                    er, ei = table[:, 0, :, 0:n], table[:, 1, :, 0:n]
                    for o, x, y, op in ((0, er, ei, ALU.subtract), (1, ei, er, ALU.add)):
                        c(dve.tensor_tensor(out=table[:, o, :, n:2 * n], in0=x, in1=pc, op=ALU.mult))
                        c(dve.tensor_tensor(out=tmp[:, :, 0:n], in0=y, in1=ps, op=ALU.mult))
                        c(dve.tensor_tensor(out=table[:, o, :, n:2 * n], in0=table[:, o, :, n:2 * n],
                                            in1=tmp[:, :, 0:n], op=op))
                for m, x in enumerate((b1, b2)):
                    c(dve.memset(b_t[:, m], 0.0))
                for m in range(2):
                    dve.wait_ge(K.pe_done.sem, pe0 + m + 1)
                    for q in range(4):
                        rows = slice(32 * q, 32 * q + 32)
                        c(dve.tensor_copy(b_t[rows, m, q:N:4, :],
                                          K.psum[rows, m, :].rearrange("p (g k) -> p g k", g=4)))
                K.dve_done.n = c.n

            @block.scalar
            def _(act):
                c = Chain(act, K.act_done)
                c.step(act.activation(dt[:], K.col("log_dt", 0, N), ACT.Exp))
                act.wait_ge(K.dve_done.sem, at["angles"])
                c.step(act.activation(sin[:], sin[:], ACT.Sin))
                c.step(act.activation(cos[:], cos[:], ACT.Sin))
                c.step(act.activation(half[:], half[:], ACT.Sin))
                c.step(act.activation(t0[:], small[:], ACT.Exp))
                K.act_done.n = c.n

            @block.tensor
            def _(pe):
                pe.wait_ge(K.dve_done.sem, at["bbar"])
                for m, x in enumerate((b1, b2)):
                    for g in range(4):
                        mm = pe.transpose(K.psum[:, m, g * P:(g + 1) * P],
                                          x[:, 4 * g:4 * g + 4, :].rearrange("p s c -> p (s c)"), K.const("ident"))
                    mm.then_inc(K.pe_done.sem, 1)
    K.load_done.n += 64
    K.pe_done.n += 2


def ssm_scan(nc, K, s5, u, ys):
    mag, power, b_t, c_re, c_im, table = s5
    N = SSM_TILES
    with ExitStack() as ctx:
        phase = K.sbuf(ctx, "phase", [P, 2, 2, S])
        t = K.sbuf(ctx, "turned_inputs", [P, 4, S])
        x = K.sbuf(ctx, "states", [P, 4, S])
        run = K.sbuf(ctx, "scanned", [P, 2, S])
        tmp = K.sbuf(ctx, "phase_tmp", [P, HALF])
        names = ("bu_ready", "inputs_turned", "input_summed", "scanned_done", "states_turned", "state_summed",
                 "phase_built", "phase_step", "c_used", "y_summed")
        (bu_ready, in_turned, in_summed, scanned, st_turned, st_summed, built, built_step, c_used, y_summed) = (
            K.flag(n).sem for n in names)
        psum = K.psum

        def two(b):
            return psum[:, b:b + 2, :].rearrange("p b f -> p (b f)")

        with nc.Block() as block:
            @block.tensor
            def _(pe):
                def outputs(s):
                    pe.wait_ge(st_summed, 2 * (s + 1))
                    if s % 4 == 0 and s:
                        pe.wait_ge(y_summed, s // 4)
                    for m, (w, part) in enumerate(((c_re, 0), (c_im, 2))):
                        for h in range(2):
                            mm = pe.matmul(psum[:, 4 + h, :], w[:, s, :], x[:, part, h * HALF:(h + 1) * HALF],
                                           start=(s % 4 == 0 and m == 0), stop=(s % 4 == 3 and m == 1))
                    mm.then_inc(c_used, 1)

                for s in range(N):
                    if s:
                        pe.wait_ge(in_turned, 4 * s)
                    for m in range(2):
                        for h in range(2):
                            mm = pe.matmul(psum[:, 2 * m + h, :], b_t[:, m, s, :],
                                           u[:, s // 4, h * HALF:(h + 1) * HALF], start=True, stop=True)
                    mm.then_inc(bu_ready, 1)
                    if s:
                        outputs(s - 1)
                outputs(N - 1)

            @block.gpsimd
            def _(pool):
                steps = 0

                def step(ins):
                    nonlocal steps
                    steps += 1
                    ins.then_inc(built_step, 1)
                    pool.wait_ge(built_step, steps)

                def build_phase(s):
                    er, ei = phase[:, s % 2, 0, :], phase[:, s % 2, 1, :]
                    step(pool.tensor_copy(er[:, 0:P], table[:, 0, s, :]))
                    step(pool.tensor_copy(ei[:, 0:P], table[:, 1, s, :]))
                    for m in range(7, 10):
                        n = 1 << m
                        pc, ps = power[:, 0, m, s:s + 1], power[:, 1, m, s:s + 1]
                        for o, a, b, op in ((er, er, ei, ALU.subtract), (ei, ei, er, ALU.add)):
                            step(pool.tensor_scalar(o[:, n:2 * n], a[:, 0:n], pc, None, op0=ALU.mult))
                            step(pool.tensor_scalar(tmp[:, 0:n], b[:, 0:n], ps, None, op0=ALU.mult))
                            ins = pool.tensor_tensor(out=o[:, n:2 * n], in0=o[:, n:2 * n], in1=tmp[:, 0:n], op=op)
                            if m < 9 or o is er:
                                step(ins)
                            else:
                                ins.then_inc(built, 1)

                def sum_states(s):
                    pool.wait_ge(st_turned, 4 * (s + 1))
                    pool.tensor_tensor(out=x[:, 0, :], in0=x[:, 0, :], in1=x[:, 1, :], op=ALU.subtract) \
                        .then_inc(st_summed, 1)
                    pool.tensor_tensor(out=x[:, 2, :], in0=x[:, 2, :], in1=x[:, 3, :], op=ALU.add) \
                        .then_inc(st_summed, 1)

                build_phase(0)
                build_phase(1)
                for s in range(N):
                    pool.wait_ge(in_turned, 4 * (s + 1))
                    pool.tensor_tensor(out=t[:, 0, :], in0=t[:, 0, :], in1=t[:, 1, :], op=ALU.add) \
                        .then_inc(in_summed, 1)
                    pool.tensor_tensor(out=t[:, 2, :], in0=t[:, 2, :], in1=t[:, 3, :], op=ALU.subtract) \
                        .then_inc(in_summed, 1)
                    if s:
                        sum_states(s - 1)
                        if s + 1 < N:
                            build_phase(s + 1)
                sum_states(N - 1)

            @block.vector
            def _(dve):
                def turn_states(s):
                    er, ei = phase[:, s % 2, 0, :], phase[:, s % 2, 1, :]
                    dve.wait_ge(scanned, 2 * (s + 1))
                    if s:
                        dve.wait_ge(c_used, s)
                    for m, (y, e) in enumerate(((0, er), (1, ei), (0, ei), (1, er))):
                        dve.tensor_tensor(out=x[:, m, :], in0=run[:, y, :], in1=e, op=ALU.mult) \
                            .then_inc(st_turned, 1)

                def finish_channels(g):
                    dve.wait_ge(c_used, 4 * (g + 1))
                    dve.scalar_tensor_tensor(out=ys[:, g, :], in0=u[:, g, :], scalar=K.col("d_skip", g),
                                             in1=two(4), op0=ALU.mult, op1=ALU.add).then_inc(y_summed, 1)

                for s in range(N):
                    er, ei = phase[:, s % 2, 0, :], phase[:, s % 2, 1, :]
                    dve.wait_ge(built, s + 1)
                    dve.wait_ge(bu_ready, s + 1)
                    if s:
                        dve.wait_ge(scanned, 2 * s)
                    for m, (b, e) in enumerate(((0, er), (2, ei), (2, er), (0, ei))):
                        dve.tensor_tensor(out=t[:, m, :], in0=two(b), in1=e, op=ALU.mult).then_inc(in_turned, 1)
                    if s:
                        turn_states(s - 1)
                    factor = mag[:, s:s + 1].broadcast_to([P, S])
                    for m in range(2):
                        dve.wait_ge(in_summed, 2 * s + m + 1)
                        if s and m == 0:
                            dve.wait_ge(st_turned, 4 * s)
                        dve.tensor_tensor_scan(run[:, m, :], factor, t[:, 2 * m, :], 0.0, ALU.mult, ALU.add) \
                            .then_inc(scanned, 1)
                    if s and s % 4 == 0:
                        finish_channels(s // 4 - 1)
                turn_states(N - 1)
                finish_channels(N // 4 - 1)

            @block.scalar
            def _(act):
                for g in range(N // 4):
                    act.wait_ge(y_summed, g + 1)
                    act.activation(ys[:, g, :], ys[:, g, :], ACT.Gelu)


def combine(nc, K, h, ya, yb, ys):
    dram = K.dram
    with ExitStack() as ctx:
        gate = K.sbuf(ctx, "sigmoid", [P, 2, 2, HALF])

        def bias(t, half):
            return K.cols[:, bass.ds(t + COL_AT["b_glu"][0] + half * KT, 1)]

        def times(of):
            def post(eng, t, j):
                tile = of[:, bass.ds(t, 1), :].rearrange("p o (b f) -> p (o b) f", b=2)
                return eng.tensor_tensor(out=tile, in0=tile, in1=gate[:, j], op=ALU.mult)
            return post

        def from_h(k, lo, n):
            return h[:, k, lo:lo + n]

        def from_ys(k, lo, n):
            return ys[:, k, lo:lo + n]
        dense(nc, K, dram["w_glu"][0:KT], KT, 1, WT, from_ys, S,
              lambda eng, acc, t, j: eng.activation(yb[:, bass.ds(t, 1), :], acc, ACT.Identity, bias=bias(t, 0)))
        dense(nc, K, dram["w_glu"][KT:2 * KT], KT, 1, WT, from_ys, S,
              lambda eng, acc, t, j: eng.activation(gate[:, j], acc, ACT.Sigmoid, bias=bias(t, 1)), post=times(yb))
        dense(nc, K, dram["w_gates"][0:KT], KT, 1, KT, from_h, S,
              lambda eng, acc, t, j: eng.activation(gate[:, j], acc, ACT.Sigmoid), post=times(ya))
        dense(nc, K, dram["w_gates"][KT:2 * KT], KT, 1, KT, from_h, S,
              lambda eng, acc, t, j: eng.activation(gate[:, j], acc, ACT.Sigmoid), post=times(yb))
        with nc.Block() as block:
            @block.vector
            def _(dve):
                for t in range(KT):
                    dve.tensor_tensor(out=ya[:, t, :], in0=ya[:, t, :], in1=yb[:, t, :], op=ALU.add)


def build(nc, dram):
    with ExitStack() as ctx:
        K = Core(nc, ctx, dram)
        load_setup(nc, K)
        ada(nc, K)
        x_t = dram["x"].rearrange("(t p) s -> p t s", p=P)
        merged = K.sbuf(ctx, "merged", [P, KT, S])
        with ExitStack() as proj:
            zu = K.sbuf(proj, "z_u", [P, 4, S])
            rot = K.sbuf(proj, "q_k_qi_ki", [P, 10, S])
            zv = K.sbuf(proj, "z_v", [P, NT, D_SGU])
            val = K.sbuf(proj, "values", [P, NT, P])
            w_idx = K.sbuf(proj, "w_idx", [P, NT, HEADS])
            with ExitStack() as inner:
                h = K.sbuf(inner, "h", [P, KT, S])
                move(nc, K, [(h[:], x_t)])
                rms_norm(nc, K, inner, h, KT, h, lambda t: K.mod[:, 8 + t:9 + t], bias=lambda t: K.mod[:, t:t + 1])
                dense(nc, K, dram["w_u"], 4, 1, KT, lambda k, lo, n: h[:, k, lo:lo + n], S,
                      lambda eng, acc, t, j: eng.activation(zu[:, bass.ds(t, 1), :], acc, ACT.Gelu_apprx_tanh))
                dense(nc, K, dram["w_rot"], 10, 1, KT, lambda k, lo, n: h[:, k, lo:lo + n], S,
                      lambda eng, acc, t, j: eng.activation(rot[:, bass.ds(t, 1), :], acc, ACT.Copy))
                token_products(nc, K, h, zv, val, w_idx)
            spatial_gating(nc, K, zu, zv, merged[:, 0:4, :])
            with ExitStack() as inner:
                cos = K.sbuf(inner, "cos", [P, S])
                sin = K.sbuf(inner, "sin", [P, S])
                rope_tables(nc, K, cos, sin)
                rope(nc, K, rot, 10, cos, sin)
            attention(nc, K, rot, val, w_idx, merged[:, 4:8, :])
        rms_norm(nc, K, ctx, merged[:, 0:4, :], 4, merged[:, 0:4, :], lambda t: K.col("g_out_sgu", t))
        rms_norm(nc, K, ctx, merged[:, 4:8, :], 4, merged[:, 4:8, :], lambda t: K.col("g_out_attn", t))
        with ExitStack() as mid:
            x2 = K.sbuf(mid, "x2", [P, KT, S])
            o = K.sbuf(mid, "o", [P, KT, S])
            dense(nc, K, dram["w_out"], KT, 1, KT, lambda k, lo, n: merged[:, k, lo:lo + n], S,
                  lambda eng, acc, t, j: eng.activation(o[:, bass.ds(t, 1), :], acc, ACT.Copy))
            move(nc, K, [(x2[:], x_t)])
            rms_norm(nc, K, mid, o, KT, x2, lambda t: K.mod[:, 16 + t:17 + t], add=x2)
            rms_norm(nc, K, mid, x2, KT, merged, lambda t: K.mod[:, 32 + t:33 + t],
                     bias=lambda t: K.mod[:, 24 + t:25 + t])
            squared_relu_mlp(nc, K, merged, dram["w_ff1"], dram["w_ff2"], o)
            rms_norm(nc, K, mid, o, KT, x2, lambda t: K.mod[:, 40 + t:41 + t], add=x2)
            rms_norm(nc, K, mid, x2, KT, merged, lambda t: K.col("norm1_g", t))
            x3 = nc.dram_tensor("x3", (P, KT, S), F32).ap()
            move(nc, K, [(x3, x2[:])])
        parts_dram = nc.dram_tensor("rwkv_parts", (NT, P, N_PARTS, WT, P), F32).ap()
        decay_dram = nc.dram_tensor("rwkv_decay", (HD, HEADS, S // CH), F32).ap()
        h_dram = nc.dram_tensor("h_block2", (P, KT, S), F32).ap()
        move(nc, K, [(h_dram, merged[:])])
        with ExitStack() as rw:
            gate, bonus = merged[:, 0:WT, :], merged[:, WT:2 * WT, :]
            with ExitStack() as inner:
                zm = K.sbuf(inner, "z_mixed", [P, SHIFT_TILES, S])
                shift_mix(nc, K, merged, zm)
                rwkv_features(nc, K, zm, gate, bonus, parts_dram, decay_dram)
            y = K.sbuf(rw, "y", [P, WT, S])
            rwkv_chunks(nc, K, parts_dram, decay_dram, y)
            rwkv_finish(nc, K, y, bonus, gate)
            dense(nc, K, dram["w_rwkv_proj"], KT, 1, WT, lambda k, lo, n: y[:, k, lo:lo + n], S,
                  lambda eng, acc, t, j: eng.activation(merged[:, bass.ds(t, 1), :], acc, ACT.Copy))
        with ExitStack() as sm:
            ys = K.sbuf(sm, "ys", [P, WT, S])
            with ExitStack() as inner:
                u = K.sbuf(inner, "u", [P, WT, S])
                with ExitStack() as inmost:
                    h = K.sbuf(inmost, "h_again", [P, KT, S])
                    move(nc, K, [(h[:], h_dram)])
                    dense(nc, K, dram["w_u2"], WT, 1, KT, lambda k, lo, n: h[:, k, lo:lo + n], S,
                          lambda eng, acc, t, j: eng.activation(u[:, bass.ds(t, 1), :], acc, ACT.Copy))
                mag = K.sbuf(inner, "magnitude", [P, SSM_TILES])
                power = K.sbuf(inner, "phase_power", [P, 2, 10, SSM_TILES])
                b_t = K.sbuf(inner, "b_turned", [P, 2, SSM_TILES, P])
                c_re = K.sbuf(inner, "c_re_sbuf", [P, SSM_TILES, P])
                c_im = K.sbuf(inner, "c_im_sbuf", [P, SSM_TILES, P])
                table = K.sbuf(inner, "phase_table", [P, 2, SSM_TILES, P])
                s5 = (mag[:], power, b_t, c_re[:], c_im[:], table)
                ssm_prepare(nc, K, s5)
                ssm_scan(nc, K, s5, u, ys)
            yb = K.sbuf(sm, "yb", [P, KT, S])
            h = K.sbuf(sm, "h_gates", [P, KT, S])
            move(nc, K, [(h[:], h_dram)])
            combine(nc, K, h, merged, yb, ys)
        with ExitStack() as last:
            x4 = K.sbuf(last, "x4", [P, KT, S])
            o = K.sbuf(last, "o2", [P, KT, S])
            dense(nc, K, dram["w_out2"], KT, 1, KT, lambda k, lo, n: merged[:, k, lo:lo + n], S,
                  lambda eng, acc, t, j: eng.activation(o[:, bass.ds(t, 1), :], acc, ACT.Copy))
            move(nc, K, [(x4[:], x3)])
            add_tiles(nc, K, x4, o)
            rms_norm(nc, K, last, x4, KT, merged, lambda t: K.col("norm2_g", t))
            squared_relu_mlp(nc, K, merged, dram["w_ff_up"], dram["w_ff_down"], o)
            add_tiles(nc, K, x4, o)
            rms_norm(nc, K, last, x4, KT, merged, lambda t: K.col("norm_f_g", t))
            move(nc, K, [(dram["out"].rearrange("(t p) s -> p t s", p=P), merged[:])])


_OUT = ("out_dram", (D, S))


def slabs(w, kt):
    k, n = w.shape
    return np.ascontiguousarray(
        w.reshape(k // (kt * P), kt, P, n // P, P).transpose(3, 0, 2, 1, 4)).reshape(-1, P, kt * P)


def columns(v):
    return np.asarray(v, np.float32).reshape(-1, P).T


def paired(w):
    return w.reshape(w.shape[:-1] + (2, 4, HD)).swapaxes(-3, -2).reshape(w.shape)


def shape_constants():
    a = np.zeros((P, N_CONSTS), np.float32)
    i = np.arange(P)

    def put(name, m):
        at, n = CONST_AT[name]
        a[:, at:at + n] = m
    put("ident", np.eye(P))
    put("ones", np.ones((P, P)))
    put("head_ones", i[:, None] // HD == i[None, :] // HD)
    swap = np.zeros((P, P))
    for m in range(P):
        if m % HD < 8:
            swap[m + 8, m] = -1.0
        elif m % HD < 16:
            swap[m - 8, m] = 1.0
    put("rope_swap", swap)
    put("t_ge_s", i[None, :] >= i[:, None])
    return a


def lay_out(x):
    w_in, q0 = x["w_in"][0], 2 * D_SGU
    wq, wk = w_in[:, q0:q0 + 512], w_in[:, q0 + 512:q0 + 640]
    wval, wqi = w_in[:, q0 + 640:q0 + 768], w_in[:, q0 + 768:q0 + 1280]
    wki, wwi = w_in[:, q0 + 1280:q0 + 1344], w_in[:, q0 + 1344:q0 + 1352]
    w_rot = np.concatenate([paired(wq), wk, wqi, wki, wki], axis=1)
    inv = np.zeros(P, np.float32)
    freq = (500000.0 ** (-np.arange(0, 16, 2, dtype=np.float64) / 16)).astype(np.float32)
    for p in range(P):
        if p % HD < 16:
            inv[p] = freq[p % 8]
    vec = {
        "c": x["c"], "b_ada": x["b_ada"], "g_pre_mix": x["g_pre_mix"], "g_sgu_v": x["g_sgu_v"],
        "g_out_sgu": x["g_out_sgu"], "g_out_attn": paired(x["g_out_attn"]), "g_post_mix": x["g_post_mix"],
        "g_pre_ffn": x["g_pre_ffn"], "g_post_ffn": x["g_post_ffn"], "norm1_g": x["norm1_g_2"],
        "mu": x["mu_shift_2"], "k_k": x["k_k_2"], "k_a": x["k_a_2"], "r_k": x["r_k_2"], "w0": x["w0_2"],
        "a0": x["a0_2"], "lnx_w": x["lnx_w_2"], "lnx_b": x["lnx_b_2"], "d_skip": x["d_skip_2"],
        "b_glu": x["b_glu_2"], "norm2_g": x["norm2_g_2"], "norm_f_g": x["norm_f_g_2"],
        "a_re": x["a_re_2"], "a_im": x["a_im_2"], "log_dt": np.repeat(x["log_dt_2"], HD, axis=-1),
        "inv_freq": inv, "eps": np.full(P, EPS), "lnx_eps": np.full(P, LNX_EPS), "minus_pi": np.zeros(P),
    }
    cols = np.concatenate([columns(vec[name]) for name, _ in COLS], axis=1)

    def by_token(w):
        return np.ascontiguousarray(w.reshape(KT, P, -1).transpose(1, 0, 2))
    out = {
        "cols": cols, "consts": shape_constants(), "x": np.ascontiguousarray(x["x"][0].T),
        "positions": x["positions"], "w_ada": slabs(x["w_ada"][0], KT), "w_u": slabs(w_in[:, 0:512], KT),
        "w_rot": slabs(w_rot, KT), "w_v": by_token(w_in[:, 512:1024]),
        "w_val": by_token(np.concatenate([wval, wwi], axis=1)),
        "w_spatial": np.ascontiguousarray(x["w_spatial"][0].transpose(2, 0, 1)),
        "b_spatial": x["b_spatial"],
        "w_out": slabs(np.concatenate([x["w_out"][0][:512], paired(x["w_out"][0][512:].T).T]), KT),
        "w_ff1": slabs(x["w_ff1"][0], KT), "w_ff2": slabs(x["w_ff2"][0], KT),
    }
    out.update(lay_out_2(x))
    return {k: np.ascontiguousarray(v) for k, v in out.items()}


def rwkv_constants():
    a = np.zeros((P, N_R), np.float32)
    r, c = np.arange(P)[:, None], np.arange(P)[None, :]
    same = r // CH == c // CH

    def put(name, m, i=0):
        at = R_AT[name][0] + i * m.shape[1]
        a[:, at:at + m.shape[1]] = m
    put("transposed", np.concatenate([-1.0 * (same & (r < c)), same & (r <= c), same & (r < c),
                                      same & (r <= c)], axis=1))
    put("minus_lower", -1.0 * (same & (r > c)))
    for i in range(6):
        n = 1 << i
        block = (r // (2 * n) == c // (2 * n)) & (r // n == c // n + 1)
        put("lower", block, i)
        put("upper", block.T, i)
    put("no_reset", np.broadcast_to(np.arange(S)[None, :] % CH != 0, (P, S)))
    return a


def state_rows(b):
    out = np.zeros((SSM_TILES, 2, HD, 2, 16), b.dtype)
    for g in range(2):
        out[:, g, :, g, :] = b[g::2]
    return out.reshape(SSM_TILES, P, 32).transpose(1, 0, 2)


def channel_columns(c):
    rows = state_rows(c.transpose(0, 2, 1)).reshape(P, SSM_TILES, 32)
    out = np.zeros((P, SSM_TILES, 4, 32), c.dtype)
    for t in range(SSM_TILES):
        out[:, t, t % 4] = rows[:, t]
    return out.reshape(P, SSM_TILES, P)


def lay_out_2(x):
    w_in = x["w_in_2"][0]
    up = np.zeros((P, 2, W2), np.float32)
    up[:, 0] = np.concatenate([x["w_decay_up_2"][0], x["w_aaa_up_2"][0]])
    up[:, 1] = x["w_gate_up_2"][0]
    return {
        "w_shift": slabs(w_in[:, :SHIFT_TILES * P], KT), "r_consts": rwkv_constants(), "lora_up": up,
        "w_u2": slabs(w_in[:, SHIFT_TILES * P:SHIFT_TILES * P + W2], KT),
        "w_gates": slabs(w_in[:, SHIFT_TILES * P + W2:], KT),
        "b_re": state_rows(x["b_re_2"][0]), "b_im": state_rows(x["b_im_2"][0]),
        "c_re": channel_columns(x["c_re_2"][0]), "c_im": channel_columns(x["c_im_2"][0]),
        "w_glu": slabs(x["w_glu_2"][0], WT), "w_out2": slabs(x["w_out_2"][0], KT),
        "w_ff_up": slabs(x["w_ff_up_2"][0], KT), "w_ff_down": slabs(x["w_ff_down_2"][0], KT),
        "w_rwkv_proj": slabs(x["w_rwkv_proj_2"][0], WT),
    }


def kernel(**inputs):
    import concourse.bacc as bacc
    from concourse.bass_utils import run_bass_kernel_spmd

    arrays = {f"in_{k}": v for k, v in lay_out({k: np.asarray(v) for k, v in inputs.items()}).items()}
    nc = bacc.Bacc("TRN2", target_bir_lowering=False, num_devices=1)
    dram = {k[3:]: nc.dram_tensor(k, a.shape, mybir.dt.from_np(a.dtype), kind="ExternalInput").ap()
            for k, a in arrays.items()}
    name, shape = _OUT
    dram["out"] = nc.dram_tensor(name, shape, F32, kind="ExternalOutput").ap()
    build(nc, dram)
    r = run_bass_kernel_spmd(nc, [arrays], core_ids=[0])
    return np.ascontiguousarray(r.results[0][name].T).reshape(1, S, D)
```

```python
from contextlib import ExitStack

import numpy as np

import concourse.bass as bass
from concourse import mybir

P = 128
S = 1024
D = 1024
HALF = 512
KT = D // P
NT = S // P
D_SGU = 512
HEADS = 8
HD = 64
TOPK = 256
D_FF = 4096
FT = D_FF // P
W2 = 512
WT = W2 // P
CH = 64
SHIFT_TILES = 14
GATE_TILES = 16
SSM_TILES = 16
RING = 4
EPS = 1e-6
LNX_EPS = 64e-5
DECAY_SCALE = float(np.exp(-0.5))
GELU_TILES = 4

FAR = -2.0e38
TAKEN = -3.0e38
NEVER = -1.0e30

F32 = mybir.dt.float32
F32R = mybir.dt.float32r
U32 = mybir.dt.uint32
I32 = mybir.dt.int32
ACT = mybir.ActivationFunctionType
ALU = mybir.AluOpType
AX = mybir.AxisListType

COLS = [
    ("c", 8), ("b_ada", 48), ("g_pre_mix", 8), ("g_sgu_v", 4), ("g_out_sgu", 4), ("g_out_attn", 4),
    ("g_post_mix", 8), ("g_pre_ffn", 8), ("g_post_ffn", 8), ("norm1_g", 8), ("mu", 14), ("k_k", 4),
    ("k_a", 4), ("r_k", 4), ("w0", 4), ("a0", 4), ("lnx_w", 4), ("lnx_b", 4), ("d_skip", 4),
    ("b_glu", 16), ("norm2_g", 8), ("norm_f_g", 8), ("a_re", 16), ("a_im", 16), ("log_dt", 16),
    ("inv_freq", 1), ("eps", 1), ("lnx_eps", 1), ("minus_pi", 1),
]
COL_AT = {}
_n = 0
for _name, _k in COLS:
    COL_AT[_name] = (_n, _k)
    _n += _k
N_COLS = _n

CONSTS = [
    ("ident", 128), ("ones", 128), ("head_ones", 128), ("rope_swap", 128), ("t_ge_s", 128),
]
CONST_AT = {}
_n = 0
for _name, _k in CONSTS:
    CONST_AT[_name] = (_n, _k)
    _n += _k
N_CONSTS = _n


class Signal:

    def __init__(self, nc, ctx, name):
        self.sem = ctx.enter_context(nc.semaphore(name))
        self.n = 0


class Core:

    def __init__(self, nc, ctx, dram):
        self.nc, self.ctx, self.dram = nc, ctx, dram
        self.names = {}
        self.ring_order, self.ring_turn = [], 0
        self.psum = ctx.enter_context(nc.psum_tensor("psum", [P, 8, HALF], F32))
        self.ring = self.sbuf(ctx, "weight_ring", [P, RING, KT * P])
        self.cols = self.sbuf(ctx, "cols", [P, N_COLS])
        self.consts = self.sbuf(ctx, "consts", [P, N_CONSTS])
        self.mod = self.sbuf(ctx, "mod", [P, 48])
        self.setup = self.flag("setup_loaded")
        self.slab_loaded = [self.flag(f"slab_loaded_{i}") for i in range(RING)]
        self.slab_used = self.flag("slab_used")
        self.slab_high = self.flag("slab_high")
        self.slab_split = self.flag("slab_split")
        self.tile_high = self.flag("tile_high")
        self.tile_split = self.flag("tile_split")
        self.part_free = self.flag("part_free")
        self.acc_free = self.flag("acc_free")
        self.posted = self.flag("posted")
        self.sq_ready = self.flag("square_ready")
        self.odd_ready = self.flag("odd_square_ready")
        self.pair_summed = self.flag("square_pair_summed")
        self.sq_used = self.flag("square_used")
        self.root_ready = self.flag("root_ready")
        self.scale_ready = self.flag("scale_ready")
        self.scaled = self.flag("scaled")
        self.act_done = self.flag("act_done")
        self.dve_done = self.flag("dve_done")
        self.pool_done = self.flag("pool_done")
        self.pe_done = self.flag("pe_done")
        self.load_done = self.flag("load_done")
        self.store_done = self.flag("store_done")

    def sbuf(self, ctx, name, shape, dt=F32):
        n = self.names[name] = self.names.get(name, 0) + 1
        return ctx.enter_context(self.nc.sbuf_tensor(name if n == 1 else f"{name}_{n}", shape, dt))

    def turn_of_ring(self):
        turn, self.ring_turn = self.ring_turn, self.ring_turn + 1
        return 0 < turn < len(self.ring_order), (self.ring_order + [None])[min(turn + 1, len(self.ring_order))]

    def pair(self, ctx, name, shape):
        return [self.sbuf(ctx, name + part, shape, F32R)[:] for part in ("_high", "_low")]

    def flag(self, name):
        return Signal(self.nc, self.ctx, name)

    def col(self, name, t=0, n=1):
        at = COL_AT[name][0] + t
        return self.cols[:, at:at + n]

    def const(self, name):
        at, n = CONST_AT[name]
        return self.consts[:, at:at + n]


class Chain:

    def __init__(self, eng, of):
        self.eng, self.of, self.n = eng, of, of.n

    def step(self, ins):
        ins.then_inc(self.of.sem, 1)
        self.n += 1
        return self.n

    def wait(self, n=None):
        self.eng.wait_ge(self.of.sem, self.n if n is None else n)

    def __call__(self, ins):
        self.step(ins)
        self.wait()


def load_setup(nc, K):
    with nc.Block() as block:
        @block.sync
        def _(sp):
            sp.dma_start(K.cols[:], K.dram["cols"]).then_inc(K.setup.sem, 16)
            sp.dma_start(K.consts[:], K.dram["consts"]).then_inc(K.setup.sem, 16)
            sp.wait_ge(K.setup.sem, 32)

        @block.tensor
        def _(pe):
            pe.sem_inc(K.slab_used.sem, RING)

        @block.scalar
        def _(act):
            act.sem_inc(K.acc_free.sem, 2)
            act.sem_inc(K.posted.sem, 2)
    K.setup.n = 32


def split(dve, chain, x, high, low):
    sem, value = chain
    dve.tensor_copy(high, x).then_inc(sem, 1)
    dve.wait_ge(sem, value)
    return dve.tensor_tensor(out=low, in0=x, in1=high.bitcast(F32), op=ALU.subtract)


def first_slabs(sp, K, weights, cols):
    for slot in range(RING):
        sp.dma_start(K.ring[:, slot, 0:cols], weights[slot]).then_inc(K.slab_loaded[slot].sem, 16)


def prefetch(sp, K, after, used0, total):
    if after is None:
        return
    weights, cols = after
    for last in range(total - RING, total):
        slot = last % RING
        sp.wait_ge(K.slab_used.sem, used0 + RING + last + 1)
        sp.dma_start(K.ring[:, slot, 0:cols], weights[slot]).then_inc(K.slab_loaded[slot].sem, 16)


def dense(nc, K, weights, n_tiles, kg, kt, rhs, width, step, on="scalar", post=None, parts=None, to_split=None,
          side=None):
    un = 4 if kg == 1 else 2
    loops, rest = n_tiles // un, n_tiles % un
    per = un * kg
    spans = [(lo, min(HALF, width - lo)) for lo in range(0, width, HALF)]
    used0, accfree0, post0 = K.slab_used.n, K.acc_free.n, K.posted.n
    high0, split0, tile0 = K.slab_high.n, K.slab_split.n, K.tile_split.n
    loaded0 = [s.n for s in K.slab_loaded]
    uses = per // RING
    total = n_tiles * kg
    psum = K.psum
    ahead, after = K.turn_of_ring()

    def acc(j):
        b = 2 * (j % 2)
        return psum[:, b:b + len(spans), 0:spans[0][1]]

    def over_tiles(eng, tile, peel=0):
        if loops - peel > 0:
            with eng.Fori(0, loops - peel) as i:
                for j in range(un):
                    tile(i, j)
        for t in range(max(0, loops - peel) * un, n_tiles):
            tile(t // un, t % un)

    with ExitStack() as ctx:
        if parts:
            w_high = K.sbuf(ctx, "weight_high", [P, 2, kt * P], F32R)
            w_low = K.sbuf(ctx, "weight_low", [P, 2, kt * P], F32R)
        block = ctx.enter_context(nc.Block())

        @block.sync
        def _(sp):
            def load(i, j):
                for s in range(j * kg, (j + 1) * kg):
                    if isinstance(i, int) and i * per + s + RING >= total:
                        continue
                    sp.wait_ge(K.slab_used.sem, i * per + (used0 + RING + s + 1))
                    sp.dma_start(K.ring[:, s % RING, 0:kt * P], weights[i * per + (s + RING)]) \
                        .then_inc(K.slab_loaded[s % RING].sem, 16)
            if not ahead:
                first_slabs(sp, K, weights, kt * P)
            for to, of in side or []:
                sp.dma_start(to, of).then_inc(K.load_done.sem, 16)
            over_tiles(sp, load, peel=1)
            prefetch(sp, K, after, used0, total)
            if side:
                sp.wait_ge(K.load_done.sem, K.load_done.n + 16 * len(side))

        @block.tensor
        def _(pe):
            def tile(i, j):
                pe.wait_ge(K.acc_free.sem, i * un + (accfree0 + j + 1))
                for g in range(kg):
                    s = j * kg + g
                    slot = s % RING
                    if parts:
                        pe.wait_ge(K.slab_split.sem, i * per + (split0 + s + 1))
                    else:
                        pe.wait_ge(K.slab_loaded[slot].sem,
                                   i * (16 * uses) + (loaded0[slot] + 16 * (s // RING + 1)))
                    for k in range(kt):
                        if to_split is not None and s == 0:
                            pe.wait_ge(K.tile_split.sem, tile0 + k + 1)
                        at = slice(k * P, (k + 1) * P)
                        passes = [(K.ring[:, slot, at], rhs)]
                        if parts:
                            high, low = tiles_of(parts[0]), tiles_of(parts[1])
                            passes = [(w_high[:, s % 2, at], high), (w_high[:, s % 2, at], low),
                                      (w_low[:, s % 2, at], high)]
                        for m, (w, x) in enumerate(passes):
                            for h, (lo, n) in enumerate(spans):
                                mm = pe.matmul(psum[:, 2 * (j % 2) + h, 0:n], w, x(g * kt + k, lo, n),
                                               start=(g == 0 and k == 0 and m == 0),
                                               stop=(g == kg - 1 and k == kt - 1 and m == len(passes) - 1))
                    mm.then_inc(K.slab_used.sem, 1)
            over_tiles(pe, tile)

        def drain(eng):
            def tile(i, j):
                if post:
                    eng.wait_ge(K.posted.sem, i * un + (post0 + j + 1))
                eng.wait_ge(K.slab_used.sem, i * per + (used0 + RING + (j + 1) * kg))
                eng.wait_ge(K.setup.sem, 32)
                step(eng, acc(j), i * un + j, j % 2).then_inc(K.acc_free.sem, 1)
            over_tiles(eng, tile)

        if on == "scalar":
            @block.scalar
            def _(act):
                drain(act)
        if on == "vector":
            @block.vector
            def _(dve):
                drain(dve)
        if post or parts:
            @block.vector
            def _(dve):
                def split_slab(i, s):
                    slot = s % RING
                    dve.wait_ge(K.slab_used.sem, i * per + (used0 + RING + s - 1))
                    dve.wait_ge(K.slab_loaded[slot].sem, i * (16 * uses) + (loaded0[slot] + 16 * (s // RING + 1)))
                    split(dve, (K.slab_high.sem, i * per + (high0 + s + 1)), K.ring[:, slot, 0:kt * P],
                          w_high[:, s % 2, :], w_low[:, s % 2, :]).then_inc(K.slab_split.sem, 1)

                def finish(i, j):
                    if parts:
                        for s in range(j * kg + 1, (j + 1) * kg + 1):
                            if not isinstance(i, int) or i * per + s < total:
                                split_slab(i, s)
                    if post:
                        dve.wait_ge(K.acc_free.sem, i * un + (accfree0 + 2 + j + 1))
                        dve.wait_ge(K.setup.sem, 32)
                        post(dve, i * un + j, j % 2).then_inc(K.posted.sem, 1)
                if parts:
                    split_slab(0, 0)
                if to_split is not None:
                    for k in range(kt):
                        split(dve, (K.tile_high.sem, K.tile_high.n + k + 1), to_split[:, k, :], parts[0][:, k, :],
                              parts[1][:, k, :]).then_inc(K.tile_split.sem, 1)
                over_tiles(dve, finish, peel=1 if parts else 0)

    K.load_done.n += 16 * len(side or [])
    K.slab_used.n += total
    K.acc_free.n += n_tiles
    K.posted.n += n_tiles if post else 0
    K.slab_high.n += total if parts else 0
    K.slab_split.n += total if parts else 0
    K.tile_high.n += kt if to_split is not None else 0
    K.tile_split.n += kt if to_split is not None else 0
    for slot in range(RING):
        K.slab_loaded[slot].n += 16 * sum(1 for s in range(total) if s % RING == slot)


def tiles_of(x):
    return lambda k, lo, n: x[:, k, lo:lo + n]


def ada(nc, K, side):
    CHUNKS = 6
    with ExitStack() as ctx:
        act_c = K.sbuf(ctx, "silu_c", [P, KT])
        part = K.sbuf(ctx, "mod_parts", [P, 2, D])
        act0, dve0, pe0, used0 = K.act_done.n, K.dve_done.n, K.pe_done.n, K.slab_used.n
        loaded0 = [f.n for f in K.slab_loaded]
        per = 2 * KT
        loops = CHUNKS // 2
        _, after = K.turn_of_ring()
        with nc.Block() as block:
            @block.sync
            def _(sp):
                with sp.Fori(0, loops) as i:
                    for s in range(per):
                        sp.wait_ge(K.slab_used.sem, i * per + (used0 + s + 1))
                        sp.dma_start(K.ring[:, s % RING, :], K.dram["w_ada"][i * per + s]) \
                            .then_inc(K.slab_loaded[s % RING].sem, 16)
                prefetch(sp, K, after, used0, CHUNKS * KT)
                sp.dma_start(side[0], side[1]).then_inc(K.load_done.sem, 16)
                sp.wait_ge(K.load_done.sem, K.load_done.n + 16)

            @block.vector
            def _(dve):
                dve.wait_ge(K.act_done.sem, act0 + 1)
                with dve.Fori(0, loops) as i:
                    for s in range(per):
                        c, k = s // KT, s % KT
                        if k == 0:
                            dve.wait_ge(K.part_free.sem, i * 2 + (c + 1))
                        else:
                            dve.wait_ge(K.slab_used.sem, i * per + (used0 + RING + s))
                        dve.wait_ge(K.slab_loaded[s % RING].sem,
                                    i * (16 * per // RING) + (loaded0[s % RING] + 16 * (s // RING + 1)))
                        w, to = K.ring[:, s % RING, :], part[:, c, :]
                        if k == 0:
                            ins = dve.tensor_scalar(to, w, act_c[:, 0:1], None, op0=ALU.mult)
                        else:
                            ins = dve.scalar_tensor_tensor(out=to, in0=w, scalar=act_c[:, k:k + 1], in1=to,
                                                           op0=ALU.mult, op1=ALU.add)
                        ins.then_inc(K.slab_used.sem, 1)

            @block.tensor
            def _(pe):
                pe.sem_inc(K.part_free.sem, 2)
                with pe.Fori(0, loops) as i:
                    for c in range(2):
                        pe.wait_ge(K.slab_used.sem, i * per + (used0 + RING + (c + 1) * KT))
                        pe.wait_ge(K.acc_free.sem, i * 2 + (K.acc_free.n + c + 1))
                        for t in range(KT):
                            mm = pe.matmul(K.psum[:, c, t:t + 1], part[:, c, t * P:(t + 1) * P],
                                           K.const("ones")[:, 0:1], start=True, stop=True)
                        mm.then_inc(K.part_free.sem, 1)

            @block.scalar
            def _(act):
                act.activation(act_c[:], K.col("c", 0, KT), ACT.Silu).then_inc(K.act_done.sem, 1)
                with act.Fori(0, loops) as i:
                    for c in range(2):
                        act.wait_ge(K.part_free.sem, i * 2 + (c + 3))
                        act.wait_ge(K.setup.sem, 32)
                        act.activation(K.mod[:, bass.ds(i * (2 * KT) + c * KT, KT)], K.psum[:, c, 0:KT], ACT.Copy) \
                            .then_inc(K.acc_free.sem, 1)
        K.act_done.n += 1
        K.load_done.n += 16
        K.slab_used.n += CHUNKS * KT
        K.acc_free.n += CHUNKS
        for f in K.slab_loaded:
            f.n += 16 * CHUNKS * KT // RING
        with nc.Block() as block:
            @block.vector
            def _(dve):
                c = Chain(dve, K.dve_done)
                c(dve.tensor_tensor(out=K.mod[:], in0=K.mod[:], in1=K.col("b_ada", 0, 48), op=ALU.add))
                for at, gain in ((8, "g_pre_mix"), (32, "g_pre_ffn")):
                    dve.scalar_tensor_tensor(out=K.mod[:, at:at + 8], in0=K.mod[:, at:at + 8], scalar=1.0,
                                             in1=K.col(gain, 0, 8), op0=ALU.add, op1=ALU.mult)
                for at, gain in ((16, "g_post_mix"), (40, "g_post_ffn")):
                    ins = dve.tensor_tensor(out=K.mod[:, at:at + 8], in0=K.mod[:, at:at + 8],
                                            in1=K.col(gain, 0, 8), op=ALU.mult)
                c(ins)
                K.dve_done.n = c.n


def rms_norm(nc, K, ctx, src, tiles, out, gain, bias=None, add=None, size=None, eps="eps",
             side=None, store=None):
    size = size or tiles * P
    with ExitStack() as ctx:
        sq = K.sbuf(ctx, "squares", [P, 2, S])
        odd = K.sbuf(ctx, "odd_squares", [P, S])
        root = K.sbuf(ctx, "root", [P, S])
        pairs = tiles // 2
        odd0, pair0 = K.odd_ready.n, K.pair_summed.n
        sq0, used0, root0, scale0, scaled0 = (K.sq_ready.n, K.sq_used.n, K.root_ready.n,
                                              K.scale_ready.n, K.scaled.n)
        with nc.Block() as block:
            if side or store is not None:
                @block.sync
                def _(sp):
                    if side:
                        sp.dma_start(side[0], side[1]).then_inc(K.load_done.sem, 16)
                        K.load_done.n += 16
                        sp.wait_ge(K.load_done.sem, K.load_done.n)
                    if store is not None:
                        for t in range(tiles):
                            sp.wait_ge(K.scaled.sem, scaled0 + t + 1)
                            sp.dma_start(store[:, t, :], out[:, t, :]).then_inc(K.store_done.sem, 16)
                        K.store_done.n += 16 * tiles
                        sp.wait_ge(K.store_done.sem, K.store_done.n)

            @block.scalar
            def _(act):
                for p in range(pairs):
                    if p >= 2:
                        act.wait_ge(K.sq_used.sem, used0 + p - 1)
                    act.activation(sq[:, p % 2, :], src[:, 2 * p, :], ACT.Square).then_inc(K.sq_ready.sem, 1)
                act.wait_ge(K.sq_used.sem, used0 + pairs)
                act.activation(root[:], K.psum[:, 4:6, :], ACT.Sqrt, scale=1.0 / size, bias=K.col(eps)) \
                    .then_inc(K.root_ready.sem, 1)
                if bias is not None:
                    for t in range(tiles):
                        act.wait_ge(K.scaled.sem, scaled0 + t + 1)
                        ins = act.activation(out[:, t, :], out[:, t, :], ACT.Identity, bias=bias(t))
                        ins.then_inc(K.act_done.sem, 1)

            @block.tensor
            def _(pe):
                for p in range(pairs):
                    pe.wait_ge(K.pair_summed.sem, pair0 + p + 1)
                    for h in range(2):
                        mm = pe.matmul(K.psum[:, 4 + h, :], K.const("ones"),
                                       sq[:, p % 2, h * HALF:(h + 1) * HALF],
                                       start=(p == 0), stop=(p == pairs - 1))
                    mm.then_inc(K.sq_used.sem, 1)

            @block.vector
            def _(dve):
                for p in range(pairs):
                    if p:
                        dve.wait_ge(K.pair_summed.sem, pair0 + p)
                    x = src[:, 2 * p + 1, :]
                    dve.tensor_tensor(out=odd[:], in0=x, in1=x, op=ALU.mult).then_inc(K.odd_ready.sem, 1)
                    dve.wait_ge(K.odd_ready.sem, odd0 + p + 1)
                    dve.wait_ge(K.sq_ready.sem, sq0 + p + 1)
                    dve.tensor_tensor(out=sq[:, p % 2, :], in0=sq[:, p % 2, :], in1=odd[:], op=ALU.add) \
                        .then_inc(K.pair_summed.sem, 1)
                dve.wait_ge(K.root_ready.sem, root0 + 1)
                dve.reciprocal(root[:], root[:]).then_inc(K.scale_ready.sem, 1)
                dve.wait_ge(K.scale_ready.sem, scale0 + 1)
                for t in range(tiles):
                    to = src if add is not None else out
                    dve.scalar_tensor_tensor(out=to[:, t, :], in0=src[:, t, :], scalar=gain(t), in1=root[:],
                                             op0=ALU.mult, op1=ALU.mult).then_inc(K.scaled.sem, 1)
                    if add is not None and t % 2 == 0:
                        dve.wait_ge(K.scaled.sem, scaled0 + t + 1)
                        dve.tensor_tensor(out=out[:, t, :], in0=src[:, t, :], in1=add[:, t, :], op=ALU.add)

            if add is not None:
                @block.gpsimd
                def _(pool):
                    for t in range(1, tiles, 2):
                        pool.wait_ge(K.scaled.sem, scaled0 + t + 1)
                        pool.tensor_tensor(out=out[:, t, :], in0=src[:, t, :], in1=add[:, t, :], op=ALU.add)
    K.sq_ready.n += pairs
    K.odd_ready.n += pairs
    K.pair_summed.n += pairs
    K.sq_used.n += pairs
    K.root_ready.n += 1
    K.scale_ready.n += 1
    K.scaled.n += tiles
    K.act_done.n += tiles if bias is not None else 0


def move(nc, K, pairs):
    with nc.Block() as block:
        @block.sync
        def _(sp):
            for to, of in pairs:
                sp.dma_start(to, of).then_inc(K.load_done.sem, 16)
                K.load_done.n += 16
            sp.wait_ge(K.load_done.sem, K.load_done.n)


def token_values(nc, K, h, wa, val, w_idx):
    ready0, free0 = K.pe_done.n, K.dve_done.n
    with nc.Block() as block:
        @block.tensor
        def _(pe):
            for n in range(NT):
                if n >= 2:
                    pe.wait_ge(K.dve_done.sem, free0 + n - 1)
                for k in range(KT):
                    mm = pe.matmul(K.psum[:, n % 2, 0:136], h[:, k, n * P:(n + 1) * P], wa[:, k, :],
                                   start=(k == 0), stop=(k == KT - 1))
                mm.then_inc(K.pe_done.sem, 1)

        @block.vector
        def _(dve):
            for n in range(NT):
                dve.wait_ge(K.pe_done.sem, ready0 + n + 1)
                dve.tensor_copy(val[:, n, :], K.psum[:, n % 2, 0:P])
                dve.tensor_scalar(w_idx[:, n, :], K.psum[:, n % 2, P:P + HEADS], HEADS ** -0.5, None,
                                  op0=ALU.mult).then_inc(K.dve_done.sem, 1)
    K.pe_done.n += NT
    K.dve_done.n += NT


def token_gelu(nc, K, parts, zv, cos, sin):
    high, low = parts
    PER = 2
    slabs = KT // PER
    assert slabs == RING
    ahead, after = K.turn_of_ring()
    with ExitStack() as ctx:
        w_high = K.sbuf(ctx, "weight_high", [P, 2, KT * P], F32R)
        w_low = K.sbuf(ctx, "weight_low", [P, 2, KT * P], F32R)
        pos_i = K.sbuf(ctx, "positions_int", [P, S], I32)
        angle = K.sbuf(ctx, "angle", [P, S])
        turns = K.sbuf(ctx, "turns", [P, S])
        used0, high0, split0 = K.slab_used.n, K.slab_high.n, K.slab_split.n
        load0 = K.load_done.n
        at = {}
        with nc.Block() as block:
            @block.sync
            def _(sp):
                sp.dma_start(pos_i[:], K.dram["positions"].broadcast_to([P, S])).then_inc(K.load_done.sem, 16)
                if not ahead:
                    first_slabs(sp, K, K.dram["w_v"], KT * P)
                prefetch(sp, K, after, used0, slabs)

            @block.vector
            def _(dve):
                c = Chain(dve, K.dve_done)
                for s in range(slabs):
                    if s == 2:
                        dve.wait_ge(K.load_done.sem, load0 + 16)
                        c(dve.tensor_copy(angle[:], pos_i[:]))
                        c(dve.tensor_scalar(angle[:], angle[:], K.col("inv_freq"), None, op0=ALU.mult))
                        reduce_angle(dve, c, sin[:], turns[:], angle[:], 0.0)
                        at["sin"] = c.n
                    if s == 3:
                        reduce_angle(dve, c, cos[:], turns[:], angle[:], 0.25)
                        at["cos"] = c.n
                    if s >= 2:
                        dve.wait_ge(K.slab_used.sem, used0 + RING + s - 1)
                    dve.wait_ge(K.slab_loaded[s].sem, K.slab_loaded[s].n + 16)
                    split(dve, (K.slab_high.sem, high0 + s + 1), K.ring[:, s, :], w_high[:, s % 2, :],
                          w_low[:, s % 2, :]).then_inc(K.slab_split.sem, 1)
                K.dve_done.n = c.n

            @block.tensor
            def _(pe):
                for s in range(slabs):
                    pe.wait_ge(K.slab_split.sem, split0 + s + 1)
                    for kk in range(PER):
                        k, cols = s * PER + kk, slice(kk * D_SGU, (kk + 1) * D_SGU)
                        for n in range(NT):
                            at = slice(n * P, (n + 1) * P)
                            for m, (x, w) in enumerate(((high, w_high), (high, w_low), (low, w_high))):
                                mm = pe.matmul(K.psum[:, n, :], x[:, k, at], w[:, s % 2, cols],
                                               start=(k == 0 and m == 0), stop=(k == KT - 1 and m == 2))
                    mm.then_inc(K.slab_used.sem, 1)

            @block.scalar
            def _(act):
                for table, name in ((sin, "sin"), (cos, "cos")):
                    act.wait_ge(K.dve_done.sem, at[name])
                    act.activation(table[:], table[:], ACT.Sin).then_inc(K.act_done.sem, 1)
                act.wait_ge(K.slab_used.sem, used0 + RING + slabs)
                for n in range(NT):
                    act.activation(zv[:, n, :], K.psum[:, n, :], ACT.Gelu_apprx_tanh)
        K.load_done.n += 16
        K.act_done.n += 2
        K.slab_used.n += slabs
        K.slab_high.n += slabs
        K.slab_split.n += slabs
        for f in K.slab_loaded:
            f.n += 16


TWO_PI_1 = 6.28125
TWO_PI_2 = float(np.float32(np.frombuffer(np.array(
    [np.frombuffer(np.float32(2 * np.pi - 6.28125).tobytes(), np.uint32)[0] & 0xFFFFF000],
    np.uint32).tobytes(), np.float32)[0]))
TWO_PI_3 = float(2 * np.pi - 6.28125 - TWO_PI_2)
MAGIC = 12582912.0
PI_IN = 3.1415925


def reduce_angle(dve, c, out, turns, angle, shift):
    c(dve.tensor_scalar(turns, angle, float(1 / (2 * np.pi)), shift, op0=ALU.mult, op1=ALU.add))
    c(dve.tensor_scalar(turns, turns, MAGIC, None, op0=ALU.add))
    c(dve.tensor_scalar(turns, turns, -MAGIC, None, op0=ALU.add))
    c(dve.scalar_tensor_tensor(out=out, in0=turns, scalar=-TWO_PI_1, in1=angle, op0=ALU.mult, op1=ALU.add))
    c(dve.scalar_tensor_tensor(out=out, in0=turns, scalar=-TWO_PI_2, in1=out, op0=ALU.mult, op1=ALU.add))
    c(dve.scalar_tensor_tensor(out=out, in0=turns, scalar=-TWO_PI_3, in1=out, op0=ALU.mult, op1=ALU.add))
    if shift:
        c(dve.tensor_scalar(out, out, float(shift * 2 * np.pi), None, op0=ALU.add))
    c(dve.tensor_scalar(out, out, PI_IN, -PI_IN, op0=ALU.min, op1=ALU.max))


def rope(nc, K, x, tiles, cos, sin):
    with ExitStack() as ctx:
        turned = K.sbuf(ctx, "turned", [P, 2, S])
        pe0, dve0, free0 = K.pe_done.n, K.dve_done.n, K.scaled.n
        with nc.Block() as block:
            @block.tensor
            def _(pe):
                with pe.Fori(0, tiles // 2) as i:
                    for j in range(2):
                        pe.wait_ge(K.acc_free.sem, i * 2 + (K.acc_free.n + j + 1))
                        for h in range(2):
                            mm = pe.matmul(K.psum[:, 2 * j + h, :], K.const("rope_swap"),
                                           x[:, bass.ds(i * 2 + j, 1), h * HALF:(h + 1) * HALF],
                                           start=True, stop=True)
                        mm.then_inc(K.pe_done.sem, 1)

            @block.vector
            def _(dve):
                with dve.Fori(0, tiles // 2) as i:
                    for j in range(2):
                        tile = x[:, bass.ds(i * 2 + j, 1), :]
                        dve.wait_ge(K.pe_done.sem, i * 2 + (pe0 + j + 1))
                        dve.wait_ge(K.setup.sem, 32)
                        dve.tensor_tensor(out=turned[:, j:j + 1, :], in0=K.psum[:, 2 * j:2 * j + 2, :],
                                          in1=sin[:], op=ALU.mult).then_inc(K.acc_free.sem, 1)
                        dve.tensor_tensor(out=tile, in0=tile, in1=cos[:], op=ALU.mult) \
                            .then_inc(K.dve_done.sem, 1)
                        dve.wait_ge(K.dve_done.sem, i * 4 + (dve0 + 2 * j + 1))
                        dve.wait_ge(K.acc_free.sem, i * 2 + (K.acc_free.n + 2 + j + 1))
                        dve.wait_ge(K.setup.sem, 32)
                        dve.tensor_tensor(out=tile, in0=tile, in1=turned[:, j:j + 1, :], op=ALU.add) \
                            .then_inc(K.dve_done.sem, 1)
    K.pe_done.n += tiles
    K.dve_done.n += 2 * tiles
    K.acc_free.n += tiles


def spatial_gating(nc, K, zu, zv, out):
    load0, act0, dve0, pe0 = K.load_done.n, K.act_done.n, K.dve_done.n, K.pe_done.n
    with ExitStack() as ctx:
        w = K.sbuf(ctx, "w_spatial", [P, 4, P])
        b = K.sbuf(ctx, "b_spatial", [P, 4, P])
        junk = K.sbuf(ctx, "square_out", [P, D_SGU])
        ms = K.sbuf(ctx, "mean_squares", [P, NT, 4])
        mixed = K.sbuf(ctx, "mixed", [P, 2, HALF])
        with nc.Block() as block:
            @block.sync
            def _(sp):
                sp.dma_start(w[:], K.dram["w_spatial"]).then_inc(K.load_done.sem, 16)
                sp.dma_start(b[:], K.dram["b_spatial"].broadcast_to([P, 4, P])).then_inc(K.load_done.sem, 16)

            @block.vector
            def _(dve):
                c = Chain(dve, K.dve_done)
                dve.wait_ge(K.load_done.sem, load0 + 32)
                for g in range(4):
                    dve.tensor_tensor(out=w[:, g, :], in0=w[:, g, :], in1=K.const("t_ge_s"), op=ALU.mult)
                for n in range(NT):
                    for g in range(4):
                        z = zv[:, n, g * P:(g + 1) * P]
                        if n:
                            c.wait(c.n - 3)
                        ins = dve.tensor_tensor_reduce(
                            out=junk[:, g * P:(g + 1) * P], in0=z, in1=z, scale=1.0, scalar=0.0,
                            op0=ALU.mult, op1=ALU.add, accum_out=ms[:, n, g:g + 1])
                        c.step(ins)
                c.wait()
                dve.wait_ge(K.act_done.sem, act0 + 1)
                c(dve.reciprocal(ms[:], ms[:]))
                for n in range(NT):
                    for g in range(4):
                        z = zv[:, n, g * P:(g + 1) * P]
                        ins = dve.tensor_scalar(z, z, ms[:, n, g:g + 1], None, op0=ALU.mult)
                    c.step(ins)
                normed = c.n
                for m in range(8):
                    g, h = m // 2, m % 2
                    bank = K.psum[:, m % 4, :]
                    dve.wait_ge(K.pe_done.sem, pe0 + m + 1)
                    bias = b[:, g:g + 1, :].broadcast_to([P, 4, P])
                    s = c.step(dve.scalar_tensor_tensor(
                        out=mixed[:, m % 2, :].rearrange("p (n t) -> p n t", n=4),
                        in0=bank.rearrange("p (n t) -> p n t", n=4), scalar=K.col("g_sgu_v", g), in1=bias,
                        op0=ALU.mult, op1=ALU.add))
                    c.wait(s)
                    ins = dve.tensor_tensor(out=out[:, g, h * HALF:(h + 1) * HALF], in0=mixed[:, m % 2, :],
                                            in1=zu[:, g, h * HALF:(h + 1) * HALF], op=ALU.mult)
                    c.step(ins)
                K.normed_at = normed
                K.dve_done.n = c.n

            @block.scalar
            def _(act):
                act.wait_ge(K.dve_done.sem, dve0 + 4 * NT)
                act.activation(ms[:], ms[:], ACT.Sqrt, scale=1.0 / P, bias=K.col("eps")) \
                    .then_inc(K.act_done.sem, 1)

            @block.tensor
            def _(pe):
                pe.wait_ge(K.dve_done.sem, K.normed_at)
                for m in range(8):
                    g, h = m // 2, m % 2
                    if m >= 4:
                        pe.wait_ge(K.dve_done.sem, K.normed_at + 2 * (m - 4) + 1)
                    for q in range(4):
                        n = h * 4 + q
                        mm = pe.matmul(K.psum[:, m % 4, q * P:(q + 1) * P], zv[:, n, g * P:(g + 1) * P],
                                       w[:, g, :], start=True, stop=True)
                    mm.then_inc(K.pe_done.sem, 1)
    K.load_done.n += 32
    K.act_done.n += 1
    K.pe_done.n += 8


def attention(nc, K, rot, val, w_idx, out):
    Q, KK, QI, KI = 0, 4, 5, 9
    blocks = [1, 0] + list(range(NT - 1, 1, -1))
    steps = NT + 2
    halves = [1 if b < 4 else 2 for b in blocks]
    rounds = TOPK // 8

    def turns(a, h):
        return HEADS * sum(halves[:a]) + (h + 1) * halves[a]

    with ExitStack() as ctx:
        names = ("scores_ready", "relu_done", "w_diag_ready", "score_step", "score_copied", "causal_done",
                 "never_ready", "logits_ready", "logits_masked", "exp_done", "sum_inverted",
                 "p_diag_ready", "p_turned", "p_copied", "pv_ready", "y_copied")
        (scores_ready, relu_done, w_diag_ready, score_step, score_copied, causal_done, never_ready,
         logits_ready, logits_masked, exp_done, sum_inverted, p_diag_ready, p_turned, p_copied, pv_ready,
         y_copied) = (K.flag(name).sem for name in names)
        relu = K.sbuf(ctx, "relu_scores", [P, 2, S])
        score = K.sbuf(ctx, "score", [P, 2, S])
        never = K.sbuf(ctx, "never", [P, S])
        logit = K.sbuf(ctx, "logits", [P, 2, S])
        turned = K.sbuf(ctx, "p_turned_sbuf", [P, 2, NT, 4, P])
        w_diag = K.sbuf(ctx, "w_diag", [P, 2, P])
        p_diag = K.sbuf(ctx, "one_over_sum_diag", [P, 2, P])
        top = K.sbuf(ctx, "top8", [P, 8])
        low = K.sbuf(ctx, "minus_max", [P, HEADS])
        total = K.sbuf(ctx, "exp_sum", [P, HEADS])
        psum = K.psum
        LOGITS, SCORES, SUM, TURNED, VALUES = 0, 2, 4, 6, 7

        def keys(bank, n):
            if n <= HALF:
                return psum[:, bank, 0:n]
            return psum[:, bank:bank + 2, :].rearrange("p b f -> p (b f)")[:, 0:n]

        with nc.Block() as block:
            @block.tensor
            def _(pe):
                def product(bank, lhs, rhs, n, start=True, stop=True):
                    for lo in range(0, n, HALF):
                        w = min(HALF, n - lo)
                        mm = pe.matmul(psum[:, bank + lo // HALF, 0:w], lhs, rhs[:, lo:lo + w],
                                       start=start, stop=stop)
                    return mm

                def score_head(a, h):
                    if a or h:
                        pe.wait_ge(relu_done, HEADS * a + h)
                    b = blocks[a]
                    at = slice((h % 2) * HD, (h % 2 + 1) * HD)
                    product(SCORES, rot[at, QI + h // 2, b * P:(b + 1) * P], rot[at, KI, :], (b + 1) * P) \
                        .then_inc(scores_ready, 1)

                def sum_head(a, h):
                    pe.wait_ge(relu_done, HEADS * a + h + 1)
                    pe.wait_ge(w_diag_ready, HEADS * a + h + 1)
                    if a and h == 0:
                        pe.wait_ge(score_copied, a)
                    product(SUM, w_diag[:, h % 2, :], relu[:, h % 2, :], (blocks[a] + 1) * P,
                            start=(h == 0), stop=(h == HEADS - 1)).then_inc(score_step, 1)

                def logits_head(a, h):
                    if a or h:
                        pe.wait_ge(logits_masked, HEADS * a + h)
                    b, g, j = blocks[a], h // 4, h % 4
                    at = slice(g * HD, (g + 1) * HD)
                    product(LOGITS, rot[at, Q + j, b * P:(b + 1) * P], rot[at, KK, :], (b + 1) * P) \
                        .then_inc(logits_ready, 1)

                def turn(a, h, half):
                    if half >= halves[a]:
                        return
                    pe.wait_ge(p_diag_ready, HEADS * a + h + 1)
                    before = turns(a, h) - halves[a] + half
                    if before:
                        pe.wait_ge(p_copied, before)
                    for c in range(4 * half, min(blocks[a] + 1, 4 * half + 4)):
                        mm = pe.matmul(psum[:, TURNED, (c % 4) * P:(c % 4 + 1) * P],
                                       logit[:, h % 2, c * P:(c + 1) * P], p_diag[:, h % 2, :],
                                       start=True, stop=True)
                    mm.then_inc(p_turned, 1)

                def values(a, g):
                    pe.wait_ge(p_copied, turns(a, 4 * g + 3))
                    if a or g:
                        pe.wait_ge(y_copied, 2 * a + g)
                    b = blocks[a]
                    for c in range(b + 1):
                        mm = pe.matmul(psum[:, VALUES, :], val[:, c, :], turned[:, g, c, :, :],
                                       start=(c == 0), stop=(c == b))
                    mm.then_inc(pv_ready, 1)

                for i in range(steps):
                    scoring, attending = i < NT, i >= 2
                    for h in range(HEADS + 1):
                        if attending and h:
                            turn(i - 2, h - 1, 0)
                        if scoring and h < HEADS:
                            score_head(i, h)
                        if attending and h:
                            turn(i - 2, h - 1, 1)
                        if scoring and h:
                            sum_head(i, h - 1)
                        if attending and h < HEADS - 1:
                            logits_head(i - 2, h + 1)
                        if attending and h == 5:
                            values(i - 2, 0)
                    if 1 <= i <= NT:
                        logits_head(i - 1, 0)
                    if attending:
                        values(i - 2, 1)

            @block.scalar
            def _(act):
                def rectify(a, h):
                    act.wait_ge(scores_ready, HEADS * a + h + 1)
                    if a or h >= 2:
                        act.wait_ge(score_step, HEADS * a + h - 1)
                    n = (blocks[a] + 1) * P
                    act.activation(relu[:, h % 2, 0:n], keys(SCORES, n), ACT.Relu, scale=HD ** -0.5) \
                        .then_inc(relu_done, 1)

                def copy_score(a):
                    act.wait_ge(score_step, HEADS * (a + 1))
                    if a >= 2:
                        act.wait_ge(never_ready, a - 1)
                    n = (blocks[a] + 1) * P
                    act.activation(score[:, a % 2, 0:n], keys(SUM, n), ACT.Copy).then_inc(score_copied, 1)

                def exponentials(a, h):
                    act.wait_ge(logits_masked, HEADS * a + h + 1)
                    n = (blocks[a] + 1) * P
                    act.activation(logit[:, h % 2, 0:n], logit[:, h % 2, 0:n], ACT.Exp, scale=-1.0,
                                   bias=low[:, h:h + 1], accum_out=total[:, h:h + 1]).then_inc(exp_done, 1)

                def copy_turned(a, h, half):
                    if half >= halves[a]:
                        return
                    g, j = h // 4, h % 4
                    act.wait_ge(p_turned, turns(a, h) - halves[a] + half + 1)
                    if a:
                        act.wait_ge(pv_ready, 2 * (a - 1) + g + 1)
                    n = min(4, blocks[a] + 1 - 4 * half)
                    act.activation(turned[:, g, 4 * half:4 * half + n, j, :],
                                   psum[:, TURNED, :].rearrange("p (c t) -> p c t", t=P)[:, 0:n, :],
                                   ACT.Copy).then_inc(p_copied, 1)

                def copy_y(a, g):
                    act.wait_ge(pv_ready, 2 * a + g + 1)
                    at, b = slice(g * HD, (g + 1) * HD), blocks[a]
                    act.activation(out[at, :, b * P:(b + 1) * P],
                                   psum[at, VALUES, :].rearrange("p (j t) -> p j t", j=4), ACT.Copy) \
                        .then_inc(y_copied, 1)

                for i in range(steps):
                    scoring, attending = i < NT, i >= 2
                    for h in range(HEADS + 1):
                        if attending and h < HEADS:
                            exponentials(i - 2, h)
                        if attending and h:
                            copy_turned(i - 2, h - 1, 0)
                        if scoring and h < HEADS:
                            rectify(i, h)
                        if attending and h:
                            copy_turned(i - 2, h - 1, 1)
                        if attending and h == 5:
                            copy_y(i - 2, 0)
                    if scoring:
                        copy_score(i)
                    if attending:
                        copy_y(i - 2, 1)

            @block.gpsimd
            def _(pool):
                def weight(a, h):
                    if a or h >= 2:
                        pool.wait_ge(score_step, HEADS * a + h - 1)
                    pool.tensor_scalar(w_diag[:, h % 2, :], K.const("ident"), w_idx[:, blocks[a], h:h + 1], None,
                                       op0=ALU.mult).then_inc(w_diag_ready, 1)

                def over_sum(a, h):
                    pool.wait_ge(sum_inverted, HEADS * a + h + 1)
                    if h >= 2 or a:
                        pool.wait_ge(p_turned, turns(a, h - 2) if h >= 2 else turns(a - 1, HEADS + h - 2))
                    pool.tensor_scalar(p_diag[:, h % 2, :], K.const("ident"), total[:, h:h + 1], None,
                                       op0=ALU.mult).then_inc(p_diag_ready, 1)

                for i in range(steps):
                    for h in range(HEADS):
                        if i < NT:
                            weight(i, h)
                        if i >= 2:
                            over_sum(i - 2, h)
                    if i < NT:
                        pool.wait_ge(score_copied, i + 1)
                        b = blocks[i]
                        own = score[:, i % 2, b * P:(b + 1) * P]
                        pool.affine_select(out=own, in_=own, pattern=[[-1, P]], compare_op=ALU.is_ge, fill=FAR,
                                           base=0, channel_multiplier=1).then_inc(causal_done, 1)

            @block.vector
            def _(dve):
                c = Chain(dve, K.dve_done)

                def mask(a, h):
                    dve.wait_ge(logits_ready, HEADS * a + h + 1)
                    if h >= 2 or a:
                        dve.wait_ge(p_turned, turns(a, h - 2) if h >= 2 else turns(a - 1, HEADS + h - 2))
                    if h == 0:
                        dve.wait_ge(never_ready, a + 1)
                    n = (blocks[a] + 1) * P
                    dve.tensor_tensor_reduce(out=logit[:, h % 2, 0:n], in0=keys(LOGITS, n), in1=never[:, 0:n],
                                             scale=-HD ** -0.5, scalar=3.0e38, op0=ALU.add, op1=ALU.min,
                                             accum_out=low[:, h:h + 1]).then_inc(logits_masked, 1)

                def invert(a, h):
                    dve.wait_ge(exp_done, HEADS * a + h + 1)
                    dve.reciprocal(total[:, h:h + 1], total[:, h:h + 1]).then_inc(sum_inverted, 1)

                def take(a, n, count):
                    s = score[:, a % 2, 0:n]
                    for _ in range(count):
                        c(dve.max(top[:], s))
                        c(dve.match_replace(s, top[:], s, TAKEN))

                for i in range(1, steps):
                    selecting, attending = i <= NT, i >= 2
                    n = (blocks[i - 1] + 1) * P if selecting else 0
                    per = rounds // HEADS if n > TOPK else 0
                    for h in range(HEADS):
                        if attending:
                            mask(i - 2, h)
                        if selecting and h == 0:
                            dve.wait_ge(causal_done, i)
                        take(i - 1, n, per // 2)
                        if attending and per:
                            invert(i - 2, h)
                        elif attending and h:
                            invert(i - 2, h - 1)
                        take(i - 1, n, per // 2)
                    if attending and not per:
                        invert(i - 2, HEADS - 1)
                    if selecting:
                        s = score[:, (i - 1) % 2, 0:n]
                        if n > TOPK:
                            ins = dve.tensor_scalar(never[:, 0:n], s, 0.5 * (TAKEN + FAR), NEVER,
                                                    op0=ALU.is_gt, op1=ALU.mult)
                        else:
                            ins = dve.tensor_scalar(never[:, 0:n], s, 0.5 * FAR, NEVER,
                                                    op0=ALU.is_lt, op1=ALU.mult)
                        ins.then_inc(never_ready, 1)
                K.dve_done.n = c.n


def squared_relu_mlp(nc, K, h, w_up, w_down):
    with ExitStack() as ctx:
        hidden = K.sbuf(ctx, "hidden", [P, FT, HALF])
        for half in range(S // HALF):
            at = half * HALF
            h_half = h[:, :, at:at + HALF]

            def square(dve, t, j):
                tile = hidden[:, bass.ds(t, 1), :]
                return dve.tensor_tensor(out=tile, in0=tile, in1=tile, op=ALU.mult)
            with ExitStack() as up:
                dense(nc, K, w_up, FT, 1, KT, None, HALF,
                      lambda eng, acc, t, j: eng.activation(hidden[:, bass.ds(t, 1), :], acc, ACT.Relu),
                      post=square, parts=K.pair(up, "h_half", [P, KT, HALF]), to_split=h_half)
            mlp_down(nc, K, hidden, w_down, h_half)


def mlp_down(nc, K, hidden, weights, out):
    PER, OUTS = 2, 4
    slabs = FT // PER
    total = slabs * (KT // OUTS)
    ahead, after = K.turn_of_ring()
    with ExitStack() as ctx:
        w_high = K.sbuf(ctx, "weight_high", [P, 2, PER * OUTS * P], F32R)
        w_low = K.sbuf(ctx, "weight_low", [P, 2, PER * OUTS * P], F32R)
        x_high = K.sbuf(ctx, "hidden_high", [P, 2, PER, HALF], F32R)
        x_low = K.sbuf(ctx, "hidden_low", [P, 2, PER, HALF], F32R)
        used0, high0, xhigh0, split0 = K.slab_used.n, K.slab_high.n, K.tile_high.n, K.slab_split.n
        loaded0 = [f.n for f in K.slab_loaded]

        def over_slabs(eng, per_slab):
            for g in range(KT // OUTS):
                with eng.Fori(0, slabs // RING) as i:
                    for s in range(RING):
                        per_slab(g, i, s)

        with nc.Block() as block:
            @block.sync
            def _(sp):
                if not ahead:
                    first_slabs(sp, K, weights, PER * OUTS * P)
                with sp.Fori(1, total // RING) as i:
                    for s in range(RING):
                        sp.wait_ge(K.slab_used.sem, i * RING + (used0 + s + 1))
                        sp.dma_start(K.ring[:, s, :], weights[i * RING + s]).then_inc(K.slab_loaded[s].sem, 16)
                prefetch(sp, K, after, used0, total)

            @block.vector
            def _(dve):
                def split_both(g, i, s):
                    n = g * slabs + s
                    dve.wait_ge(K.slab_used.sem, i * RING + (used0 + RING + n - 1))
                    dve.wait_ge(K.slab_loaded[s].sem, i * 16 + (loaded0[s] + 16 * (g * slabs // RING + 1)))
                    split(dve, (K.slab_high.sem, i * RING + (high0 + n + 1)), K.ring[:, s, :],
                          w_high[:, s % 2, :], w_low[:, s % 2, :])
                    split(dve, (K.tile_high.sem, i * RING + (xhigh0 + n + 1)),
                          hidden[:, bass.ds(i * (RING * PER) + s * PER, PER), :], x_high[:, s % 2], x_low[:, s % 2]) \
                        .then_inc(K.slab_split.sem, 1)
                over_slabs(dve, split_both)

            @block.tensor
            def _(pe):
                def products(g, i, s, first, last):
                    pe.wait_ge(K.slab_split.sem, i * RING + (split0 + g * slabs + s + 1))
                    for kk in range(PER):
                        for t in range(OUTS):
                            at = slice((kk * OUTS + t) * P, (kk * OUTS + t + 1) * P)
                            for m, (w, x) in enumerate(((w_high, x_high), (w_high, x_low), (w_low, x_high))):
                                mm = pe.matmul(K.psum[:, g * OUTS + t, :], w[:, s % 2, at], x[:, s % 2, kk, :],
                                               start=(first and kk == 0 and m == 0),
                                               stop=(last and kk == PER - 1 and m == 2))
                    mm.then_inc(K.slab_used.sem, 1)
                loops = slabs // RING
                for g in range(KT // OUTS):
                    for s in range(RING):
                        products(g, 0, s, s == 0, False)
                    with pe.Fori(1, loops - 1) as i:
                        for s in range(RING):
                            products(g, i, s, False, False)
                    for s in range(RING):
                        products(g, loops - 1, s, False, s == RING - 1)

            @block.scalar
            def _(act):
                for g in range(KT // OUTS):
                    act.wait_ge(K.slab_used.sem, used0 + RING + (g + 1) * slabs)
                    for t in range(g * OUTS, (g + 1) * OUTS):
                        act.activation(out[:, t, :], K.psum[:, t, :], ACT.Copy)
    K.slab_used.n += total
    K.slab_high.n += total
    K.slab_split.n += total
    K.tile_high.n += total
    for f in K.slab_loaded:
        f.n += 16 * total // RING


def add_tiles(nc, K, x, o):
    with nc.Block() as block:
        @block.vector
        def _(dve):
            for t in range(0, KT, 2):
                dve.tensor_tensor(out=x[:, t, :], in0=x[:, t, :], in1=o[:, t, :], op=ALU.add)

        @block.gpsimd
        def _(pool):
            for t in range(1, KT, 2):
                pool.tensor_tensor(out=x[:, t, :], in0=x[:, t, :], in1=o[:, t, :], op=ALU.add)


R_CONSTS = [("transposed", 4 * P), ("minus_lower", P), ("lower", 6 * P), ("upper", 6 * P), ("no_reset", S)]
R_AT = {}
_n = 0
for _name, _k in R_CONSTS:
    R_AT[_name] = (_n, _k)
    _n += _k
N_R = _n
ALPHA, RHO, BETA, KAPPA, BETA_END, KAPPA_END, V_PART, N_PARTS = 0, 1, 2, 3, 4, 5, 6, 7


def rwkv_features(nc, K, zm, gate, bonus, parts_dram, decay_dram):
    dram = K.dram
    with ExitStack() as ctx:
        def buf(name, shape=(P, S)):
            return K.sbuf(ctx, name, list(shape))
        up = buf("lora_up", (P, 2, W2))
        no_reset = buf("no_reset", (P, S))
        kk, norm, k_mod, b, run, tmp = (buf(n) for n in ("kk", "norm", "k_mod", "b", "run", "tmp"))
        rates, rates_a, e = (buf(n, (P, 2, S)) for n in ("rate", "a", "exps"))
        end = buf("decay_end", (P, WT, S // CH))
        parts = buf("parts", (P, 6, S))
        load0 = K.load_done.n
        pe_sem, act_sem, dve_sem, st_sem = (K.pe_done.sem, K.act_done.sem, K.dve_done.sem, K.store_done.sem)
        pe0, act0, dve0, st0 = K.pe_done.n, K.act_done.n, K.dve_done.n, K.store_done.n
        PE_PER, ACT_PER, DVE_PER, ST_PER = 3, 10, 19, 9 * 16

        def act_at(j, k):
            return act0 + 5 + ACT_PER * j + k - (3 if j == WT - 1 and k > 5 else 0)

        def drained(j):
            return act_at(j - 1, 5) if j else act0 + 5

        def pe_at(j, k):
            return pe0 + PE_PER * j + (1 if j == 0 else 0, 2, 3 if j == WT - 1 else 4)[k]
        R, KF, V = 0, 4, 8
        psum = K.psum

        def two(bank):
            return psum[:, bank:bank + 2, :].rearrange("p b f -> p (b f)")

        with nc.Block() as block:
            @block.sync
            def _(sp):
                sp.dma_start(up[:], dram["lora_up"]).then_inc(K.load_done.sem, 16)
                sp.dma_start(no_reset[:], dram["r_consts"][:, R_AT["no_reset"][0]:R_AT["no_reset"][0] + S]) \
                    .then_inc(K.load_done.sem, 16)
                for j in range(WT):
                    sp.wait_ge(dve_sem, dve0 + DVE_PER * (j + 1))
                    for c in range(6):
                        sp.dma_start(parts_dram[:, :, c, j, :].rearrange("n p t -> p n t"),
                                     parts[:, c, :].rearrange("p (n t) -> p n t", t=P)).then_inc(st_sem, 16)
                    sp.dma_start(parts_dram[:, :, V_PART, j, :].rearrange("n p t -> p n t"),
                                 zm[:, V + j, :].rearrange("p (n t) -> p n t", t=P)).then_inc(st_sem, 16)
                    for half in range(2):
                        sp.dma_start(decay_dram[:, 2 * j + half, :], end[half * HD:(half + 1) * HD, j, :]) \
                            .then_inc(st_sem, 16)
                sp.wait_ge(st_sem, st0 + ST_PER * WT)

            @block.tensor
            def _(pe):
                pe.wait_ge(K.load_done.sem, load0 + 32)
                pe.wait_ge(act_sem, act0 + 2)
                def lora(j):
                    cols = slice(j * P, (j + 1) * P)
                    if j:
                        pe.wait_ge(act_sem, drained(j - 1))
                    for h in range(2):
                        at = slice(h * HALF, (h + 1) * HALF)
                        pe.matmul(psum[:, h, :], up[0:64, 0, cols], zm[0:64, 12, at], start=True, stop=True)
                        pe.matmul(psum[:, 2 + h, :], up[64:128, 0, cols], zm[64:128, 12, at],
                                  start=True, stop=True)
                        mm = pe.matmul(psum[:, 4 + h, :], up[:, 1, cols], zm[:, 13, at], start=True, stop=True)
                    mm.then_inc(pe_sem, 1)

                def head_sums(x):
                    for h in range(2):
                        mm = pe.matmul(psum[:, 6 + h, :], K.const("head_ones"), x[:, h * HALF:(h + 1) * HALF],
                                       start=True, stop=True)
                    mm.then_inc(pe_sem, 1)

                lora(0)
                for j in range(WT):
                    if j:
                        pe.wait_ge(dve_sem, dve0 + DVE_PER * j)
                    pe.wait_ge(act_sem, act_at(j, 1))
                    head_sums(norm)
                    if j < WT - 1:
                        lora(j + 1)
                    pe.wait_ge(dve_sem, dve0 + DVE_PER * j + 14)
                    head_sums(tmp)

            @block.scalar
            def _(act):
                c = Chain(act, K.act_done)
                c.step(act.activation(zm[0:64, 12, :], zm[0:64, 12, :], ACT.Tanh))
                c.step(act.activation(zm[:, 13, :], zm[:, 13, :], ACT.Sigmoid))
                def drain(j):
                    act.wait_ge(pe_sem, pe_at(j, 0))
                    c.step(act.activation(rates[:, j % 2, :], two(0), ACT.Sigmoid, bias=K.col("w0", j)))
                    c.step(act.activation(rates_a[:, j % 2, :], two(2), ACT.Sigmoid, bias=K.col("a0", j)))
                    c.step(act.activation(gate[:, j, :], two(4), ACT.Copy))

                drain(0)
                for j in range(WT):
                    base = dve0 + DVE_PER * j
                    act.wait_ge(dve_sem, base + 1)
                    c.step(act.activation(norm[:], kk[:], ACT.Square))
                    act.wait_ge(pe_sem, pe_at(j, 1))
                    c(act.activation(norm[:], two(6), ACT.Sqrt))
                    if j < WT - 1:
                        drain(j + 1)
                    act.wait_ge(dve_sem, base + 5)
                    c.step(act.activation(e[:, 0, :], tmp[:], ACT.Exp, scale=-DECAY_SCALE))
                    c.step(act.activation(e[:, 1, :], run[:], ACT.Exp, scale=-DECAY_SCALE))
                    act.wait_ge(dve_sem, base + 10)
                    c.step(act.activation(e[:, 0, :], run[:], ACT.Exp, scale=DECAY_SCALE))
                    c.step(act.activation(end[:, j, :], run[:, CH - 1:S:CH], ACT.Exp, scale=-DECAY_SCALE))
                    act.wait_ge(dve_sem, base + 16)
                    c.step(act.activation(e[:, 1, :], run[:], ACT.Exp, scale=-DECAY_SCALE))
                K.act_done.n = c.n

            @block.vector
            def _(dve):
                c = Chain(dve, K.dve_done)
                dve.wait_ge(K.load_done.sem, load0 + 32)
                for j in range(WT):
                    r, k, v = zm[:, R + j, :], zm[:, KF + j, :], zm[:, V + j, :]
                    rate, a = rates[:, j % 2, :], rates_a[:, j % 2, :]
                    c(dve.tensor_scalar(kk[:], k, K.col("k_k", j), None, op0=ALU.mult))
                    dve.wait_ge(act_sem, drained(j))
                    c(dve.tensor_scalar(k_mod[:], a, -1.0, K.col("k_a", j), op0=ALU.add, op1=ALU.mult))
                    c(dve.scalar_tensor_tensor(out=k_mod[:], in0=k_mod[:], scalar=1.0, in1=k,
                                               op0=ALU.add, op1=ALU.mult))
                    c(dve.tensor_tensor_scan(run[:], no_reset[:], rate, 0.0, ALU.mult, ALU.add))
                    c(dve.tensor_tensor(out=tmp[:], in0=run[:], in1=rate, op=ALU.subtract))
                    dve.wait_ge(act_sem, act_at(j, 2))
                    c(dve.tensor_scalar(norm[:], norm[:], 1e-12, None, op0=ALU.max))
                    c(dve.reciprocal(norm[:], norm[:]))
                    c(dve.tensor_tensor(out=kk[:], in0=kk[:], in1=norm[:], op=ALU.mult))
                    c(dve.tensor_tensor(out=b[:], in0=kk[:], in1=a, op=ALU.mult))
                    if j:
                        dve.wait_ge(st_sem, st0 + ST_PER * j)
                    dve.wait_ge(act_sem, act_at(j, 6))
                    c(dve.tensor_tensor(out=parts[:, ALPHA, :], in0=e[:, 0, :], in1=kk[:], op=ALU.mult))
                    dve.wait_ge(act_sem, act_at(j, 7))
                    c(dve.tensor_tensor(out=parts[:, RHO, :], in0=e[:, 1, :], in1=r, op=ALU.mult))
                    dve.wait_ge(act_sem, act_at(j, 8))
                    c(dve.tensor_tensor(out=parts[:, BETA, :], in0=e[:, 0, :], in1=b[:], op=ALU.mult))
                    c(dve.tensor_tensor(out=parts[:, KAPPA, :], in0=e[:, 0, :], in1=k_mod[:], op=ALU.mult))
                    c(dve.scalar_tensor_tensor(out=tmp[:], in0=r, scalar=K.col("r_k", j), in1=k_mod[:],
                                               op0=ALU.mult, op1=ALU.mult))
                    dve.wait_ge(act_sem, act_at(j, 9))
                    left = run[:].rearrange("p (c t) -> p c t", t=CH)
                    c(dve.tensor_copy(norm[:, 0:S // CH], run[:, CH - 1:S:CH]))
                    c(dve.tensor_tensor(out=left, in0=norm[:, 0:S // CH].unsqueeze(2).broadcast_to([P, S // CH, CH]),
                                        in1=left, op=ALU.subtract))
                    dve.wait_ge(act_sem, act_at(j, 10))
                    c(dve.tensor_tensor(out=parts[:, BETA_END, :], in0=e[:, 1, :], in1=b[:], op=ALU.mult))
                    c(dve.tensor_tensor(out=parts[:, KAPPA_END, :], in0=e[:, 1, :], in1=k_mod[:], op=ALU.mult))
                    dve.wait_ge(pe_sem, pe_at(j, 2))
                    c(dve.tensor_tensor(out=bonus[:, j, :], in0=two(6), in1=v, op=ALU.mult))
                K.dve_done.n = c.n
    K.load_done.n += 32
    K.pe_done.n += PE_PER * WT
    K.store_done.n += ST_PER * WT


def shift_mix(nc, K, h, zm, side):
    with ExitStack() as ctx:
        one_less = K.sbuf(ctx, "one_less_mu", [P, SHIFT_TILES])
        before = K.sbuf(ctx, "z_before", [P, 2, S + 1])
        dve0 = K.dve_done.n
        with nc.Block() as block:
            @block.vector
            def _(dve):
                dve.memset(before[:, :, 0:1], 0.0)
                dve.tensor_scalar(one_less[:], K.col("mu", 0, SHIFT_TILES), -1.0, 1.0, op0=ALU.mult, op1=ALU.add) \
                    .then_inc(K.dve_done.sem, 1)
                dve.wait_ge(K.dve_done.sem, dve0 + 1)
        K.dve_done.n += 1

        def drain(eng, acc, t, j):
            eng.activation(before[:, j, 1:S + 1], acc.rearrange("p b f -> p (b f)"), ACT.Copy)
            return eng.activation(zm[:, bass.ds(t, 1), :], acc, ACT.Identity, scale=one_less[:, bass.ds(t, 1)])

        def add(eng, t, j):
            tile = zm[:, bass.ds(t, 1), :]
            return eng.scalar_tensor_tensor(
                out=tile, in0=before[:, j:j + 1, 0:S], scalar=K.cols[:, bass.ds(t + COL_AT["mu"][0], 1)], in1=tile,
                op0=ALU.mult, op1=ALU.add)
        dense(nc, K, K.dram["w_shift"], SHIFT_TILES, 1, KT, None, S, drain, post=add,
              parts=K.pair(ctx, "h", [P, KT, S]), to_split=h, side=side)


def rwkv_chunks(nc, K, parts_dram, decay_dram, y):
    H = HEADS
    with ExitStack() as ctx:
        def buf(name, shape):
            return K.sbuf(ctx, name, list(shape))

        def signals(*names):
            return [K.flag(n).sem for n in names]
        (loaded0, loaded1, masked, turned, copied, pe_low, low_masked, t_made, pe_w, w_copied, pe_delta,
         t_grown, pe_bv, bv_copied, pe_gu, gu_copied, pe_m, m_made, pe_rho, rho_copied, pe_z, z_copied, pe_y,
         y_copied, pe_abde) = signals(
            "parts_loaded_0", "parts_loaded_1", "abde_masked", "parts_turned", "turned_copied",
            "a_ready", "a_masked", "t_started", "w_ready", "w_copied", "delta_ready", "t_grown", "bv_ready",
            "bv_copied", "gu_ready", "gu_copied", "m_ready", "m_made", "rho_ready", "rho_copied", "z_ready",
            "z_copied", "y_ready", "y_tile_copied", "abde_ready")
        loaded = [loaded0, loaded1]
        con = buf("r_consts_sbuf", (P, N_R - S))
        decay = buf("decay", (HD, H, S // CH))
        parts = buf("parts_in", (P, 2, N_PARTS, WT, P))
        abde = buf("abde", (P, H, 4, P))
        low = buf("a_low", (P, H, P))
        T = buf("t", (P, H, P))
        TT = buf("t_turned", (P, H, P))
        W = buf("w", (P, H, P))
        tok = buf("token_major", (P, 2, W2))
        ends = buf("ends", (P, 2, 2, W2))
        bv = buf("bv", (P, W2))
        gu = buf("minus_g_u", (P, 2, W2))
        m_t = buf("m_turned", (HD, 2, H, HD))
        dd = buf("decay_diagonal", (HD, 2, H, HD))
        rho = buf("rho_less_dg", (HD, H, P))
        z = buf("state", (HD, 2, H, HD))
        idle = buf("idle", (P, 3))
        psum = K.psum
        load0 = K.load_done.n
        LEVELS = [2, 4, 8, 16, 32]

        def mask(name, i=0, n=P):
            at = R_AT[name][0] + i * n
            return con[:, at:at + n]

        def head(h):
            return slice((h % 2) * HD, (h % 2 + 1) * HD), h // 2

        def four(bank):
            return psum[:, bank, :].rearrange("p (h t) -> p h t", h=4)

        def body(eng, per_tile):
            with eng.Fori(0, NT // 2) as i:
                for s in range(2):
                    per_tile(i, s)

        def count(i, s, per, k):
            return i * (2 * per) + (s * per + k)

        with nc.Block() as block:
            @block.sync
            def _(sp):
                sp.dma_start(con[:], K.dram["r_consts"][:, 0:N_R - S]).then_inc(K.load_done.sem, 16)
                sp.dma_start(decay[:], decay_dram).then_inc(K.load_done.sem, 16)

                def tile(i, s):
                    sp.wait_ge(y_copied, count(i, s, 1, 1))
                    sp.dma_start(parts[:, s], parts_dram[i * 2 + s]).then_inc(loaded[s], 16)
                body(sp, tile)

            @block.gpsimd
            def _(pool):
                pool.wait_ge(K.load_done.sem, load0 + 32)

                def tile(i, s):
                    pool.wait_ge(m_made, count(i, s, 2, 1))
                    for c in range(2):
                        ins = pool.tensor_tensor(
                            out=dd[:, c], in0=K.const("ident")[0:HD, 0:HD].unsqueeze(1).broadcast_to([HD, H, HD]),
                            in1=decay[:, :, bass.ds(i * 4 + (2 * s + c), 1)].broadcast_to([HD, H, HD]), op=ALU.mult)
                    ins.then_inc(K.pool_done.sem, 1)
                body(pool, tile)

            @block.tensor
            def _(pe):
                pe.wait_ge(K.load_done.sem, load0 + 32)

                def tile(i, s):
                    x = parts[:, s]
                    pe.wait_ge(loaded[s], i * 16 + 16)
                    for h in range(H):
                        at, j = head(h)
                        if h >= 4:
                            pe.wait_ge(masked, count(i, s, H, h - 3))
                        pe.matmul(psum[:, h % 4, 0:2 * P], x[at, BETA, j, :], x[at, 0:2, j, :],
                                  start=True, stop=True)
                        pe.matmul(psum[:, h % 4, 2 * P:4 * P], x[at, KAPPA, j, :], x[at, 0:2, j, :],
                                  start=True, stop=True).then_inc(pe_abde, 1)
                    for h in range(H):
                        at, j = head(h)
                        mm = pe.matmul(four(4 + h % 2)[:, j, :], x[at, ALPHA, j, :], x[at, BETA, j, :],
                                       start=True, stop=True)
                        if h >= H - 2:
                            mm.then_inc(pe_low, 1)
                    for m, part in enumerate((ALPHA, BETA_END, KAPPA_END, V_PART)):
                        if m >= 2:
                            pe.wait_ge(copied, count(i, s, 4, m - 1))
                        for j in range(WT):
                            mm = pe.transpose(psum[:, 6 + m % 2, j * P:(j + 1) * P], x[:, part, j, :],
                                              K.const("ident"))
                        mm.then_inc(turned, 1)
                    pe.wait_ge(t_made, count(i, s, 1, 1))
                    for lv in range(len(LEVELS)):
                        last = lv == len(LEVELS) - 1
                        for q in range(2):
                            if lv:
                                pe.wait_ge(t_grown, count(i, s, 2 * len(LEVELS), 2 * (lv - 1) + q + 1))
                            for h in range(4 * q, 4 * q + 4):
                                mm = pe.matmul(four(3 * q)[:, h % 4, :], abde[:, h, 0, :], T[:, h, :],
                                               start=True, stop=True)
                            mm.then_inc(pe_w, 1)
                        for q in range(2):
                            pe.wait_ge(w_copied, count(i, s, 2 * len(LEVELS), 2 * lv + q + 1))
                            for h in range(4 * q, 4 * q + 4):
                                if not last:
                                    pe.matmul(four(3 * q + 1)[:, h % 4, :], TT[:, h, :], W[:, h, :],
                                              start=True, stop=True)
                                mm = pe.matmul(four(3 * q + 2)[:, h % 4, :], W[:, h, :], TT[:, h, :],
                                               start=True, stop=True)
                            mm.then_inc(pe_delta, 1)
                    pe.wait_ge(copied, count(i, s, 4, 4))
                    for h in range(H):
                        mm = pe.matmul(psum[:, 6, h * HD:(h + 1) * HD], abde[:, h, 2, :],
                                       tok[:, 1, h * HD:(h + 1) * HD], start=True, stop=True)
                    mm.then_inc(pe_bv, 1)
                    pe.wait_ge(t_grown, count(i, s, 2 * len(LEVELS), 2 * len(LEVELS)))
                    for h in range(H):
                        cols = slice(h * HD, (h + 1) * HD)
                        pe.matmul(psum[:, 7, cols], TT[:, h, :], tok[:, 0, cols], start=True, stop=True)
                    pe.wait_ge(bv_copied, count(i, s, 1, 1))
                    for h in range(H):
                        cols = slice(h * HD, (h + 1) * HD)
                        mm = pe.matmul(psum[:, 0, cols], TT[:, h, :], bv[:, cols], start=True, stop=True)
                    mm.then_inc(pe_gu, 1)
                    pe.wait_ge(gu_copied, count(i, s, 1, 1))
                    for c in range(2):
                        for h in range(H):
                            cols = slice(h * HD, (h + 1) * HD)
                            mm = pe.matmul(psum[0:HD, 1 + c, cols], gu[:, 0, cols], ends[:, c, 0, cols],
                                           start=True, stop=True)
                        mm.then_inc(pe_m, 1)
                    for h in range(H):
                        at, j = head(h)
                        o = psum[0:HD, 3 + h // 4, (h % 4) * P:(h % 4 + 1) * P]
                        pe.matmul(o, gu[:, 0, h * HD:(h + 1) * HD], abde[:, h, 1, :], start=(h % 4 == 0), stop=False,
                                  skip_group_check=True)
                        mm = pe.matmul(o, K.const("ident")[:, at], x[:, RHO, j, :], start=False, stop=(h % 4 == 3),
                                       skip_group_check=True)
                    mm.then_inc(pe_rho, 1)
                    for c in range(2):
                        o = psum[0:HD, 5 + c, :]
                        for h in range(H):
                            cols = slice(h * HD, (h + 1) * HD)
                            pe.matmul(o[:, cols], ends[:, c, 1, cols], tok[:, 1, cols], start=(h == 0), stop=False,
                                      skip_group_check=True)
                            if h == H - 1:
                                pe.wait_ge(m_made, count(i, s, 2, c + 2))
                                pe.wait_ge(z_copied, count(i, s, 2, c + 1))
                            pe.matmul(o[:, cols], ends[:, c, 0, cols], gu[:, 1, cols], start=False, stop=False,
                                      skip_group_check=True)
                        for h in range(H):
                            cols = slice(h * HD, (h + 1) * HD)
                            mm = pe.matmul(o[:, cols], m_t[:, c, h, :], z[:, c, h, :], start=False, stop=(h == H - 1),
                                           skip_group_check=True)
                        if c == 0:
                            mm.then_inc(pe_z, 1)
                    pe.wait_ge(rho_copied, count(i, s, 1, 1))
                    for odd in range(2):
                        o = psum[:, 7 if odd == 0 else 0, :]
                        for j in range(WT):
                            h = 2 * j + odd
                            pair = slice(j * P, (j + 1) * P)
                            cols = slice(j * P, (j + 1) * P)
                            pe.matmul(o[:, cols], tok[:, 1, pair], abde[:, h, 3, :], start=(j == 0), stop=False,
                                      skip_group_check=True)
                            pe.matmul(o[:, cols], gu[:, 1, pair], abde[:, h, 1, :], start=False, stop=False,
                                      skip_group_check=True)
                            for c in range(2):
                                mm = pe.matmul(o[:, j * P + c * CH:j * P + (c + 1) * CH], z[:, c, 2 * j:2 * j + 2, :],
                                               rho[:, h, c * CH:(c + 1) * CH], start=False,
                                               stop=(j == WT - 1 and c == 1), skip_group_check=True)
                    mm.then_inc(pe_y, 1)
                    pe.wait_ge(z_copied, count(i, s, 2, 3))
                    pe.wait_ge(y_copied, count(i, s, 1, 3))
                body(pe, tile)

            @block.scalar
            def _(act):
                act.wait_ge(z_copied, 1)

                def tile(i, s):
                    for m in range(4):
                        act.wait_ge(turned, count(i, s, 4, m + 1))
                        of = psum[:, 6 + m % 2, :]
                        if m in (0, 3):
                            ins = act.activation(tok[:, m // 3, :], of, ACT.Copy)
                        else:
                            for c in range(2):
                                rows = slice(c * CH, (c + 1) * CH)
                                ins = act.activation(ends[rows, c, m - 1, :], of[rows], ACT.Copy)
                        ins.then_inc(copied, 1)
                    for lv in range(len(LEVELS)):
                        for q in range(2):
                            act.wait_ge(pe_w, count(i, s, 2 * len(LEVELS), 2 * lv + q + 1))
                            act.activation(W[:, 4 * q:4 * q + 4, :], four(3 * q), ACT.Copy).then_inc(w_copied, 1)
                    act.wait_ge(pe_bv, count(i, s, 1, 1))
                    act.activation(bv[:], psum[:, 6, :], ACT.Copy).then_inc(bv_copied, 1)
                    act.wait_ge(pe_gu, count(i, s, 1, 1))
                    act.activation(gu[:, 0, :], psum[:, 7, :], ACT.Copy, scale=-1.0)
                    act.activation(gu[:, 1, :], psum[:, 0, :], ACT.Copy, scale=-1.0).then_inc(gu_copied, 1)
                    act.wait_ge(pe_rho, count(i, s, 1, 1))
                    act.activation(rho[:, 0:4, :], four(3)[0:HD], ACT.Copy)
                    act.activation(rho[:, 4:8, :], four(4)[0:HD], ACT.Copy).then_inc(rho_copied, 1)
                body(act, tile)

            @block.vector
            def _(dve):
                dve.memset(ends[:], 0.0)
                dve.memset(z[:], 0.0).then_inc(z_copied, 1)
                dve.sem_inc(m_made, 1)
                dve.sem_inc(y_copied, 2)
                dve.wait_ge(K.load_done.sem, load0 + 32)

                def tile(i, s):
                    for h in range(H):
                        dve.wait_ge(pe_abde, count(i, s, H, h + 1))
                        dve.tensor_tensor(out=abde[:, h].rearrange("p a t -> p (a t)"), in0=psum[:, h % 4, :],
                                          in1=mask("transposed", 0, 4 * P), op=ALU.mult).then_inc(masked, 1)
                    dve.wait_ge(pe_low, count(i, s, 2, 2))
                    for q in range(2):
                        dve.tensor_tensor(out=low[:, q:H:2, :], in0=four(4 + q),
                                          in1=mask("minus_lower").unsqueeze(1).broadcast_to([P, 4, P]), op=ALU.mult) \
                            .then_inc(low_masked, 1)
                    for m in (T, TT):
                        ins = dve.tensor_copy(m[:], K.const("ident").unsqueeze(1).broadcast_to([P, H, P]))
                    ins.then_inc(low_masked, 1)
                    dve.wait_ge(low_masked, count(i, s, 3, 3))
                    dve.wait_ge(masked, count(i, s, H, H))
                    dve.memset(idle[:, 2:3], 0.0)
                    for m, name, of in ((T, "lower", low[:]), (TT, "upper", abde[:, :, 0, :])):
                        ins = dve.copy_predicated(
                            m[:], mask(name, 0).bitcast(U32).unsqueeze(1).broadcast_to([P, H, P]), of)
                    ins.then_inc(t_made, 1)
                    for lv in range(len(LEVELS)):
                        for q in range(2):
                            dve.wait_ge(pe_delta, count(i, s, 2 * len(LEVELS), 2 * lv + q + 1))
                            dve.memset(idle[:, q:q + 1], 0.0)
                            for m, name, bank in ((T, "lower", 3 * q + 1), (TT, "upper", 3 * q + 2)):
                                if lv == len(LEVELS) - 1 and m is T:
                                    continue
                                ins = dve.copy_predicated(
                                    m[:, 4 * q:4 * q + 4, :],
                                    mask(name, lv + 1).bitcast(U32).unsqueeze(1).broadcast_to([P, 4, P]), four(bank))
                            ins.then_inc(t_grown, 1)
                    dve.wait_ge(K.pool_done.sem, count(i, s, 1, K.pool_done.n + 1))
                    for c in range(2):
                        dve.wait_ge(pe_m, count(i, s, 2, c + 1))
                        dve.tensor_tensor(out=m_t[:, c], in0=psum[0:HD, 1 + c, :].rearrange("p (h k) -> p h k", h=H),
                                          in1=dd[:, c], op=ALU.add).then_inc(m_made, 1)
                    dve.wait_ge(pe_z, count(i, s, 1, 1))
                    dve.tensor_copy(z[:, 1], psum[0:HD, 5, :].rearrange("p (h k) -> p h k", h=H)).then_inc(z_copied, 1)
                    dve.wait_ge(pe_y, count(i, s, 1, 1))
                    dve.tensor_copy(z[:, 0], psum[0:HD, 6, :].rearrange("p (h k) -> p h k", h=H)).then_inc(z_copied, 1)
                    for odd in range(2):
                        rows = slice(odd * HD, (odd + 1) * HD)
                        ins = dve.tensor_copy(y[rows, :, bass.ds(i * (2 * P) + s * P, P)],
                                              psum[rows, 7 if odd == 0 else 0, :].rearrange("p (j t) -> p j t", j=WT))
                    ins.then_inc(y_copied, 1)
                body(dve, tile)
    K.load_done.n += 32
    K.pool_done.n += NT


def rwkv_finish(nc, K, y, bonus, gate):
    with ExitStack() as ctx:
        sq = K.sbuf(ctx, "centred_squares", [P, 2, S])
        root = K.sbuf(ctx, "head_root", [P, 2, S])
        pe0, act0, dve0 = K.pe_done.n, K.act_done.n, K.dve_done.n
        pe_sem, act_sem, dve_sem = K.pe_done.sem, K.act_done.sem, K.dve_done.sem

        def two(b):
            return K.psum[:, b:b + 2, :].rearrange("p b f -> p (b f)")

        def first(t):
            return 2 * t if t else 1

        def second(t):
            return 2 * t + 3 if t < WT - 1 else 2 * WT

        def centred(t):
            return dve0 + (5 * t - 3 if t else 1)

        with nc.Block() as block:
            @block.tensor
            def _(pe):
                def mean(t):
                    if t >= 2:
                        pe.wait_ge(dve_sem, centred(t - 2))
                    for h in range(2):
                        mm = pe.matmul(K.psum[:, 2 * (t % 2) + h, :], K.const("head_ones"),
                                       y[:, t, h * HALF:(h + 1) * HALF], start=True, stop=True)
                    mm.then_inc(pe_sem, 1)
                mean(0)
                for t in range(WT):
                    if t + 1 < WT:
                        mean(t + 1)
                    pe.wait_ge(act_sem, act0 + first(t))
                    for h in range(2):
                        mm = pe.matmul(K.psum[:, 4 + 2 * (t % 2) + h, :], K.const("head_ones"),
                                       sq[:, t % 2, h * HALF:(h + 1) * HALF], start=True, stop=True)
                    mm.then_inc(pe_sem, 1)

            @block.scalar
            def _(act):
                def square(t):
                    if t >= 2:
                        act.wait_ge(pe_sem, pe0 + second(t - 2))
                    act.wait_ge(dve_sem, centred(t))
                    act.activation(sq[:, t % 2, :], y[:, t, :], ACT.Square).then_inc(act_sem, 1)
                square(0)
                for t in range(WT):
                    if t + 1 < WT:
                        square(t + 1)
                    act.wait_ge(pe_sem, pe0 + second(t))
                    if t >= 2:
                        act.wait_ge(dve_sem, centred(t - 1) + 4)
                    act.activation(root[:, t % 2, :], two(4 + 2 * (t % 2)), ACT.Sqrt, scale=1.0 / HD,
                                   bias=K.col("lnx_eps")).then_inc(act_sem, 1)

            @block.vector
            def _(dve):
                c = Chain(dve, K.dve_done)

                def centre(t):
                    dve.wait_ge(pe_sem, pe0 + first(t))
                    c(dve.scalar_tensor_tensor(out=y[:, t, :], in0=two(2 * (t % 2)), scalar=-1.0 / HD,
                                               in1=y[:, t, :], op0=ALU.mult, op1=ALU.add))
                centre(0)
                for t in range(WT):
                    if t + 1 < WT:
                        centre(t + 1)
                    dve.wait_ge(act_sem, act0 + second(t))
                    c(dve.reciprocal(root[:, t % 2, :], root[:, t % 2, :]))
                    c(dve.scalar_tensor_tensor(out=y[:, t, :], in0=y[:, t, :], scalar=K.col("lnx_w", t),
                                               in1=root[:, t % 2, :], op0=ALU.mult, op1=ALU.mult))
                    c(dve.scalar_tensor_tensor(out=y[:, t, :], in0=y[:, t, :], scalar=K.col("lnx_b", t),
                                               in1=bonus[:, t, :], op0=ALU.add, op1=ALU.add))
                    c(dve.tensor_tensor(out=y[:, t, :], in0=y[:, t, :], in1=gate[:, t, :], op=ALU.mult))
                K.dve_done.n = c.n
    K.pe_done.n += 2 * WT
    K.act_done.n += 2 * WT


def ssm_prepare(nc, K, s5):
    mag, power, b_t, c_re, c_im, table = s5
    N = SSM_TILES
    with ExitStack() as ctx:
        def buf(name, shape=(P, N)):
            return K.sbuf(ctx, name, list(shape))
        dt, are, small, em, theta, turns, cos, sin, half = (
            buf(n) for n in ("dt", "are", "dt_are", "expm1", "theta", "theta_turns", "cos_theta", "sin_theta",
                             "sin_half"))
        t0, t1, nr, ai, rden, cr, ci = (buf(n) for n in ("s5_t0", "s5_t1", "nr", "abar_im", "rden", "coef_re", "coef_im"))
        b_re, b_im, b1, b2 = (buf(n, (P, N, 32)) for n in ("b_re", "b_im", "bbar_re", "bbar_im"))
        tmp = buf("s5_tmp", (P, N, 64))
        a_im = K.col("a_im", 0, N)
        act0, dve0, load0, pe0 = K.act_done.n, K.dve_done.n, K.load_done.n, K.pe_done.n
        at = {}

        def wide(x, n):
            return x.unsqueeze(2).broadcast_to([P, N, n])

        with nc.Block() as block:
            @block.sync
            def _(sp):
                for to, name in ((b_re, "b_re"), (b_im, "b_im"), (c_re, "c_re"), (c_im, "c_im")):
                    sp.dma_start(to[:], K.dram[name]).then_inc(K.load_done.sem, 16)

            @block.vector
            def _(dve):
                c = Chain(dve, K.dve_done)
                dve.wait_ge(K.act_done.sem, act0 + 1)
                c(dve.tensor_scalar(are[:], K.col("a_re", 0, N), -1e-4, None, op0=ALU.min))
                c(dve.tensor_tensor(out=small[:], in0=dt[:], in1=are[:], op=ALU.mult))
                c(dve.tensor_tensor(out=theta[:], in0=dt[:], in1=a_im, op=ALU.mult))
                reduce_angle(dve, c, sin[:], turns[:], theta[:], 0.0)
                reduce_angle(dve, c, cos[:], turns[:], theta[:], 0.25)
                c(dve.tensor_scalar(theta[:], theta[:], 0.5, None, op0=ALU.mult))
                reduce_angle(dve, c, half[:], turns[:], theta[:], 0.0)
                at["angles"] = c.n
                c(dve.tensor_scalar(em[:], small[:], 1.0 / 10, 1.0, op0=ALU.mult, op1=ALU.add))
                for m in range(9, 1, -1):
                    c(dve.scalar_tensor_tensor(out=em[:], in0=em[:], scalar=1.0 / m, in1=small[:],
                                               op0=ALU.mult, op1=ALU.mult))
                    c(dve.tensor_scalar(em[:], em[:], 1.0, None, op0=ALU.add))
                c(dve.tensor_tensor(out=em[:], in0=em[:], in1=small[:], op=ALU.mult))
                dve.wait_ge(K.act_done.sem, act0 + 5)
                c(dve.tensor_scalar(t0[:], t0[:], -1.0, None, op0=ALU.add))
                c(dve.tensor_scalar(t1[:], small[:], -0.5, None, op0=ALU.is_lt))
                c(dve.copy_predicated(em[:], t1[:].bitcast(U32), t0[:]))
                c(dve.tensor_scalar(mag, em[:], 1.0, None, op0=ALU.add))
                c(dve.tensor_tensor(out=nr[:], in0=em[:], in1=cos[:], op=ALU.mult))
                c(dve.scalar_tensor_tensor(out=half[:], in0=half[:], scalar=-2.0, in1=half[:], op0=ALU.mult,
                                           op1=ALU.mult))
                c(dve.tensor_tensor(out=nr[:], in0=nr[:], in1=half[:], op=ALU.add))
                c(dve.tensor_tensor(out=ai[:], in0=mag, in1=sin[:], op=ALU.mult))
                c(dve.tensor_tensor(out=t0[:], in0=are[:], in1=are[:], op=ALU.mult))
                c(dve.tensor_tensor(out=t1[:], in0=a_im, in1=a_im, op=ALU.mult))
                c(dve.tensor_tensor(out=rden[:], in0=t0[:], in1=t1[:], op=ALU.add))
                c(dve.reciprocal(rden[:], rden[:]))
                for o, x, y, op in ((cr, are[:], a_im, ALU.add), (ci, a_im, are[:], ALU.subtract)):
                    c(dve.tensor_tensor(out=t0[:], in0=nr[:], in1=x, op=ALU.mult))
                    c(dve.tensor_tensor(out=t1[:], in0=ai[:], in1=y, op=ALU.mult))
                    c(dve.tensor_tensor(out=o[:], in0=t1[:], in1=t0[:], op=op))
                    c(dve.tensor_tensor(out=o[:], in0=o[:], in1=rden[:], op=ALU.mult))
                dve.wait_ge(K.load_done.sem, load0 + 64)
                t32 = tmp[:, :, 0:32]
                for o, x, y, op in ((b1, b_re, b_im, ALU.subtract), (b2, b_im, b_re, ALU.add)):
                    c(dve.tensor_tensor(out=o[:], in0=x[:], in1=wide(cr[:], 32), op=ALU.mult))
                    c(dve.tensor_tensor(out=t32, in0=y[:], in1=wide(ci[:], 32), op=ALU.mult))
                    c(dve.tensor_tensor(out=o[:], in0=o[:], in1=t32, op=op))
                at["bbar"] = c.n
                c(dve.tensor_scalar(c_im, c_im, -1.0, None, op0=ALU.mult))
                c(dve.tensor_copy(power[:, 0, 0, :], cos[:]))
                c(dve.tensor_copy(power[:, 1, 0, :], sin[:]))
                for m in range(1, 10):
                    pc, ps = power[:, 0, m - 1, :], power[:, 1, m - 1, :]
                    c(dve.tensor_tensor(out=t0[:], in0=pc, in1=pc, op=ALU.mult))
                    c(dve.tensor_tensor(out=t1[:], in0=ps, in1=ps, op=ALU.mult))
                    c(dve.tensor_tensor(out=power[:, 0, m, :], in0=t0[:], in1=t1[:], op=ALU.subtract))
                    c(dve.scalar_tensor_tensor(out=power[:, 1, m, :], in0=pc, scalar=2.0, in1=ps, op0=ALU.mult,
                                               op1=ALU.mult))
                c(dve.memset(table[:, 0, :, 0:1], 1.0))
                c(dve.memset(table[:, 1, :, 0:1], 0.0))
                for m in range(7):
                    n = 1 << m
                    pc, ps = wide(power[:, 0, m, :], n), wide(power[:, 1, m, :], n)
                    er, ei = table[:, 0, :, 0:n], table[:, 1, :, 0:n]
                    for o, x, y, op in ((0, er, ei, ALU.subtract), (1, ei, er, ALU.add)):
                        c(dve.tensor_tensor(out=table[:, o, :, n:2 * n], in0=x, in1=pc, op=ALU.mult))
                        c(dve.tensor_tensor(out=tmp[:, :, 0:n], in0=y, in1=ps, op=ALU.mult))
                        c(dve.tensor_tensor(out=table[:, o, :, n:2 * n], in0=table[:, o, :, n:2 * n],
                                            in1=tmp[:, :, 0:n], op=op))
                for m, x in enumerate((b1, b2)):
                    c(dve.memset(b_t[:, m], 0.0))
                for m in range(2):
                    dve.wait_ge(K.pe_done.sem, pe0 + m + 1)
                    for q in range(4):
                        rows = slice(32 * q, 32 * q + 32)
                        c(dve.tensor_copy(b_t[rows, m, q:N:4, :],
                                          K.psum[rows, m, :].rearrange("p (g k) -> p g k", g=4)))
                K.dve_done.n = c.n

            @block.scalar
            def _(act):
                c = Chain(act, K.act_done)
                c.step(act.activation(dt[:], K.col("log_dt", 0, N), ACT.Exp))
                act.wait_ge(K.dve_done.sem, at["angles"])
                c.step(act.activation(sin[:], sin[:], ACT.Sin))
                c.step(act.activation(cos[:], cos[:], ACT.Sin))
                c.step(act.activation(half[:], half[:], ACT.Sin))
                c.step(act.activation(t0[:], small[:], ACT.Exp))
                K.act_done.n = c.n

            @block.tensor
            def _(pe):
                pe.wait_ge(K.dve_done.sem, at["bbar"])
                for m, x in enumerate((b1, b2)):
                    for g in range(4):
                        mm = pe.transpose(K.psum[:, m, g * P:(g + 1) * P],
                                          x[:, 4 * g:4 * g + 4, :].rearrange("p s c -> p (s c)"), K.const("ident"))
                    mm.then_inc(K.pe_done.sem, 1)
    K.load_done.n += 64
    K.pe_done.n += 2


def ssm_scan(nc, K, s5, u, h, ya, gate_dram):
    mag, power, b_t, c_re, c_im, table = s5
    N = SSM_TILES
    with ExitStack() as ctx:
        phase = K.sbuf(ctx, "phase", [P, 2, 2, S])
        t = K.sbuf(ctx, "turned_inputs", [P, 4, S])
        x = K.sbuf(ctx, "states", [P, 4, S])
        run = K.sbuf(ctx, "scanned", [P, 2, S])
        tmp = K.sbuf(ctx, "phase_tmp", [P, 2, HALF])
        gate = K.sbuf(ctx, "gates", [P, S])
        names = ("bu_ready", "inputs_turned", "input_summed", "scanned_done", "states_turned", "state_summed",
                 "phase_scaled", "phase_grown", "c_used", "y_summed", "gate_made", "gate_used", "gate_stored",
                 "phase_started")
        (bu_ready, in_turned, in_summed, scanned, st_turned, st_summed, ph_scaled, ph_grown, c_used, y_summed,
         gate_made, gate_used, gate_stored, ph_started) = (K.flag(n).sem for n in names)
        psum = K.psum
        slab0, loaded0 = K.slab_used.n, [f.n for f in K.slab_loaded]
        ahead, after = K.turn_of_ring()
        assert GATE_TILES == N

        def two(b):
            return psum[:, b:b + 2, :].rearrange("p b f -> p (b f)")

        with nc.Block() as block:
            @block.sync
            def _(sp):
                if not ahead:
                    first_slabs(sp, K, K.dram["w_gates"], KT * P)
                for s in range(N):
                    if s >= RING:
                        sp.wait_ge(K.slab_used.sem, slab0 + s + 1)
                        sp.dma_start(K.ring[:, s % RING, :], K.dram["w_gates"][s]) \
                            .then_inc(K.slab_loaded[s % RING].sem, 16)
                    if s >= KT + 1:
                        sp.wait_ge(gate_made, s)
                        sp.dma_start(gate_dram[:, s - 1 - KT, :], gate[:]).then_inc(gate_stored, 16)
                prefetch(sp, K, after, slab0, N)
                sp.wait_ge(gate_made, N)
                sp.dma_start(gate_dram[:, KT - 1, :], gate[:]).then_inc(gate_stored, 16)
                sp.wait_ge(gate_stored, 16 * KT)

            @block.tensor
            def _(pe):
                def outputs(s):
                    pe.wait_ge(st_summed, 2 * (s + 1))
                    if s % 4 == 0 and s:
                        pe.wait_ge(y_summed, s // 4)
                    rows = slice(32 * (s % 4), 32 * (s % 4) + 32)
                    for h_ in range(2):
                        for m, (w, part) in enumerate(((c_re, 0), (c_im, 2))):
                            mm = pe.matmul(psum[rows, 4 + h_, :], w[:, s, :],
                                           x[:, part, h_ * HALF:(h_ + 1) * HALF], start=(m == 0), stop=(m == 1))
                    mm.then_inc(c_used, 1)

                def gates(s):
                    slot = s % RING
                    pe.wait_ge(K.slab_loaded[slot].sem, loaded0[slot] + 16 * (s // RING + 1))
                    if s:
                        pe.wait_ge(gate_made, s)
                    for k in range(KT):
                        for h_ in range(2):
                            mm = pe.matmul(psum[:, 6 + h_, :], K.ring[:, slot, k * P:(k + 1) * P],
                                           h[:, k, h_ * HALF:(h_ + 1) * HALF], start=(k == 0), stop=(k == KT - 1))
                    mm.then_inc(K.slab_used.sem, 1)

                for s in range(N):
                    if s:
                        pe.wait_ge(in_turned, 4 * s)
                    for m in range(2):
                        for h_ in range(2):
                            mm = pe.matmul(psum[:, 2 * m + h_, :], b_t[:, m, s, :],
                                           u[:, s // 4, h_ * HALF:(h_ + 1) * HALF], start=True, stop=True)
                    mm.then_inc(bu_ready, 1)
                    gates(s)
                    if s:
                        outputs(s - 1)
                outputs(N - 1)

            @block.gpsimd
            def _(pool):
                def grow_phase(s):
                    er, ei = phase[:, s % 2, 0, :], phase[:, s % 2, 1, :]
                    for m in range(7, 10):
                        n = 1 << m
                        pool.wait_ge(ph_scaled, 3 * s + m - 6)
                        pool.tensor_tensor(out=er[:, n:2 * n], in0=er[:, n:2 * n], in1=tmp[:, 0, 0:n],
                                           op=ALU.subtract)
                        pool.tensor_tensor(out=ei[:, n:2 * n], in0=ei[:, n:2 * n], in1=tmp[:, 1, 0:n], op=ALU.add) \
                            .then_inc(ph_grown, 1)

                grow_phase(0)
                grow_phase(1)
                for s in range(N):
                    pool.wait_ge(in_turned, 4 * s + 2)
                    pool.tensor_tensor(out=t[:, 0, :], in0=t[:, 0, :], in1=t[:, 1, :], op=ALU.add) \
                        .then_inc(in_summed, 1)
                    pool.wait_ge(in_turned, 4 * (s + 1))
                    pool.tensor_tensor(out=t[:, 2, :], in0=t[:, 2, :], in1=t[:, 3, :], op=ALU.subtract) \
                        .then_inc(in_summed, 1)
                    if s and s + 1 < N:
                        grow_phase(s + 1)

            @block.vector
            def _(dve):
                def turn_states(s):
                    er, ei = phase[:, s % 2, 0, :], phase[:, s % 2, 1, :]
                    dve.wait_ge(scanned, 2 * (s + 1))
                    if s:
                        dve.wait_ge(c_used, s)
                    for m, (y, e) in enumerate(((0, er), (1, ei), (0, ei), (1, er))):
                        dve.tensor_tensor(out=x[:, m, :], in0=run[:, y, :], in1=e, op=ALU.mult) \
                            .then_inc(st_turned, 1)
                    for m, op in ((0, ALU.subtract), (2, ALU.add)):
                        dve.wait_ge(st_turned, 4 * s + m + 2)
                        dve.tensor_tensor(out=x[:, m, :], in0=x[:, m, :], in1=x[:, m + 1, :], op=op) \
                            .then_inc(st_summed, 1)

                def finish_channels(g):
                    dve.wait_ge(c_used, 4 * (g + 1))
                    dve.scalar_tensor_tensor(out=u[:, g, :], in0=u[:, g, :], scalar=K.col("d_skip", g),
                                             in1=two(4), op0=ALU.mult, op1=ALU.add).then_inc(y_summed, 1)

                def use_gate(s):
                    dve.wait_ge(gate_made, s + 1)
                    dve.tensor_tensor(out=ya[:, s, :], in0=ya[:, s, :], in1=gate[:], op=ALU.mult) \
                        .then_inc(gate_used, 1)

                for s in range(N):
                    er, ei = phase[:, s % 2, 0, :], phase[:, s % 2, 1, :]
                    dve.wait_ge(ph_grown, 3 * (s + 1))
                    dve.wait_ge(bu_ready, s + 1)
                    if s:
                        dve.wait_ge(scanned, 2 * s)
                    for m, (b, e) in enumerate(((0, er), (2, ei), (2, er), (0, ei))):
                        dve.tensor_tensor(out=t[:, m, :], in0=two(b), in1=e, op=ALU.mult).then_inc(in_turned, 1)
                    if s:
                        turn_states(s - 1)
                    factor = mag[:, s:s + 1].broadcast_to([P, S])
                    for m in range(2):
                        dve.wait_ge(in_summed, 2 * s + m + 1)
                        if s and m == 0:
                            dve.wait_ge(st_turned, 4 * s)
                        dve.tensor_tensor_scan(run[:, m, :], factor, t[:, 2 * m, :], 0.0, ALU.mult, ALU.add) \
                            .then_inc(scanned, 1)
                    if 0 < s <= KT:
                        use_gate(s - 1)
                    if s and s % 4 == 0:
                        finish_channels(s // 4 - 1)
                turn_states(N - 1)
                finish_channels(N // 4 - 1)

            @block.scalar
            def _(act):
                def scale_phase(s):
                    if s >= 2:
                        act.wait_ge(st_turned, 4 * (s - 1))
                    for o in range(2):
                        act.activation(phase[:, s % 2, o, 0:P], table[:, o, s, :], ACT.Copy).then_inc(ph_started, 1)
                    act.wait_ge(ph_started, 2 * (s + 1))
                    er, ei = phase[:, s % 2, 0, :], phase[:, s % 2, 1, :]
                    for m in range(7, 10):
                        n = 1 << m
                        if s or m > 7:
                            act.wait_ge(ph_grown, 3 * s + m - 7)
                        pc, ps = power[:, 0, m, s:s + 1], power[:, 1, m, s:s + 1]
                        for o, of, to, f in ((er, er, 0, pc), (ei, ei, 1, pc)):
                            act.activation(o[:, n:2 * n], of[:, 0:n], ACT.Identity, scale=f)
                        act.activation(tmp[:, 0, 0:n], ei[:, 0:n], ACT.Identity, scale=ps)
                        act.activation(tmp[:, 1, 0:n], er[:, 0:n], ACT.Identity, scale=ps).then_inc(ph_scaled, 1)

                scale_phase(0)
                scale_phase(1)
                for s in range(N):
                    if s and s + 1 < N:
                        scale_phase(s + 1)
                    act.wait_ge(K.slab_used.sem, slab0 + RING + s + 1)
                    if 0 < s <= KT:
                        act.wait_ge(gate_used, s)
                    if s > KT:
                        act.wait_ge(gate_stored, 16 * (s - KT))
                    act.activation(gate[:], two(6), ACT.Sigmoid).then_inc(gate_made, 1)
                for g in range(N // 4):
                    act.wait_ge(y_summed, g + 1)
                    act.activation(u[:, g, :], u[:, g, :], ACT.Gelu)
    K.slab_used.n += N
    for slot in range(RING):
        K.slab_loaded[slot].n += 16 * (N // RING)


def combine(nc, K, ya, yb, ys, gate, gate_dram):
    dram = K.dram
    dve0 = K.dve_done.n
    with ExitStack() as ctx:
        stage = K.sbuf(ctx, "sigmoid", [P, 2, 2, HALF])

        def bias(t, half):
            return K.cols[:, bass.ds(t + COL_AT["b_glu"][0] + half * KT, 1)]

        parts = K.pair(ctx, "ys", [P, WT, S])

        def times_yb(eng, t, j):
            tile = yb[:, bass.ds(t, 1), :].rearrange("p o (b f) -> p (o b) f", b=2)
            return eng.tensor_tensor(out=tile, in0=tile, in1=stage[:, j], op=ALU.mult)
        dense(nc, K, dram["w_glu"][0:KT], KT, 1, WT, None, S,
              lambda eng, acc, t, j: eng.activation(yb[:, bass.ds(t, 1), :], acc, ACT.Identity, bias=bias(t, 0)),
              parts=parts, to_split=ys, side=[(gate[:], gate_dram)])
        dense(nc, K, dram["w_glu"][KT:2 * KT], KT, 1, WT, None, S,
              lambda eng, acc, t, j: eng.activation(stage[:, j], acc, ACT.Sigmoid, bias=bias(t, 1)), post=times_yb,
              parts=parts)
        with nc.Block() as block:
            @block.vector
            def _(dve):
                for t in range(KT):
                    dve.tensor_tensor(out=yb[:, t, :], in0=yb[:, t, :], in1=gate[:, t, :], op=ALU.mult) \
                        .then_inc(K.dve_done.sem, 1)
                    dve.wait_ge(K.dve_done.sem, dve0 + t + 1)
                    dve.tensor_tensor(out=ya[:, t, :], in0=ya[:, t, :], in1=yb[:, t, :], op=ALU.add)
    K.dve_done.n += KT


def build(nc, dram):
    with ExitStack() as ctx:
        K = Core(nc, ctx, dram)
        full, narrow = KT * P, WT * P
        K.ring_order = [
            (dram["w_ada"], full), (dram["w_rot"], full), (dram["w_v"], full), (dram["w_u"], full),
            (dram["w_out"], full), (dram["w_ff1"], full), (dram["w_ff2"], full), (dram["w_ff1"], full),
            (dram["w_ff2"], full), (dram["w_shift"], full), (dram["w_rwkv_proj"], narrow), (dram["w_u2"], full),
            (dram["w_gates"], full), (dram["w_glu"][0:KT], narrow), (dram["w_glu"][KT:2 * KT], narrow),
            (dram["w_out2"], full), (dram["w_ff_up"], full), (dram["w_ff_down"], full), (dram["w_ff_up"], full),
            (dram["w_ff_down"], full),
        ]
        load_setup(nc, K)
        x_t = dram["x"].rearrange("(t p) s -> p t s", p=P)
        merged = K.sbuf(ctx, "merged", [P, KT, S])
        ada(nc, K, (merged[:], x_t))
        with ExitStack() as proj:
            rot = K.sbuf(proj, "q_k_qi_ki", [P, 10, S])
            val = K.sbuf(proj, "values", [P, NT, P])
            w_idx = K.sbuf(proj, "w_idx", [P, NT, HEADS])
            cos = K.sbuf(proj, "cos", [P, S])
            sin = K.sbuf(proj, "sin", [P, S])
            w_val = K.sbuf(proj, "w_val", [P, KT, 136])
            rms_norm(nc, K, proj, merged, KT, merged, lambda t: K.mod[:, 8 + t:9 + t],
                     bias=lambda t: K.mod[:, t:t + 1], side=(w_val[:], dram["w_val"]))
            token_values(nc, K, merged, w_val, val, w_idx)
            with ExitStack() as inner:
                parts = K.pair(inner, "h", [P, KT, S])
                dense(nc, K, dram["w_rot"], 10, 1, KT, None, S,
                      lambda eng, acc, t, j: eng.activation(rot[:, bass.ds(t, 1), :], acc, ACT.Copy),
                      parts=parts, to_split=merged)
                zu = merged[:, 0:4, :]
                zv = merged[:, 4:8, :].rearrange("p t (a f) -> p (t a) f", f=D_SGU)
                token_gelu(nc, K, parts, zv, cos, sin)
                dense(nc, K, dram["w_u"], 4, 1, KT, None, S,
                      lambda eng, acc, t, j: eng.activation(zu[:, bass.ds(t, 1), :], acc, ACT.Gelu_apprx_tanh),
                      parts=parts)
            spatial_gating(nc, K, zu, zv, zu)
            rope(nc, K, rot, 10, cos, sin)
            attention(nc, K, rot, val, w_idx, merged[:, 4:8, :])
        rms_norm(nc, K, ctx, merged[:, 0:4, :], 4, merged[:, 0:4, :], lambda t: K.col("g_out_sgu", t))
        rms_norm(nc, K, ctx, merged[:, 4:8, :], 4, merged[:, 4:8, :], lambda t: K.col("g_out_attn", t))
        x3 = nc.dram_tensor("x3", (P, KT, S), F32).ap()
        with ExitStack() as mid:
            x2 = K.sbuf(mid, "x2", [P, KT, S])
            with ExitStack() as inner:
                o = K.sbuf(inner, "o", [P, KT, S])
                with ExitStack() as split_m:
                    dense(nc, K, dram["w_out"], KT, 1, KT, None, S,
                          lambda eng, acc, t, j: eng.activation(o[:, bass.ds(t, 1), :], acc, ACT.Copy),
                          parts=K.pair(split_m, "merged", [P, KT, S]), to_split=merged, side=[(x2[:], x_t)])
                rms_norm(nc, K, mid, o, KT, x2, lambda t: K.mod[:, 16 + t:17 + t], add=x2)
            rms_norm(nc, K, mid, x2, KT, merged, lambda t: K.mod[:, 32 + t:33 + t],
                     bias=lambda t: K.mod[:, 24 + t:25 + t])
            squared_relu_mlp(nc, K, merged, dram["w_ff1"], dram["w_ff2"])
            rms_norm(nc, K, mid, merged, KT, x2, lambda t: K.mod[:, 40 + t:41 + t], add=x2)
            rms_norm(nc, K, mid, x2, KT, merged, lambda t: K.col("norm1_g", t), side=(x3, x2[:]))
        parts_dram = nc.dram_tensor("rwkv_parts", (NT, P, N_PARTS, WT, P), F32).ap()
        decay_dram = nc.dram_tensor("rwkv_decay", (HD, HEADS, S // CH), F32).ap()
        h_dram = nc.dram_tensor("h_block2", (P, KT, S), F32).ap()
        gate, bonus = merged[:, 0:WT, :], merged[:, WT:2 * WT, :]
        with ExitStack() as inner:
            zm = K.sbuf(inner, "z_mixed", [P, SHIFT_TILES, S])
            shift_mix(nc, K, merged, zm, [(h_dram, merged[:])])
            rwkv_features(nc, K, zm, gate, bonus, parts_dram, decay_dram)
        late = ctx.enter_context(ExitStack())
        h = K.sbuf(late, "h_again", [P, KT, S])
        with ExitStack() as rw:
            y = K.sbuf(rw, "y", [P, WT, S])
            rwkv_chunks(nc, K, parts_dram, decay_dram, y)
            rwkv_finish(nc, K, y, bonus, gate)
            dense(nc, K, dram["w_rwkv_proj"], KT, 1, WT, None, S,
                  lambda eng, acc, t, j: eng.activation(merged[:, bass.ds(t, 1), :], acc, ACT.Copy),
                  parts=K.pair(rw, "y", [P, WT, S]), to_split=y,
                  side=[(h[:], h_dram)])
        gate_dram = nc.dram_tensor("ssm_gate_dram", (P, KT, S), F32).ap()
        with late as sm:
            u = K.sbuf(sm, "u", [P, WT, S])
            with ExitStack() as inner:
                with ExitStack() as split_h:
                    dense(nc, K, dram["w_u2"], WT, 1, KT, None, S,
                          lambda eng, acc, t, j: eng.activation(u[:, bass.ds(t, 1), :], acc, ACT.Copy),
                          parts=K.pair(split_h, "h", [P, KT, S]), to_split=h)
                mag = K.sbuf(inner, "magnitude", [P, SSM_TILES])
                power = K.sbuf(inner, "phase_power", [P, 2, 10, SSM_TILES])
                b_t = K.sbuf(inner, "b_turned", [P, 2, SSM_TILES, P])
                c_re = K.sbuf(inner, "c_re_sbuf", [P, SSM_TILES, 32])
                c_im = K.sbuf(inner, "c_im_sbuf", [P, SSM_TILES, 32])
                table = K.sbuf(inner, "phase_table", [P, 2, SSM_TILES, P])
                s5 = (mag[:], power, b_t, c_re[:], c_im[:], table)
                ssm_prepare(nc, K, s5)
                ssm_scan(nc, K, s5, u, h, merged, gate_dram)
            yb = K.sbuf(sm, "yb", [P, KT, S])
            combine(nc, K, merged, yb, u, h, gate_dram)
        with ExitStack() as last:
            x4 = K.sbuf(last, "x4", [P, KT, S])
            with ExitStack() as inner:
                o = K.sbuf(inner, "o2", [P, KT, S])
                with ExitStack() as split_m:
                    dense(nc, K, dram["w_out2"], KT, 1, KT, None, S,
                          lambda eng, acc, t, j: eng.activation(o[:, bass.ds(t, 1), :], acc, ACT.Copy),
                          parts=K.pair(split_m, "mix", [P, KT, S]), to_split=merged, side=[(x4[:], x3)])
                add_tiles(nc, K, x4, o)
            rms_norm(nc, K, last, x4, KT, merged, lambda t: K.col("norm2_g", t))
            squared_relu_mlp(nc, K, merged, dram["w_ff_up"], dram["w_ff_down"])
            add_tiles(nc, K, x4, merged)
            rms_norm(nc, K, last, x4, KT, merged, lambda t: K.col("norm_f_g", t),
                     store=dram["out"].rearrange("(t p) s -> p t s", p=P))


_OUT = ("out_dram", (D, S))


def slabs(w, kt):
    k, n = w.shape
    return np.ascontiguousarray(
        w.reshape(k // (kt * P), kt, P, n // P, P).transpose(3, 0, 2, 1, 4)).reshape(-1, P, kt * P)


def k_slabs(w, n):
    k, out = w.shape
    return w.reshape(k // (2 * P), 2, P, out // n, n).transpose(3, 0, 2, 1, 4).reshape(-1, P, 2 * n)


def columns(v):
    return np.asarray(v, np.float32).reshape(-1, P).T


def paired(w):
    return w.reshape(w.shape[:-1] + (2, 4, HD)).swapaxes(-3, -2).reshape(w.shape)


def shape_constants():
    a = np.zeros((P, N_CONSTS), np.float32)
    i = np.arange(P)

    def put(name, m):
        at, n = CONST_AT[name]
        a[:, at:at + n] = m
    put("ident", np.eye(P))
    put("ones", np.ones((P, P)))
    put("head_ones", i[:, None] // HD == i[None, :] // HD)
    swap = np.zeros((P, P))
    for m in range(P):
        if m % HD < 8:
            swap[m + 8, m] = -1.0
        elif m % HD < 16:
            swap[m - 8, m] = 1.0
    put("rope_swap", swap)
    put("t_ge_s", i[None, :] >= i[:, None])
    return a


def lay_out(x):
    w_in, q0 = x["w_in"][0], 2 * D_SGU
    wq, wk = w_in[:, q0:q0 + 512], w_in[:, q0 + 512:q0 + 640]
    wval, wqi = w_in[:, q0 + 640:q0 + 768], w_in[:, q0 + 768:q0 + 1280]
    wki, wwi = w_in[:, q0 + 1280:q0 + 1344], w_in[:, q0 + 1344:q0 + 1352]
    w_rot = np.concatenate([paired(wq), wk, wqi, wki, wki], axis=1)
    inv = np.zeros(P, np.float32)
    freq = (500000.0 ** (-np.arange(0, 16, 2, dtype=np.float64) / 16)).astype(np.float32)
    for p in range(P):
        if p % HD < 16:
            inv[p] = freq[p % 8]
    vec = {
        "c": x["c"], "b_ada": x["b_ada"], "g_pre_mix": x["g_pre_mix"], "g_sgu_v": x["g_sgu_v"],
        "g_out_sgu": x["g_out_sgu"], "g_out_attn": paired(x["g_out_attn"]), "g_post_mix": x["g_post_mix"],
        "g_pre_ffn": x["g_pre_ffn"], "g_post_ffn": x["g_post_ffn"], "norm1_g": x["norm1_g_2"],
        "mu": x["mu_shift_2"], "k_k": x["k_k_2"], "k_a": x["k_a_2"], "r_k": x["r_k_2"], "w0": x["w0_2"],
        "a0": x["a0_2"], "lnx_w": x["lnx_w_2"], "lnx_b": x["lnx_b_2"], "d_skip": x["d_skip_2"],
        "b_glu": x["b_glu_2"], "norm2_g": x["norm2_g_2"], "norm_f_g": x["norm_f_g_2"],
        "a_re": x["a_re_2"], "a_im": x["a_im_2"], "log_dt": np.repeat(x["log_dt_2"], HD, axis=-1),
        "inv_freq": inv, "eps": np.full(P, EPS), "lnx_eps": np.full(P, LNX_EPS), "minus_pi": np.zeros(P),
    }
    cols = np.concatenate([columns(vec[name]) for name, _ in COLS], axis=1)

    def by_token(w):
        return np.ascontiguousarray(w.reshape(KT, P, -1).transpose(1, 0, 2))
    out = {
        "cols": cols, "consts": shape_constants(), "x": np.ascontiguousarray(x["x"][0].T),
        "positions": x["positions"], "w_ada": x["w_ada"][0].reshape(KT, P, 6, D).transpose(2, 0, 1, 3).reshape(6 * KT, P, D), "w_u": slabs(w_in[:, 0:512], KT),
        "w_rot": slabs(w_rot, KT), "w_v": k_slabs(w_in[:, 512:1024], D_SGU),
        "w_val": by_token(np.concatenate([wval, wwi], axis=1)),
        "w_spatial": np.ascontiguousarray(x["w_spatial"][0].transpose(2, 0, 1)),
        "b_spatial": x["b_spatial"],
        "w_out": slabs(np.concatenate([x["w_out"][0][:512], paired(x["w_out"][0][512:].T).T]), KT),
        "w_ff1": slabs(x["w_ff1"][0], KT), "w_ff2": k_slabs(x["w_ff2"][0], HALF),
    }
    out.update(lay_out_2(x))
    return {k: np.ascontiguousarray(v) for k, v in out.items()}


def rwkv_constants():
    a = np.zeros((P, N_R), np.float32)
    r, c = np.arange(P)[:, None], np.arange(P)[None, :]
    same = r // CH == c // CH

    def put(name, m, i=0):
        at = R_AT[name][0] + i * m.shape[1]
        a[:, at:at + m.shape[1]] = m
    put("transposed", np.concatenate([-1.0 * (same & (r < c)), same & (r <= c), same & (r < c),
                                      same & (r <= c)], axis=1))
    put("minus_lower", -1.0 * (same & (r > c)))
    for i in range(6):
        n = 1 << i
        block = (r // (2 * n) == c // (2 * n)) & (r // n == c // n + 1)
        put("lower", block, i)
        put("upper", block.T, i)
    put("no_reset", np.broadcast_to(np.arange(S)[None, :] % CH != 0, (P, S)))
    return a


def state_rows(b):
    out = np.zeros((SSM_TILES, 2, HD, 2, 16), b.dtype)
    for g in range(2):
        out[:, g, :, g, :] = b[g::2]
    return out.reshape(SSM_TILES, P, 32).transpose(1, 0, 2)


def lay_out_2(x):
    w_in = x["w_in_2"][0]
    up = np.zeros((P, 2, W2), np.float32)
    up[:, 0] = np.concatenate([x["w_decay_up_2"][0], x["w_aaa_up_2"][0]])
    up[:, 1] = x["w_gate_up_2"][0]
    return {
        "w_shift": slabs(w_in[:, :SHIFT_TILES * P], KT), "r_consts": rwkv_constants(), "lora_up": up,
        "w_u2": slabs(w_in[:, SHIFT_TILES * P:SHIFT_TILES * P + W2], KT),
        "w_gates": slabs(w_in[:, SHIFT_TILES * P + W2:], KT),
        "b_re": state_rows(x["b_re_2"][0]), "b_im": state_rows(x["b_im_2"][0]),
        "c_re": state_rows(x["c_re_2"][0].transpose(0, 2, 1)), "c_im": state_rows(x["c_im_2"][0].transpose(0, 2, 1)),
        "w_glu": slabs(x["w_glu_2"][0], WT), "w_out2": slabs(x["w_out_2"][0], KT),
        "w_ff_up": slabs(x["w_ff_up_2"][0], KT), "w_ff_down": k_slabs(x["w_ff_down_2"][0], HALF),
        "w_rwkv_proj": slabs(x["w_rwkv_proj_2"][0], WT),
    }


def kernel(**inputs):
    import concourse.bacc as bacc
    from concourse.bass_utils import run_bass_kernel_spmd

    arrays = {f"in_{k}": v for k, v in lay_out({k: np.asarray(v) for k, v in inputs.items()}).items()}
    nc = bacc.Bacc("TRN2", target_bir_lowering=False, num_devices=1)
    dram = {k[3:]: nc.dram_tensor(k, a.shape, mybir.dt.from_np(a.dtype), kind="ExternalInput").ap()
            for k, a in arrays.items()}
    name, shape = _OUT
    dram["out"] = nc.dram_tensor(name, shape, F32, kind="ExternalOutput").ap()
    build(nc, dram)
    r = run_bass_kernel_spmd(nc, [arrays], core_ids=[0])
    return np.ascontiguousarray(r.results[0][name].T).reshape(1, S, D)
```
